# Optimizing a Trainium2 kernel written in Bass

```python
import jax, jax.numpy as jnp
from jax import lax
import numpy as np

D_MODEL = 1024
BATCH = 1
SEQ = 256
DEPTH = 2

MLA_HEADS = 6
MLA_NOPE = 64
MLA_ROPE = 32
MLA_V = 64
MLA_Q_RANK = 256
MLA_KV_RANK = 128
MLA_WIDTH = MLA_HEADS * MLA_V

LRU_WIDTH = 384
LRU_BLOCKS = 6
LRU_BLOCK = LRU_WIDTH // LRU_BLOCKS
LRU_C = 8.0
CONV_WIDTH = 4
CONV_PAD = (1, 2)

SWA_Q_HEADS = 4
SWA_KV_HEADS = 2
SWA_HEAD_DIM = 64
SWA_WINDOW = 128
SWA_WIDTH = SWA_Q_HEADS * SWA_HEAD_DIM

MIX_WIDTH = MLA_WIDTH + LRU_WIDTH + SWA_WIDTH
BLOCK_Q = 128
ROPE_THETA = 10000.0
EPS = 1e-6
NEG_BIG = -1e30

IN_SPLITS = (MLA_Q_RANK, MLA_KV_RANK, MLA_ROPE,
             SWA_WIDTH, SWA_KV_HEADS * SWA_HEAD_DIM, SWA_KV_HEADS * SWA_HEAD_DIM,
             LRU_WIDTH, LRU_WIDTH)
IN_WIDTH = 1696

PEER_HEADS = 8
PEER_NKEYS = 128
PEER_EXPERTS = PEER_NKEYS * PEER_NKEYS
PEER_DKEY = 256
PEER_TOPK = 16
PEER_CHUNK = 128

kernel_name = 'hybrid_mla_rglru_swa_peer_encoder'

def rmsnorm(x, g):
    xf = x.astype(jnp.float32)
    y = xf * lax.rsqrt(jnp.mean(xf * xf, axis=-1, keepdims=True) + EPS)
    return (y * g.astype(jnp.float32)).astype(x.dtype)

def rope(x, positions):
    d = x.shape[-1]
    inv = ROPE_THETA ** (-jnp.arange(0, d, 2, dtype=jnp.float32) / d)
    ang = positions.astype(jnp.float32)[..., None] * inv
    cos = jnp.cos(ang)[:, :, None, :]
    sin = jnp.sin(ang)[:, :, None, :]
    xf = x.astype(jnp.float32)
    x1, x2 = xf[..., : d // 2], xf[..., d // 2:]
    return jnp.concatenate([x1 * cos - x2 * sin, x2 * cos + x1 * sin], axis=-1).astype(x.dtype)

def mla_mixer(c_q, c_kv, k_rope, positions, q_norm, w_uq, kv_norm, w_ukv):
    B, S, _ = c_q.shape
    q = (rmsnorm(c_q, q_norm) @ w_uq).reshape(B, S, MLA_HEADS, MLA_NOPE + MLA_ROPE)
    q_nope = q[..., :MLA_NOPE]
    q_rope = rope(q[..., MLA_NOPE:], positions)
    kv = (rmsnorm(c_kv, kv_norm) @ w_ukv).reshape(B, S, MLA_HEADS, MLA_NOPE + MLA_V)
    k_nope, v = kv[..., :MLA_NOPE], kv[..., MLA_NOPE:]
    k_r = rope(k_rope[:, :, None, :], positions)[:, :, 0]
    scale = (MLA_NOPE + MLA_ROPE) ** -0.5
    nb = S // BLOCK_Q

    def to_blocks(t):
        return jnp.moveaxis(t.reshape(B, nb, BLOCK_Q, *t.shape[2:]), 1, 0)

    def attend(qb):
        qn, qr = qb
        s = (jnp.einsum('bqhd,bkhd->bhqk', qn, k_nope, preferred_element_type=jnp.float32)
             + jnp.einsum('bqhr,bkr->bhqk', qr, k_r, preferred_element_type=jnp.float32))
        p = jax.nn.softmax(s * scale, axis=-1)
        return jnp.einsum('bhqk,bkhd->bqhd', p.astype(v.dtype), v)

    o = lax.map(attend, (to_blocks(q_nope), to_blocks(q_rope)))
    return jnp.moveaxis(o, 0, 1).reshape(B, S, MLA_WIDTH)

def _lin_combine(left, right):
    a_l, b_l = left
    a_r, b_r = right
    return a_l * a_r, a_r * b_l + b_r

def rglru_mixer(x_branch, gate_branch, conv_w, conv_b, wa, ba, wx, bx, lam):
    B, S, _ = x_branch.shape
    xc = lax.conv_general_dilated(
        x_branch, conv_w[:, None, :].astype(x_branch.dtype), window_strides=(1,),
        padding=[CONV_PAD], dimension_numbers=('NWC', 'WIO', 'NWC'),
        feature_group_count=LRU_WIDTH) + conv_b
    xf = xc.astype(jnp.float32)
    xb = xf.reshape(B, S, LRU_BLOCKS, LRU_BLOCK)

    def direction(d, reverse):
        r = jax.nn.sigmoid(jnp.einsum('bsni,nij->bsnj', xb, wa[d].astype(jnp.float32))
                           + ba[d].astype(jnp.float32)).reshape(B, S, LRU_WIDTH)
        i = jax.nn.sigmoid(jnp.einsum('bsni,nij->bsnj', xb, wx[d].astype(jnp.float32))
                           + bx[d].astype(jnp.float32)).reshape(B, S, LRU_WIDTH)
        log_a = -LRU_C * r * jax.nn.softplus(-lam[d].astype(jnp.float32))
        a = jnp.exp(log_a)
        b = jnp.sqrt(-jnp.expm1(2.0 * log_a)) * (i * xf)
        _, h = lax.associative_scan(_lin_combine, (a, b), axis=1, reverse=reverse)
        return h

    h = direction(0, False) + direction(1, True)
    return (h * jax.nn.gelu(gate_branch.astype(jnp.float32), approximate=False)).astype(x_branch.dtype)

def swa_mixer(q, k, v, positions, sink):
    B, S, _ = q.shape
    G = SWA_Q_HEADS // SWA_KV_HEADS
    nb = S // BLOCK_Q
    q = rope(q.reshape(B, S, SWA_Q_HEADS, SWA_HEAD_DIM), positions)
    q = q.reshape(B, nb, BLOCK_Q, SWA_KV_HEADS, G, SWA_HEAD_DIM)
    k = rope(k.reshape(B, S, SWA_KV_HEADS, SWA_HEAD_DIM), positions)
    v = v.reshape(B, S, SWA_KV_HEADS, SWA_HEAD_DIM)
    pad = ((0, 0), (SWA_WINDOW, SWA_WINDOW), (0, 0), (0, 0))

    def band(t):
        tp = jnp.pad(t, pad)
        views = [tp[:, j * BLOCK_Q: j * BLOCK_Q + S].reshape(B, nb, BLOCK_Q, SWA_KV_HEADS, SWA_HEAD_DIM)
                 for j in range(3)]
        return jnp.concatenate(views, axis=2)

    kb, vb = band(k), band(v)
    s = jnp.einsum('bnqkgd,bnjkd->bnkgqj', q, kb, preferred_element_type=jnp.float32) * SWA_HEAD_DIM ** -0.5
    qi = jnp.arange(BLOCK_Q)[None, :, None]
    kj = jnp.arange(3 * BLOCK_Q)[None, None, :]
    kglob = jnp.arange(nb)[:, None, None] * BLOCK_Q - SWA_WINDOW + kj
    valid = (jnp.abs(kj - SWA_WINDOW - qi) <= SWA_WINDOW) & (kglob >= 0) & (kglob < S)
    s = jnp.where(valid[None, :, None, None], s, NEG_BIG)
    sink_logit = jnp.broadcast_to(sink.astype(jnp.float32).reshape(1, 1, SWA_KV_HEADS, G, 1, 1),
                                  s.shape[:-1] + (1,))
    p = jax.nn.softmax(jnp.concatenate([s, sink_logit], axis=-1), axis=-1)[..., :-1]
    o = jnp.einsum('bnkgqj,bnjkd->bnqkgd', p.astype(vb.dtype), vb)
    return o.reshape(B, S, SWA_WIDTH)

def peer_ffn(x, wq, subkeys, u, v):
    B, S, D = x.shape
    T = B * S
    xt = x.reshape(T, D)
    q = (xt @ wq).reshape(T, PEER_HEADS, 2, PEER_DKEY // 2)
    s1 = jnp.einsum('thd,nd->thn', q[:, :, 0], subkeys[0], preferred_element_type=jnp.float32)
    s2 = jnp.einsum('thd,nd->thn', q[:, :, 1], subkeys[1], preferred_element_type=jnp.float32)
    v1, i1 = lax.top_k(s1, PEER_TOPK)
    v2, i2 = lax.top_k(s2, PEER_TOPK)
    cand = (v1[..., :, None] + v2[..., None, :]).reshape(T, PEER_HEADS, PEER_TOPK * PEER_TOPK)
    sc, ci = lax.top_k(cand, PEER_TOPK)
    e1 = jnp.take_along_axis(i1, ci // PEER_TOPK, axis=-1)
    e2 = jnp.take_along_axis(i2, ci % PEER_TOPK, axis=-1)
    nc = T // PEER_CHUNK
    expert = (e1 * PEER_NKEYS + e2).reshape(nc, PEER_CHUNK, PEER_HEADS * PEER_TOPK)
    gate = jax.nn.softmax(sc, axis=-1).astype(x.dtype).reshape(nc, PEER_CHUNK, PEER_HEADS * PEER_TOPK)

    def chunk(args):
        xc, ec, gc = args
        hid = jax.nn.gelu(jnp.einsum('cd,ced->ce', xc, u[ec]), approximate=False)
        return jnp.einsum('ce,ced->cd', gc * hid, v[ec])

    y = lax.map(chunk, (xt.reshape(nc, PEER_CHUNK, D), expert, gate))
    return y.reshape(B, S, D)

def setup_inputs(seed: int = 0) -> dict:
    key = jax.random.key(seed)
    ks = jax.random.split(key, 32)
    f32 = jnp.float32

    def nrm(k, shape, scale):
        return jax.random.normal(k, shape, f32) * scale

    def gain(k, shape):
        return 1.0 + 0.02 * jax.random.normal(k, shape, f32)

    x = nrm(ks[0], (BATCH, SEQ, D_MODEL), 1.0)
    offs = jax.random.randint(ks[1], (BATCH, 1), 0, 1024, dtype=jnp.int32)
    positions = offs + jnp.arange(SEQ, dtype=jnp.int32)[None, :]
    a_c = jax.random.uniform(ks[14], (DEPTH, 2, LRU_WIDTH), f32, minval=0.9, maxval=0.999)
    p_a = a_c ** (1.0 / LRU_C)
    lru_lambda = jnp.log(p_a) - jnp.log1p(-p_a)
    return {
        'x': x,
        'positions': positions,
        'norm_mix': gain(ks[2], (DEPTH, D_MODEL)),
        'w_in': nrm(ks[3], (DEPTH, D_MODEL, IN_WIDTH), D_MODEL ** -0.5),
        'q_norm': gain(ks[4], (DEPTH, MLA_Q_RANK)),
        'w_uq': nrm(ks[5], (DEPTH, MLA_Q_RANK, MLA_HEADS * (MLA_NOPE + MLA_ROPE)), MLA_Q_RANK ** -0.5),
        'kv_norm': gain(ks[6], (DEPTH, MLA_KV_RANK)),
        'w_ukv': nrm(ks[7], (DEPTH, MLA_KV_RANK, MLA_HEADS * (MLA_NOPE + MLA_V)), MLA_KV_RANK ** -0.5),
        'conv_w': nrm(ks[8], (DEPTH, CONV_WIDTH, LRU_WIDTH), CONV_WIDTH ** -0.5),
        'conv_b': nrm(ks[9], (DEPTH, LRU_WIDTH), 0.01),
        'lru_wa': nrm(ks[10], (DEPTH, 2, LRU_BLOCKS, LRU_BLOCK, LRU_BLOCK), LRU_BLOCK ** -0.5),
        'lru_ba': nrm(ks[11], (DEPTH, 2, LRU_BLOCKS, LRU_BLOCK), 0.01),
        'lru_wx': nrm(ks[12], (DEPTH, 2, LRU_BLOCKS, LRU_BLOCK, LRU_BLOCK), LRU_BLOCK ** -0.5),
        'lru_bx': nrm(ks[13], (DEPTH, 2, LRU_BLOCKS, LRU_BLOCK), 0.01),
        'lru_lambda': lru_lambda,
        'swa_sink': nrm(ks[15], (DEPTH, SWA_Q_HEADS), 1.0),
        'grp_norm': gain(ks[16], (DEPTH, MIX_WIDTH)),
        'w_out': nrm(ks[17], (DEPTH, MIX_WIDTH, D_MODEL), MIX_WIDTH ** -0.5),
        'norm_ffn': gain(ks[18], (DEPTH, D_MODEL)),
        'peer_wq': nrm(ks[19], (DEPTH, D_MODEL, PEER_HEADS * PEER_DKEY), D_MODEL ** -0.5),
        'peer_subkeys': nrm(ks[20], (DEPTH, 2, PEER_NKEYS, PEER_DKEY // 2), (PEER_DKEY // 2) ** -0.5),
        'peer_u': nrm(ks[21], (DEPTH, PEER_EXPERTS, D_MODEL), D_MODEL ** -0.5),
        'peer_v': nrm(ks[22], (DEPTH, PEER_EXPERTS, D_MODEL), 0.5),
        'norm_final': gain(ks[23], (D_MODEL,)),
    }

def reference(x, positions, norm_mix, w_in, q_norm, w_uq, kv_norm, w_ukv, conv_w, conv_b,
              lru_wa, lru_ba, lru_wx, lru_bx, lru_lambda, swa_sink, grp_norm, w_out,
              norm_ffn, peer_wq, peer_subkeys, peer_u, peer_v, norm_final):
    split_points = np.cumsum(IN_SPLITS)[:-1].tolist()
    g_a, g_b = MLA_WIDTH, MLA_WIDTH + LRU_WIDTH
    for l in range(DEPTH):
        xn = rmsnorm(x, norm_mix[l])
        proj = xn @ w_in[l]
        c_q, c_kv, k_r, s_q, s_k, s_v, l_x, l_g = jnp.split(proj, split_points, axis=-1)
        o_mla = mla_mixer(c_q, c_kv, k_r, positions, q_norm[l], w_uq[l], kv_norm[l], w_ukv[l])
        o_lru = rglru_mixer(l_x, l_g, conv_w[l], conv_b[l], lru_wa[l], lru_ba[l],
                            lru_wx[l], lru_bx[l], lru_lambda[l])
        o_swa = swa_mixer(s_q, s_k, s_v, positions, swa_sink[l])
        g = grp_norm[l]
        mixed = jnp.concatenate([rmsnorm(o_mla, g[:g_a]),
                                 rmsnorm(o_lru, g[g_a:g_b]),
                                 rmsnorm(o_swa, g[g_b:])], axis=-1)
        x = x + mixed @ w_out[l]
        x = x + peer_ffn(rmsnorm(x, norm_ffn[l]), peer_wq[l], peer_subkeys[l], peer_u[l], peer_v[l])
    return rmsnorm(x, norm_final)


_drawn_inputs = setup_inputs


def setup_inputs(seed=0):
    import zlib

    import numpy as np

    out = dict(_drawn_inputs(seed))
    spreads = {}
    factors = {'lru_ba': 5.697, 'lru_bx': 4.334, 'swa_sink': 7.472, 'norm_final': 2.935}
    for name, (base, spread) in spreads.items():
        noise = np.random.default_rng([zlib.crc32(name.encode()), seed]).standard_normal(out[name].shape)
        drawn = base * np.exp(spread * noise) if base else spread * noise
        out[name] = __import__('jax').numpy.asarray(drawn.astype(out[name].dtype))
    for name, factor in factors.items():
        out[name] = (out[name] * factor).astype(out[name].dtype)
    return out
```

```python
from contextlib import ExitStack

import numpy as np

import concourse.bass as bass
from concourse import mybir

EPS = 1e-6
NEG_BIG = -1e30
P = 128
D = 1024
DC = D // P
SEQ = 256
NT = SEQ // P
DEPTH = 2
H_MLA, NOPE, ROPE, V_MLA = 6, 64, 32, 64
QK = NOPE + ROPE
Q_RANK, KV_RANK = 256, 128
MLA_W = H_MLA * V_MLA
LRU_W = 384
LC = LRU_W // P
LRU_C = 8.0
HALO = 3
H_SWA, KV_SWA, HD = 4, 2, 64
SWA_W = H_SWA * HD
WINDOW = 128
IN_A = Q_RANK + KV_RANK + ROPE + SWA_W + 2 * KV_SWA * HD
IN_W = IN_A + 2 * LRU_W
SQ0 = Q_RANK + KV_RANK + ROPE
SV0 = SQ0 + SWA_W + KV_SWA * HD
KR0 = Q_RANK + KV_RANK
PH = 8
NK = 128
TOP = 16
SLOTS = PH * TOP
F32 = mybir.dt.float32
F32R = mybir.dt.float32r
U32 = mybir.dt.uint32
I32 = mybir.dt.int32
ALU = mybir.AluOpType
ACT = mybir.ActivationFunctionType
AX = mybir.AxisListType
MAX_NEG = -3.0e38
ROUND = 1.5 * 2.0 ** 23
TWO_PI_1, TWO_PI_2 = 6.28125, 0.00193500518798828125
TWO_PI_3 = 2 * np.pi - TWO_PI_1 - TWO_PI_2
PI_IN = 3.1415925

C_ID, C_IOTA, C_INV, C_MASK = 0, 128, 256, 304
C_EPS = C_MASK + NT * SEQ
C_W = C_EPS + 1
NF = HD // 2 + ROPE // 2
V_NMIX, V_NFFN, V_QN, V_KVN, V_GRP = 0, 8, 16, 18, 19
V_CW, V_CB, V_BA, V_BX, V_LAM, V_SINK = 27, 39, 42, 48, 54, 60
V_W = 64


def encoder(nc, x_in, pos_in, const_in, vec_in, w_in, w_uq, w_ukv, w_lru, w_out, w_q, sub_k,
            peer_u, peer_v, norm_f, x_spill, out):
    ctx = ExitStack()
    with ctx:
        def sem(name):
            return ctx.enter_context(nc.semaphore(name))

        base_byte = -(-nc.sbuf_base // 32) * 32
        ctx.enter_context(nc.sbuf_tensor("arena", [P, 53200], F32))

        def at(name, word, shape, dt=F32):
            return nc.alloc_sbuf_tensor_at(name, shape, dt, offset=base_byte + 4 * word)

        const = at("const", 0, [P, C_W])
        cos = at("cos", 824, [P, NT, NF])
        sin = at("sin", 920, [P, NT, NF])
        vec = at("vec", 1016, [P, V_W])
        skT = at("skT", 1080, [P, 2, NK])
        stat = at("stat", 1336, [P, 256])
        x = at("x", 1600, [P, NT, D])
        xT = at("xT", 3648, [P, DC, SEQ])
        mixT = at("mixT", 5696, [P, DC, SEQ])
        ARENA_A = 7744
        ARENA_B = ARENA_A + 32768
        win_a = at("win_a", ARENA_A, [P, DC, IN_A])
        win_b = at("win_b", ARENA_A + DC * IN_A, [P, DC, 2 * LRU_W])
        wq = at("wq", ARENA_A, [P, 2 * PH, DC, P])
        wout = at("wout", ARENA_A + 16384, [P, DC, D])
        wuq = at("wuq", ARENA_A + 24576, [P, 2, H_MLA * QK])
        wukv = at("wukv", ARENA_A + 25728, [P, H_MLA * (NOPE + V_MLA)])
        wlru = at("wlru", ARENA_A + 26496, [P, 12, P])
        xs = at("xs", ARENA_A + 28032, [P, NT, D])
        ropeA = at("ropeA", ARENA_A + 28032, [P, 384])
        ropeB = at("ropeB", ARENA_A + 28032 + 384, [P, 384])
        ones = at("ones", ARENA_A + 32384, [P, P])
        qb = at("qb", ARENA_A + 30080, [P, NT, H_MLA, QK])
        kb = at("kb", ARENA_A + 31232, [P, NT, H_MLA, QK])
        gate = at("gate", ARENA_A, [P, NK * SEQ])
        lxp = at("lxp", ARENA_A, [P, LC, SEQ + HALO])
        xc = at("xc", ARENA_A + 784, [P, LC, SEQ])
        lr = at("lr", ARENA_A + 1552, [P, 2, LC, SEQ])
        li = at("li", ARENA_A + 3088, [P, 2, LC, SEQ])
        la = at("la", ARENA_A + 4624, [P, 2, LC, SEQ])
        lt = at("lt", ARENA_A + 6160, [P, 2, LC, SEQ])
        proj = at("proj", ARENA_B, [P, NT, IN_A])
        cT = at("cT", ARENA_B + 1856, [P, 3, SEQ])
        qkT = at("qkT", ARENA_B + 2624, [P, H_MLA, 2 * SEQ])
        vb = at("vb", ARENA_B + 5696, [P, NT, H_MLA, V_MLA])
        sT = at("sT", ARENA_B + 6464, [P, 6, SEQ])
        o = at("o", ARENA_B + 8000, [P, NT, MLA_W + SWA_W])
        pr = at("pr", ARENA_B + 9280, [P, 2, NT * SEQ])
        prT = at("prT", ARENA_B + 10304, [P, 2, 2 * SEQ])
        lg = at("lg", ARENA_B + 11328, [P, LC, SEQ])
        sw = at("sw", ARENA_B + 12096, [P, NT * SEQ])
        qT = at("qT", ARENA_B, [P, 2, SEQ])
        tmp = at("tmp", ARENA_B + 512, [P, SEQ])
        top_v = at("top_v", ARENA_B + 768, [P, NT, PH, 2, TOP])
        top_i = at("top_i", ARENA_B + 1280, [P, NT, PH, 2, TOP], U32)
        top_f = at("top_f", ARENA_B + 1792, [P, NT, PH, 2, TOP])
        cand = at("cand", ARENA_B + 2304, [P, 2, NT, TOP, TOP])
        sc = at("sc", ARENA_B + 3328, [P, NT, PH, TOP])
        ci = at("ci", ARENA_B + 3584, [P, NT, PH, TOP], U32)
        ca = at("ca", ARENA_B + 3840, [P, 2, NT, PH, TOP], U32)
        cf = at("cf", ARENA_B + 4352, [P, 2, NT, PH, TOP])
        eg = at("eg", ARENA_B + 4864, [P, 3, NT, PH, TOP])
        egT = at("egT", ARENA_B + 5632, [P, 3, SEQ])
        hot = at("hot", ARENA_B + 6400, [P, PH, TOP, TOP])
        one_j = at("one_j", ARENA_B + 8448, [P, 8, NK])
        one_i = at("one_i", ARENA_B + 9472, [P, 8, NK])
        raw_u = at("raw_u", ARENA_B, [P, 2, D])
        raw_v = at("raw_v", ARENA_B + 2048, [P, 2, D])
        x_back = at("x_back", ARENA_B, [P, NT, D])
        u_hl = [at(f"u_hl{s}", ARENA_B + 4096 + 2048 * s, [P, 2, DC, P], F32R) for s in range(2)]
        v_hl = [at(f"v_hl{s}", ARENA_B + 8192 + 2048 * s, [P, 2, D], F32R) for s in range(2)]
        hid_g = at("hid_g", 1600, [P, 2, SEQ])
        p_full = at("p_full", 1600 + 512, [P, 2, SEQ])
        p_hl = at("p_hl", 1600 + 1024, [P, 2, 2, SEQ], F32R)
        x_lo = at("x_lo", 3648, [P, DC, SEQ], F32R)
        x_hi = at("x_hi", 5696, [P, DC, SEQ], F32R)
        bank = [ctx.enter_context(nc.psum_tensor(f"bank{b}", [P, 512], F32)) for b in range(8)]

        ident = const[:, C_ID:C_ID + P]
        iota = const[:, C_IOTA:C_IOTA + NK]
        eps = const[:, C_EPS:C_EPS + 1]
        ang = at("ang", ARENA_B, [P, 5, NT, NF])
        posi = at("posi", ARENA_B + 600, [P, NT], I32)
        posf = at("posf", ARENA_B + 608, [P, NT])
        norm_fb = at("norm_fb", ARENA_A, [P, D])

        s_const, s_pos, s_x, s_vec, s_win_a, s_win_b, s_wuq, s_wukv, s_lru, s_wout, s_wq1, s_wq0, s_sk = (
            sem("ld_" + n) for n in ("const", "pos", "x", "vec", "win_a", "win_b", "wuq", "wukv", "lru",
                                     "wout", "wq1", "wq0", "sk"))
        final = sem("final")
        s_nf, s_spill, s_back, s_out = sem("ld_nf"), sem("spilled"), sem("x_back"), sem("stored")
        ld_u = [sem(f"ld_u{s}") for s in range(2)]
        ld_v = [sem(f"ld_v{s}") for s in range(2)]
        zeroed, ones_ready = sem("zeroed"), sem("ones_ready")
        ang_ready, trig = sem("ang_ready"), sem("trig")
        x_ready, rms_ready, xs_ready, xT_ps, xT_ready = (
            sem(n) for n in ("x_ready", "rms_ready", "xs_ready", "xT_ps", "xT_ready"))
        proj_ps, proj_a, proj_d, lru_ps, lx_ready, lg_ready = (
            sem(n) for n in ("proj_ps", "proj_a", "proj_d", "lru_ps", "lx_ready", "lg_ready"))
        c_rms, cn_ready, cT_ps, cT_ready, q_ps, kv_ps, q_nope, q_rope, kv_a, k_rope, s_rope = (
            sem(n) for n in ("c_rms", "cn_ready", "cT_ps", "cT_ready", "q_ps", "kv_ps", "q_nope", "q_rope",
                             "kv_a", "k_rope", "s_rope"))
        qk_ps, qk_ready, sT_ps, sT_ready = (sem(n) for n in ("qk_ps", "qk_ready", "sT_ps", "sT_ready"))
        lam_u, lam_ready, xc_ready, gates_ps, gates_ready, a_ready, t_ready, bq_ready, b_root = (
            sem(n) for n in ("lam_u", "lam_ready", "xc_ready", "gates_ps", "gates_ready", "a_ready",
                             "t_ready", "bq_ready", "b_root"))
        osq_ready, osum_ps, orms = sem("osq_ready"), sem("osum_ps"), sem("orms")
        sc_ps, negm, p_ready, pt_ps, pt_ready, o_ps, o_done = (
            sem(n) for n in ("sc_ps", "negm", "p_ready", "pt_ps", "pt_ready", "o_ps", "o_done"))
        o_rms, on_ready, oT_ps, mix_a, mix_d, out_ps, x_mid = (
            sem(n) for n in ("o_rms", "on_ready", "oT_ps", "mix_a", "mix_d", "out_ps", "x_mid"))
        ph_q, ph_qT, ph_s, top1, cand_ready, top2, ge_in, ge_out, eg_ready, egT_ps, egT_ready = (
            sem(n) for n in ("ph_q", "ph_qT", "ph_s", "top1", "cand_ready", "top2", "ge_in", "ge_out",
                             "eg_ready", "egT_ps", "egT_ready"))
        one_ready, gate_ps, gate_ready, split_ready = (
            sem(n) for n in ("one_ready", "gate_ps", "gate_ready", "split_ready"))
        u_hi, u_lo, v_hi, v_lo, hid_ps, gelu_done, pf_done, p_hi, p_lo, v_used = (
            sem(n) for n in ("u_hi", "u_lo", "v_hi", "v_lo", "hid_ps", "gelu_done", "pf_done", "p_hi",
                             "p_lo", "v_used"))
        CH = NK
        GROUPS = SEQ // 4

        def lru_bank(j):
            c = j % LC
            return bank[4 + 2 * (j // LC) + c // 2][:, (c % 2) * SEQ:(c % 2 + 1) * SEQ]

        def mix_bank(j):
            b, w = (j // 2, j % 2) if j < 3 else (2, j - 3)
            return bank[b][:, w * SEQ:(w + 1) * SEQ]

        block = ctx.enter_context(nc.Block())

        @block.sync
        def _(sp):
            sp.dma_start(x[:], x_in).then_inc(s_x, 16)
            sp.dma_start(const[:], const_in).then_inc(s_const, 16)
            sp.dma_start(posi[:], pos_in).then_inc(s_pos, 16)
            for lay in range(DEPTH):
                if lay:
                    sp.wait_ge(pf_done, lay * CH)
                sp.dma_start(vec[:], vec_in[lay]).then_inc(s_vec, 16)
                sp.dma_start(win_a[:], w_in[lay, :, 0:DC * IN_A]).then_inc(s_win_a, 16)
                sp.dma_start(win_b[:], w_in[lay, :, DC * IN_A:]).then_inc(s_win_b, 16)
                sp.dma_start(wuq[:], w_uq[lay]).then_inc(s_wuq, 16)
                sp.dma_start(wukv[:], w_ukv[lay]).then_inc(s_wukv, 16)
                sp.wait_ge(zeroed, lay + 1)
                sp.dma_start(wlru[0:64, :, 0:64], w_lru[lay, 0:64]).then_inc(s_lru, 16)
                sp.dma_start(wlru[64:P, :, 64:P], w_lru[lay, 64:P]).then_inc(s_lru, 16)
                sp.dma_start(wout[:], w_out[lay]).then_inc(s_wout, 16)
                sp.dma_start(skT[:], sub_k[lay]).then_inc(s_sk, 16)
                sp.wait_ge(lru_ps, 6 * (lay + 1))
                sp.wait_ge(proj_ps, 4 * (lay + 1))
                sp.dma_start(wq[:, PH:], w_q[lay, :, PH:]).then_inc(s_wq1, 16)
                sp.wait_ge(mix_d, 5 * (lay + 1))
                sp.dma_start(wq[:, 0:PH], w_q[lay, :, 0:PH]).then_inc(s_wq0, 16)
                sp.wait_ge(x_mid, 4 * (lay + 1))
                sp.dma_start(x_spill, x[:]).then_inc(s_spill, 16)

                sp.wait_ge(gate_ready, GROUPS * (lay + 1))
                for k in range(2):
                    sp.dma_start(raw_u[:, k], peer_u[lay, k]).then_inc(ld_u[k], 16)
                    sp.dma_start(raw_v[:, k], peer_v[lay, k]).then_inc(ld_v[k], 16)
                with sp.Fori(1, CH // 2) as m:
                    for s in range(2):
                        sp.wait_ge(u_lo, m * 2 + (lay * CH + s - 1))
                        sp.dma_start(raw_u[:, s], peer_u[lay, bass.ds(m * 2 + s, 1)]
                                     .rearrange("a p e -> p (a e)")).then_inc(ld_u[s], 16)
                        sp.wait_ge(v_lo, m * 2 + (lay * CH + s - 1))
                        sp.dma_start(raw_v[:, s], peer_v[lay, bass.ds(m * 2 + s, 1)]
                                     .rearrange("a p e -> p (a e)")).then_inc(ld_v[s], 16)
                sp.wait_ge(u_lo, CH * (lay + 1))
                sp.wait_ge(s_spill, 16 * (lay + 1))
                sp.dma_start(x_back[:], x_spill).then_inc(s_back, 16)
            sp.wait_ge(pf_done, DEPTH * CH)
            sp.dma_start(norm_fb[:], norm_f.partition_broadcast(P)).then_inc(s_nf, 16)
            sp.wait_ge(final, NT)
            sp.dma_start(out, xs[:]).then_inc(s_out, 16)
            sp.wait_ge(s_out, 16)

        @block.tensor
        def _(pe):
            mm = nc.tensor.matmul
            tr = nc.tensor.transpose

            def transpose_x(o_):
                pe.wait_ge(xs_ready, 2 * (o_ + 1))
                for c in range(DC):
                    b, w = bank[4 + c // 2], (c % 2) * SEQ
                    for n in range(NT):
                        last = tr(b[:, w + n * P:w + (n + 1) * P], xs[:, n, c * P:(c + 1) * P], ident)
                    if c % 2:
                        last.then_inc(xT_ps, 1)

            pe.wait_ge(s_const, 16)
            for lay in range(DEPTH):
                transpose_x(2 * lay)

                pe.wait_ge(s_win_a, 16 * (lay + 1))
                pe.wait_ge(xT_ready, 8 * (2 * lay + 1))
                HALF = IN_A // 2
                for n in range(NT):
                    for half in range(2):
                        for c in range(DC):
                            last = mm(bank[2 * n + half][:, 0:HALF], xT[:, c, n * P:(n + 1) * P],
                                      win_a[:, c, half * HALF:(half + 1) * HALF], start=c == 0, stop=c == DC - 1)
                        last.then_inc(proj_ps, 1)
                pe.wait_ge(s_win_b, 16 * (lay + 1))
                for j in range(2 * LC):
                    for c in range(DC):
                        last = mm(lru_bank(j),
                                  win_b[:, c, j * P:(j + 1) * P], xT[:, c, :], start=c == 0, stop=c == DC - 1)
                    last.then_inc(lru_ps, 1)

                pe.wait_ge(cn_ready, lay + 1)
                for j in range(3):
                    for n in range(NT):
                        last = tr(bank[j // 2][:, (j % 2) * SEQ + n * P:(j % 2) * SEQ + (n + 1) * P],
                                  proj[:, n, j * P:(j + 1) * P], ident)
                last.then_inc(cT_ps, 1)
                pe.wait_ge(cT_ready, 3 * (lay + 1))
                pe.wait_ge(s_wuq, 16 * (lay + 1))
                W3 = 3 * QK
                for n in range(NT):
                    for half in range(2):
                        for c in range(2):
                            last = mm(bank[2 * n + half][:, 0:W3], cT[:, c, n * P:(n + 1) * P],
                                      wuq[:, c, half * W3:(half + 1) * W3], start=c == 0, stop=c == 1)
                        last.then_inc(q_ps, 1)
                pe.wait_ge(lx_ready, 3 * (lay + 1))
                pe.wait_ge(lg_ready, 3 * (lay + 1))
                pe.wait_ge(s_wukv, 16 * (lay + 1))
                W3 = 3 * (NOPE + V_MLA)
                for n in range(NT):
                    for half in range(2):
                        mm(bank[4 + 2 * n + half][:, 0:W3], cT[:, 2, n * P:(n + 1) * P],
                           wukv[:, half * W3:(half + 1) * W3], start=True, stop=True).then_inc(kv_ps, 1)

                pe.wait_ge(q_nope, 4 * (lay + 1))
                pe.wait_ge(q_rope, 4 * (lay + 1))
                pe.wait_ge(kv_a, 4 * (lay + 1))
                pe.wait_ge(k_rope, 2 * (lay + 1))
                for h in range(H_MLA):
                    if h >= 4:
                        pe.wait_ge(qk_ready, H_MLA * lay + h - 3)
                    for w, src in enumerate((qb, kb)):
                        for n in range(NT):
                            last = tr(bank[h % 4][0:QK, w * SEQ + n * P:w * SEQ + (n + 1) * P],
                                      src[:, n, h, :], ident)
                    last.then_inc(qk_ps, 1)
                pe.wait_ge(s_rope, 2 * (lay + 1))
                for j in range(H_SWA + KV_SWA):
                    for n in range(NT):
                        last = tr(bank[4 + j // 2][0:HD, (j % 2) * SEQ + n * P:(j % 2) * SEQ + (n + 1) * P],
                                  proj[:, n, SQ0 + j * HD:SQ0 + (j + 1) * HD], ident)
                    if j % 2:
                        last.then_inc(sT_ps, 1)

                pe.wait_ge(xc_ready, lay + 1)
                pe.wait_ge(s_lru, 32 * (lay + 1))
                pe.wait_ge(sT_ready, 3 * (lay + 1))
                for g in range(12):
                    if g >= 4:
                        pe.wait_ge(gates_ready, 12 * lay + 2 * (g // 2) - 2)
                    mm(bank[4 + (g // 2) % 2][:, (g % 2) * SEQ:(g % 2 + 1) * SEQ], wlru[:, g, :],
                       xc[:, g % LC, :], start=True, stop=True).then_inc(gates_ps, 1)

                NH = H_MLA + H_SWA

                def scores(h):
                    if h >= 2:
                        pe.wait_ge(p_ready, NH * lay + h - 1)
                    for n in range(NT):
                        if h < H_MLA:
                            q_, k_ = qkT[0:QK, h, n * P:(n + 1) * P], qkT[0:QK, h, SEQ:]
                        else:
                            g = h - H_MLA
                            q_, k_ = sT[0:HD, g, n * P:(n + 1) * P], sT[0:HD, H_SWA + g // 2, :]
                        last = mm(bank[h % 2][:, n * SEQ:(n + 1) * SEQ], q_, k_, start=True, stop=True)
                    last.then_inc(sc_ps, 1)

                def transpose_p(h):
                    pe.wait_ge(p_ready, NH * lay + h + 1)
                    if h >= 2:
                        pe.wait_ge(pt_ready, NH * lay + h - 1)
                    for kt in range(NT):
                        for n in range(NT):
                            last = tr(bank[2 + h % 2][:, (kt * NT + n) * P:(kt * NT + n + 1) * P],
                                      pr[:, h % 2, n * SEQ + kt * P:n * SEQ + (kt + 1) * P], ident)
                    last.then_inc(pt_ps, 1)

                def weigh_v(h):
                    pe.wait_ge(pt_ready, NH * lay + h + 1)
                    if h >= 2:
                        pe.wait_ge(o_done, NH * lay + h - 1)
                    for n in range(NT):
                        for kt in range(NT):
                            if h < H_MLA:
                                v_ = vb[:, kt, h, :]
                            else:
                                g = (h - H_MLA) // 2
                                v_ = proj[:, kt, SV0 + g * HD:SV0 + (g + 1) * HD]
                            last = mm(bank[6 + h % 2][:, n * HD:(n + 1) * HD],
                                      prT[:, h % 2, (kt * NT + n) * P:(kt * NT + n + 1) * P], v_,
                                      start=kt == 0, stop=kt == NT - 1)
                    last.then_inc(o_ps, 1)

                pe.wait_ge(qk_ready, H_MLA * (lay + 1))
                scores(0)
                for h in range(NH):
                    if h + 1 < NH:
                        scores(h + 1)
                    transpose_p(h)
                    if h:
                        weigh_v(h - 1)
                weigh_v(NH - 1)

                pe.wait_ge(ones_ready, lay + 1)
                pe.wait_ge(osq_ready, lay + 1)
                for c in range(LC):
                    last = mm(bank[4][:, 0:SEQ], ones[:], lt[:, 0, c, :], start=c == 0, stop=c == LC - 1)
                last.then_inc(osum_ps, 1)

                pe.wait_ge(on_ready, 2 * (lay + 1))
                for j in range(5):
                    for n in range(NT):
                        last = tr(mix_bank(j)[:, n * P:(n + 1) * P],
                                  o[:, n, j * P:(j + 1) * P], ident)
                last.then_inc(oT_ps, 1)
                pe.wait_ge(mix_d, 5 * (lay + 1))
                pe.wait_ge(mix_a, 3 * (lay + 1))
                pe.wait_ge(s_wout, 16 * (lay + 1))
                for n in range(NT):
                    for half in range(2):
                        for c in range(DC):
                            last = mm(bank[4 + 2 * n + half][:], mixT[:, c, n * P:(n + 1) * P],
                                      wout[:, c, half * 512:(half + 1) * 512], start=c == 0, stop=c == DC - 1)
                        last.then_inc(out_ps, 1)

                transpose_x(2 * lay + 1)

                pe.wait_ge(xT_ready, 8 * (2 * lay + 2))
                pe.wait_ge(s_sk, 16 * (lay + 1))
                pe.wait_ge(s_wq1, 16 * (lay + 1))

                def key_scores(i):
                    pe.wait_ge(ph_qT, 16 * lay + i + 1)
                    if i >= 2:
                        pe.wait_ge(top1, 16 * lay + i - 1)
                    for n in range(NT):
                        last = mm(bank[2 + i % 2][:, n * NK:(n + 1) * NK], qT[:, i % 2, n * P:(n + 1) * P],
                                  skT[:, i % 2, :], start=True, stop=True)
                    last.then_inc(ph_s, 1)

                for i in range(2 * PH):
                    blk = (i + PH) % (2 * PH)
                    if i == PH:
                        pe.wait_ge(s_wq0, 16 * (lay + 1))
                    if i >= 2:
                        pe.wait_ge(ph_qT, 16 * lay + i - 1)
                    for c in range(DC):
                        last = mm(bank[i % 2][:, 0:SEQ], wq[:, blk, c, :], xT[:, c, :], start=c == 0,
                                  stop=c == DC - 1)
                    last.then_inc(ph_q, 1)
                    if i:
                        key_scores(i - 1)
                key_scores(2 * PH - 1)

                pe.wait_ge(eg_ready, lay + 1)
                for w in range(3):
                    for n in range(NT):
                        last = tr(bank[4 + w // 2][:, (w % 2) * SEQ + n * P:(w % 2) * SEQ + (n + 1) * P],
                                  eg[:, w, n].rearrange("p h s -> p (h s)"), ident)
                last.then_inc(egT_ps, 1)

                def gates_of(g, wait_value, first):
                    pe.wait_ge(one_ready, wait_value + 1)
                    if not first:
                        pe.wait_ge(gate_ready, wait_value - 3)
                    for t in range(4):
                        last = mm(bank[g][:, t * NK:(t + 1) * NK], one_j[:, (g % 2) * 4 + t, :],
                                  one_i[:, (g % 2) * 4 + t, :], start=True, stop=True)
                    last.then_inc(gate_ps, 1)

                for g in range(4):
                    gates_of(g, GROUPS * lay + g, True)
                with pe.Fori(1, GROUPS // 4) as m:
                    for g in range(4):
                        gates_of(g, m * 4 + (GROUPS * lay + g), False)

                def apply_u(s, k, first):
                    pe.wait_ge(u_lo, k + 1)
                    if not first:
                        pe.wait_ge(gelu_done, k - 1)
                    i = 0
                    for c in range(DC):
                        for (uh, xh) in ((0, x_hi), (0, x_lo), (1, x_hi)):
                            last = mm(bank[4 + s][:, 0:SEQ], u_hl[s][:, uh, c, :], xh[:, c, :], start=i == 0,
                                      stop=i == 3 * DC - 1)
                            i += 1
                    last.then_inc(hid_ps, 1)

                def apply_v(s, k, first=False, last_chunk=False):
                    pe.wait_ge(p_lo, k + 1)
                    pe.wait_ge(v_lo, k + 1)
                    for n in range(NT):
                        for (ph, vh) in ((0, 0), (0, 1), (1, 0)):
                            for half in range(2):
                                last = mm(bank[2 * n + half][:], p_hl[:, s, ph, n * P:(n + 1) * P],
                                          v_hl[s][:, vh, half * 512:(half + 1) * 512], start=first and ph == vh,
                                          stop=last_chunk and ph == 1)
                    last.then_inc(v_used, 1)

                pe.wait_ge(split_ready, lay + 1)
                pe.wait_ge(gate_ready, GROUPS * (lay + 1))
                apply_u(0, CH * lay, True)
                apply_u(1, CH * lay + 1, True)
                apply_v(0, CH * lay, first=True)
                with pe.Fori(1, CH // 2) as m:
                    apply_u(0, m * 2 + CH * lay, False)
                    apply_v(1, m * 2 + (CH * lay - 1))
                    apply_u(1, m * 2 + (CH * lay + 1), False)
                    apply_v(0, m * 2 + CH * lay)
                apply_v(1, CH * lay + CH - 1, last_chunk=True)

        @block.scalar
        def _(act):
            af = nc.scalar.activation

            def rms(o_):
                act.wait_ge(x_ready, 4 * (o_ + 1))
                for n in range(NT):
                    af(xs[:, n, :], x[:, n, :], ACT.Square, accum_out=stat[:, n:n + 1])
                act.drain()
                af(stat[:, 2:4], stat[:, 0:2], ACT.Sqrt, bias=eps, scale=1.0 / D).then_inc(rms_ready, 1)

            def copy_xT(o_, gain):
                for b in (0, 2):
                    act.wait_ge(xT_ps, 4 * o_ + b + 1)
                    for c in (2 * b, 2 * b + 1):
                        af(xT[:, c, :], bank[4 + b][:, (c % 2) * SEQ:(c % 2 + 1) * SEQ], ACT.Copy,
                           scale=vec[:, gain + c:gain + c + 1]).then_inc(xT_ready, 1)

            act.wait_ge(s_const, 16)
            act.wait_ge(ang_ready, 1)
            af(sin[:], ang[:, 1], ACT.Sin).then_inc(trig, 1)
            af(cos[:], ang[:, 2], ACT.Sin).then_inc(trig, 1)
            for lay in range(DEPTH):
                rms(2 * lay)
                act.wait_ge(s_vec, 16 * (lay + 1))
                af(stat[:, 16:22], vec[:, V_LAM:V_LAM + 6], ACT.Abs)
                act.drain()
                af(stat[:, 16:22], stat[:, 16:22], ACT.Exp, scale=-1.0).then_inc(lam_u, 1)
                copy_xT(2 * lay, V_NMIX)

                HALF = IN_A // 2
                for half in range(2):
                    act.wait_ge(proj_ps, 4 * lay + half + 1)
                    af(proj[:, 0, half * HALF:(half + 1) * HALF], bank[half][:, 0:HALF],
                       ACT.Copy).then_inc(proj_a, 1)
                act.wait_ge(proj_d, 2 * (lay + 1))
                act.drain()
                for w, (c0, c1) in enumerate(((0, Q_RANK), (Q_RANK, KR0))):
                    for n in range(NT):
                        af(xs[:, 0, 0:c1 - c0], proj[:, n, c0:c1], ACT.Square,
                           accum_out=stat[:, 4 + 2 * w + n:5 + 2 * w + n])
                        act.drain()
                af(stat[:, 8:10], stat[:, 4:6], ACT.Sqrt, bias=eps, scale=1.0 / Q_RANK)
                af(stat[:, 10:12], stat[:, 6:8], ACT.Sqrt, bias=eps, scale=1.0 / KV_RANK).then_inc(c_rms, 1)
                for c in range(LC):
                    j = LC + c
                    act.wait_ge(lru_ps, 6 * (lay + 1))
                    af(lg[:, c, :], lru_bank(j), ACT.Gelu).then_inc(lg_ready, 1)
                act.wait_ge(cT_ps, lay + 1)
                for j in range(3):
                    g = V_QN + j if j < 2 else V_KVN
                    af(cT[:, j, :], bank[j // 2][:, (j % 2) * SEQ:(j % 2 + 1) * SEQ], ACT.Copy,
                       scale=vec[:, g:g + 1]).then_inc(cT_ready, 1)
                for n in range(NT):
                    for half in range(2):
                        act.wait_ge(q_ps, 4 * lay + 2 * n + half + 1)
                        b = bank[2 * n + half][:, 0:3 * QK].rearrange("p (h d) -> p h d", h=3)
                        af(qb[:, n, 3 * half:3 * half + 3, 0:NOPE], b[:, :, 0:NOPE], ACT.Copy).then_inc(q_nope, 1)
                for n in range(NT):
                    for half in range(2):
                        act.wait_ge(kv_ps, 4 * lay + 2 * n + half + 1)
                        b = bank[4 + 2 * n + half][:, 0:3 * (NOPE + V_MLA)].rearrange("p (h d) -> p h d", h=3)
                        af(kb[:, n, 3 * half:3 * half + 3, 0:NOPE], b[:, :, 0:NOPE], ACT.Copy)
                        af(vb[:, n, 3 * half:3 * half + 3, :], b[:, :, NOPE:], ACT.Copy).then_inc(kv_a, 1)
                for h in range(H_MLA):
                    act.wait_ge(qk_ps, H_MLA * lay + h + 1)
                    af(qkT[0:QK, h, :], bank[h % 4][0:QK, :], ACT.Copy).then_inc(qk_ready, 1)

                for g in range(12):
                    d, kind, c = g // 6, (g // 3) % 2, g % 3
                    act.wait_ge(gates_ps, 12 * lay + 2 * (g // 2) + 2)
                    v0 = (V_BX if kind else V_BA) + 3 * d + c
                    af((li if kind else lr)[:, d, c, :], bank[4 + (g // 2) % 2][:, (g % 2) * SEQ:(g % 2 + 1) * SEQ],
                       ACT.Sigmoid, bias=vec[:, v0:v0 + 1]).then_inc(gates_ready, 1)
                act.drain()
                act.wait_ge(lam_ready, lay + 1)
                for g in range(6):
                    last = af(la[:, g // 3, g % 3, :], lr[:, g // 3, g % 3, :], ACT.Exp, scale=stat[:, 28 + g:29 + g])
                last.then_inc(a_ready, 1)
                for g in range(6):
                    last = af(lr[:, g // 3, g % 3, :], lr[:, g // 3, g % 3, :], ACT.Tanh, scale=stat[:, 22 + g:23 + g])
                last.then_inc(t_ready, 1)

                NH = H_MLA + H_SWA
                for h in range(NH):
                    act.wait_ge(negm, NH * lay + h + 1)
                    if h >= 2:
                        act.wait_ge(pt_ps, NH * lay + h - 1)
                    for n in range(NT):
                        src = bank[h % 2] if h < H_MLA else sw
                        last = af(pr[:, h % 2, n * SEQ:(n + 1) * SEQ], src[:, n * SEQ:(n + 1) * SEQ], ACT.Exp,
                                  bias=stat[:, 84 + 2 * h + n:85 + 2 * h + n],
                                  scale=QK ** -0.5 if h < H_MLA else 1.0,
                                  accum_out=stat[:, 104 + 2 * h + n:105 + 2 * h + n])
                        if h >= H_MLA:
                            g = V_SINK + h - H_MLA
                            last = af(stat[:, 124 + 2 * h + n:125 + 2 * h + n], vec[:, g:g + 1], ACT.Exp,
                                      bias=stat[:, 84 + 2 * h + n:85 + 2 * h + n])
                    last.then_inc(p_ready, 1)
                    if h == 6:
                        act.wait_ge(bq_ready, lay + 1)
                        af(lr[:], lr[:], ACT.Sqrt, scale=2.0).then_inc(b_root, 1)

                act.wait_ge(o_done, NH * (lay + 1))
                for w, (c0, c1) in enumerate(((0, MLA_W), (MLA_W, MLA_W + SWA_W))):
                    for n in range(NT):
                        af(xs[:, 0, 0:c1 - c0], o[:, n, c0:c1], ACT.Square,
                           accum_out=stat[:, 164 + 2 * w + n:165 + 2 * w + n])
                        act.drain()
                af(stat[:, 168:170], stat[:, 164:166], ACT.Sqrt, bias=eps, scale=1.0 / MLA_W)
                af(stat[:, 170:172], stat[:, 166:168], ACT.Sqrt, bias=eps, scale=1.0 / SWA_W).then_inc(o_rms, 1)
                act.wait_ge(osum_ps, lay + 1)
                af(lt[:, 1, 0, :], bank[4][:, 0:SEQ], ACT.Sqrt, bias=eps, scale=1.0 / LRU_W).then_inc(orms, 1)
                act.wait_ge(oT_ps, lay + 1)
                for j in range(3):
                    af(mixT[:, j, :], mix_bank(j), ACT.Copy,
                       scale=vec[:, V_GRP + j:V_GRP + j + 1]).then_inc(mix_a, 1)

                rms(2 * lay + 1)
                copy_xT(2 * lay + 1, V_NFFN)
                for i in range(2 * PH):
                    act.wait_ge(ph_q, 16 * lay + i + 1)
                    if i >= 2:
                        act.wait_ge(ph_s, 16 * lay + i - 1)
                    af(qT[:, i % 2, :], bank[i % 2][:, 0:SEQ], ACT.Copy).then_inc(ph_qT, 1)
                act.wait_ge(ge_in, lay + 1)
                af(sc[:], sc[:], ACT.Exp).then_inc(ge_out, 1)
                act.wait_ge(egT_ps, lay + 1)
                af(egT[:, 0:2, :], bank[4][:], ACT.Copy)
                af(egT[:, 2, :], bank[5][:, 0:SEQ], ACT.Copy).then_inc(egT_ready, 1)

                gate_v = gate[:].rearrange("p (i t) -> p t i", t=SEQ)

                with act.Fori(0, GROUPS // 4) as m:
                    for g in range(4):
                        act.wait_ge(gate_ps, m * 4 + (GROUPS * lay + g + 1))
                        af(gate_v[:, bass.ds(m * 16 + 4 * g, 4), :],
                           bank[g][:].rearrange("p (t i) -> p t i", t=4), ACT.Copy).then_inc(gate_ready, 1)

                def split_u(s, k, first):
                    act.wait_ge(ld_u[s], slot_loads(k, s))
                    if not first:
                        act.wait_ge(hid_ps, k - 1)
                    af(u_hl[s][:, 0].rearrange("p c e -> p (c e)"), raw_u[:, s], ACT.Copy).then_inc(u_hi, 1)

                def split_v(s, k, first):
                    act.wait_ge(ld_v[s], slot_loads(k, s))
                    if not first:
                        act.wait_ge(v_used, k - 1)
                    af(v_hl[s][:, 0], raw_v[:, s], ACT.Copy).then_inc(v_hi, 1)

                def slot_loads(k, s):
                    return (k - s) * 8 + 16

                def activate(s, k, first):
                    act.wait_ge(hid_ps, k + 1)
                    if not first:
                        act.wait_ge(pf_done, k - 1)
                    af(hid_g[:, s], bank[4 + s][:, 0:SEQ], ACT.Gelu).then_inc(gelu_done, 1)

                def split_p(s, k, first):
                    act.wait_ge(pf_done, k + 1)
                    if not first:
                        act.wait_ge(v_used, k - 1)
                    af(p_hl[:, s, 0], p_full[:, s], ACT.Copy).then_inc(p_hi, 1)

                K0 = CH * lay
                act.wait_ge(s_spill, 16 * (lay + 1))
                for s in range(2):
                    split_u(s, K0 + s, True)
                    if s:
                        activate(0, K0, True)
                        split_p(0, K0, True)
                    split_v(s, K0 + s, True)
                with act.Fori(1, CH // 2) as m:
                    split_u(0, m * 2 + K0, False)
                    activate(1, m * 2 + (K0 - 1), False)
                    split_p(1, m * 2 + (K0 - 1), False)
                    split_v(0, m * 2 + K0, False)
                    split_u(1, m * 2 + (K0 + 1), False)
                    activate(0, m * 2 + K0, False)
                    split_p(0, m * 2 + K0, False)
                    split_v(1, m * 2 + (K0 + 1), False)
                activate(1, K0 + CH - 1, False)
                split_p(1, K0 + CH - 1, False)
            rms(2 * DEPTH)

        @block.vector
        def _(dve):
            v = nc.vector
            cp, tt, ts, stt = v.tensor_copy, v.tensor_tensor, v.tensor_scalar, v.scalar_tensor_tensor

            def scale_x(o_):
                dve.wait_ge(rms_ready, o_ + 1)
                v.reciprocal(stat[:, 2:4], stat[:, 2:4])
                dve.drain()
                for n in range(NT):
                    ts(xs[:, n, :], x[:, n, :], stat[:, 2 + n:3 + n], None, ALU.mult).then_inc(xs_ready, 1)

            def copy_xT(o_, gain):
                for b in (1, 3):
                    dve.wait_ge(xT_ps, 4 * o_ + b + 1)
                    for c in (2 * b, 2 * b + 1):
                        ts(xT[:, c, :], bank[4 + b][:, (c % 2) * SEQ:(c % 2 + 1) * SEQ],
                           vec[:, gain + c:gain + c + 1], None, ALU.mult).then_inc(xT_ready, 1)

            def rotate(out1, out2, src, trig_n, heads, half):
                c0 = 0 if half == HD // 2 else HD // 2
                shape = [P, heads, 2, half]
                a = ropeA[:, 0:heads * 2 * half].rearrange("p (h w d) -> p h w d", h=heads, w=2)
                b = ropeB[:, 0:heads * 2 * half].rearrange("p (h w d) -> p h w d", h=heads, w=2)
                cs, sn = (t[:, trig_n, c0:c0 + half].unsqueeze(1).unsqueeze(1).broadcast_to(shape)
                          for t in (cos, sin))
                tt(a, src, cs, ALU.mult)
                tt(b, src, sn, ALU.mult)
                dve.drain()
                tt(out1, a[:, :, 0], b[:, :, 1], ALU.subtract)
                r = tt(out2, a[:, :, 1], b[:, :, 0], ALU.add)
                dve.drain()
                return r

            dve.wait_ge(s_pos, 16)
            dve.wait_ge(s_const, 16)
            cp(posf[:], posi[:])
            dve.drain()
            for n in range(NT):
                ts(ang[:, 0, n], const[:, C_INV:C_INV + NF], posf[:, n:n + 1], None, ALU.mult)
            dve.drain()
            for w, quarter in ((1, 0.0), (2, 0.25)):
                ts(ang[:, 3], ang[:, 0], 1.0 / (2 * np.pi), quarter, ALU.mult, ALU.add)
                dve.drain()
                ts(ang[:, 3], ang[:, 3], ROUND, ROUND, ALU.add, ALU.subtract)
                dve.drain()
                src = ang[:, 0]
                for part in (TWO_PI_1, TWO_PI_2, TWO_PI_3):
                    stt(ang[:, w], ang[:, 3], -part, src, ALU.mult, ALU.add)
                    src = ang[:, w]
                    dve.drain()
                ts(ang[:, w], ang[:, w], quarter * 2 * np.pi, PI_IN, ALU.add, ALU.min)
                dve.drain()
                ts(ang[:, w], ang[:, w], -PI_IN, None, ALU.max)
            dve.drain()
            cp(ang[:, 4], ang[:, 3]).then_inc(ang_ready, 1)
            dve.wait_ge(s_x, 16)
            v.memset(stat[:, 12:13], 0.0).then_inc(x_ready, 4)
            for lay in range(DEPTH):
                scale_x(2 * lay)
                dve.wait_ge(lam_u, lay + 1)
                u, z, z2, q, s8, n8 = (stat[:, 16 + 6 * k:22 + 6 * k] for k in (0, 3, 4, 5, 1, 2))
                ts(z, u, 2.0, None, ALU.add)
                dve.drain()
                v.reciprocal(z, z)
                dve.drain()
                tt(z, z, u, ALU.mult)
                dve.drain()
                tt(z2, z, z, ALU.mult)
                dve.drain()
                ts(q, z2, 1.0 / 19, None, ALU.mult)
                for k in range(8, 0, -1):
                    dve.drain()
                    stt(q, q, 1.0 / (2 * k + 1), z2, ALU.add, ALU.mult)
                ts(s8, vec[:, V_LAM:V_LAM + 6], -LRU_C, 0.0, ALU.mult, ALU.max)
                dve.drain()
                stt(q, q, 1.0, z, ALU.add, ALU.mult)
                dve.drain()
                stt(s8, q, 2 * LRU_C, s8, ALU.mult, ALU.add)
                dve.drain()
                ts(n8, s8, -1.0, None, ALU.mult).then_inc(lam_ready, 1)
                copy_xT(2 * lay, V_NMIX)

                HALF = IN_A // 2
                for half in range(2):
                    dve.wait_ge(proj_ps, 4 * lay + 2 + half + 1)
                    cp(proj[:, 1, half * HALF:(half + 1) * HALF], bank[2 + half][:, 0:HALF]).then_inc(proj_d, 1)
                dve.wait_ge(lru_ps, 6 * (lay + 1))
                v.memset(lxp[:, :, 0:1], 0.0)
                v.memset(lxp[:, :, SEQ + 1:], 0.0)
                for c in range(LC):
                    cp(lxp[:, c, 1:SEQ + 1], lru_bank(c)).then_inc(lx_ready, 1)
                dve.wait_ge(c_rms, lay + 1)
                v.reciprocal(stat[:, 8:12], stat[:, 8:12])
                dve.drain()
                for w, (c0, c1) in enumerate(((0, Q_RANK), (Q_RANK, KR0))):
                    for n in range(NT):
                        last = ts(proj[:, n, c0:c1], proj[:, n, c0:c1], stat[:, 8 + 2 * w + n:9 + 2 * w + n],
                                  None, ALU.mult)
                last.then_inc(cn_ready, 1)
                dve.wait_ge(proj_a, 2 * (lay + 1))
                dve.wait_ge(trig, 2)
                for n in range(NT):
                    src = proj[:, n, SQ0:SV0].rearrange("p (h w d) -> p h w d", h=6, w=2)
                    rotate(src[:, :, 0], src[:, :, 1], src, n, 6, HD // 2).then_inc(s_rope, 1)
                for n in range(NT):
                    src = proj[:, n, KR0:KR0 + ROPE].rearrange("p (h w d) -> p h w d", h=1, w=2)
                    rotate(src[:, :, 0], src[:, :, 1], src, n, 1, ROPE // 2)
                    cp(kb[:, n, :, NOPE:], proj[:, n, KR0:KR0 + ROPE].unsqueeze(1)
                       .broadcast_to([P, H_MLA, ROPE])).then_inc(k_rope, 1)
                for n in range(NT):
                    for half in range(2):
                        dve.wait_ge(q_nope, 4 * lay + 2 * n + half + 1)
                        src = (bank[2 * n + half][:, 0:3 * QK].rearrange("p (h d) -> p h d", h=3)[:, :, NOPE:]
                               .rearrange("p h (w d) -> p h w d", w=2))
                        dst = qb[:, n, 3 * half:3 * half + 3, NOPE:]
                        rotate(dst[:, :, 0:ROPE // 2], dst[:, :, ROPE // 2:], src, n, 3,
                               ROPE // 2).then_inc(q_rope, 1)
                for k in range(HALO + 1):
                    for c in range(LC):
                        w_ = vec[:, V_CW + LC * k + c:V_CW + LC * k + c + 1]
                        src = lxp[:, c, k:k + SEQ]
                        if k == 0:
                            last = ts(xc[:, c], src, w_, vec[:, V_CB + c:V_CB + c + 1], ALU.mult, ALU.add)
                        else:
                            last = stt(xc[:, c], src, w_, xc[:, c], ALU.mult, ALU.add)
                    if k < HALO:
                        dve.drain()
                last.then_inc(xc_ready, 1)
                for j in range(3):
                    dve.wait_ge(sT_ps, 3 * lay + j + 1)
                    cp(sT[0:HD, 2 * j:2 * j + 2].rearrange("p a t -> p (a t)"), bank[4 + j][0:HD, :]).then_inc(sT_ready, 1)

                NH = H_MLA + H_SWA

                def row_max(h):
                    dve.wait_ge(sc_ps, NH * lay + h + 1)
                    nm = stat[:, 84 + 2 * h:86 + 2 * h]
                    mx = stat[:, 64 + 2 * h:66 + 2 * h]
                    if h < H_MLA:
                        v.reduce_max(mx, bank[h % 2][:].rearrange("p (n k) -> p n k", n=NT), AX.X)
                        dve.drain()
                        ts(nm, mx, -QK ** -0.5, None, ALU.mult).then_inc(negm, 1)
                    else:
                        if h > H_MLA:
                            dve.wait_ge(p_ready, NH * lay + h)
                        stt(sw[:], bank[h % 2][:], HD ** -0.5, const[:, C_MASK:C_MASK + NT * SEQ], ALU.mult, ALU.add)
                        dve.drain()
                        v.reduce_max(mx, sw[:].rearrange("p (n k) -> p n k", n=NT), AX.X)
                        dve.drain()
                        g = V_SINK + h - H_MLA
                        ts(nm, mx, vec[:, g:g + 1], -1.0, ALU.max, ALU.mult).then_inc(negm, 1)

                def copy_pT(h):
                    dve.wait_ge(pt_ps, NH * lay + h + 1)
                    if h >= 2:
                        dve.wait_ge(o_ps, NH * lay + h - 1)
                    cp(prT[:, h % 2, :], bank[2 + h % 2][:]).then_inc(pt_ready, 1)

                def norm_o(h):
                    dve.wait_ge(o_ps, NH * lay + h + 1)
                    s_ = stat[:, 104 + 2 * h:106 + 2 * h]
                    if h >= H_MLA:
                        tt(s_, s_, stat[:, 124 + 2 * h:126 + 2 * h], ALU.add)
                        dve.drain()
                    v.reciprocal(s_, s_)
                    dve.drain()
                    for n in range(NT):
                        last = ts(o[:, n, h * HD:(h + 1) * HD], bank[6 + h % 2][:, n * HD:(n + 1) * HD],
                                  stat[:, 104 + 2 * h + n:105 + 2 * h + n], None, ALU.mult)
                    last.then_inc(o_done, 1)

                def flat(t):
                    return t[:].rearrange("p d c t -> p (d c t)")

                def lru_gain():
                    dve.wait_ge(t_ready, lay + 1)
                    ts(flat(lt), flat(lr), 1.0, None, ALU.add)
                    dve.drain()
                    v.reciprocal(flat(lt), flat(lt))
                    dve.drain()
                    tt(flat(lr), flat(lr), flat(lt), ALU.mult).then_inc(bq_ready, 1)
                    tt(li[:].rearrange("p d c t -> p d (c t)"), li[:].rearrange("p d c t -> p d (c t)"),
                       xc[:].rearrange("p c t -> p (c t)").unsqueeze(1).broadcast_to([P, 2, LC * SEQ]), ALU.mult)

                def lru_scan():
                    dve.wait_ge(b_root, lay + 1)
                    dve.wait_ge(a_ready, lay + 1)
                    tt(flat(li), flat(li), flat(lr), ALU.mult)
                    dve.drain()
                    for c in range(LC):
                        v.tensor_tensor_scan(lr[:, 0, c, :], la[:, 0, c, :], li[:, 0, c, :], 0.0, ALU.mult, ALU.add)
                        v.tensor_tensor_scan(lr[:, 1, c, ::-1], la[:, 1, c, ::-1], li[:, 1, c, ::-1], 0.0,
                                             ALU.mult, ALU.add)

                def lru_out():
                    f = [lr[:, d].rearrange("p c t -> p (c t)") for d in range(2)]
                    tt(f[0], f[0], f[1], ALU.add)
                    dve.drain()
                    tt(f[0], f[0], lg[:].rearrange("p c t -> p (c t)"), ALU.mult)
                    dve.drain()
                    tt(lt[:, 0].rearrange("p c t -> p (c t)"), f[0], f[0], ALU.mult).then_inc(osq_ready, 1)

                row_max(0)
                for h in range(NH):
                    if h + 1 < NH:
                        row_max(h + 1)
                    copy_pT(h)
                    if h:
                        norm_o(h - 1)
                    if h == 3:
                        lru_gain()
                    if h == 7:
                        lru_scan()
                norm_o(NH - 1)
                lru_out()
                dve.wait_ge(lg_ready, 3 * (lay + 1))

                dve.wait_ge(o_rms, lay + 1)
                v.reciprocal(stat[:, 168:172], stat[:, 168:172])
                dve.drain()
                for w, (c0, c1) in enumerate(((0, MLA_W), (MLA_W, MLA_W + SWA_W))):
                    for n in range(NT):
                        last = ts(o[:, n, c0:c1], o[:, n, c0:c1], stat[:, 168 + 2 * w + n:169 + 2 * w + n], None,
                                  ALU.mult)
                    last.then_inc(on_ready, 1)
                dve.wait_ge(orms, lay + 1)
                v.reciprocal(lt[:, 1, 0, :], lt[:, 1, 0, :])
                dve.drain()
                for c in range(LC):
                    stt(mixT[:, 3 + c, :], lr[:, 0, c, :], vec[:, V_GRP + 3 + c:V_GRP + 4 + c], lt[:, 1, 0, :],
                        ALU.mult, ALU.mult).then_inc(mix_d, 1)
                dve.wait_ge(oT_ps, lay + 1)
                for j in (3, 4):
                    ts(mixT[:, 3 + j, :], mix_bank(j),
                       vec[:, V_GRP + 3 + j:V_GRP + 4 + j], None, ALU.mult).then_inc(mix_d, 1)
                for n in range(NT):
                    for half in range(2):
                        dve.wait_ge(out_ps, 4 * lay + 2 * n + half + 1)
                        w = x[:, n, half * 512:(half + 1) * 512]
                        r = tt(w, w, bank[4 + 2 * n + half][:], ALU.add)
                        r.then_inc(x_mid, 1)
                dve.drain()
                v.memset(stat[:, 12:13], 0.0).then_inc(x_ready, 4)
                scale_x(2 * lay + 1)
                copy_xT(2 * lay + 1, V_NFFN)

                def top16(val, idx, src, work):
                    v.max(val[:, 0:8], src)
                    dve.drain()
                    v.max_index(idx[:, 0:8], val[:, 0:8], src)
                    v.match_replace(work, val[:, 0:8], src, MAX_NEG)
                    dve.drain()
                    v.max(val[:, 8:16], work)
                    dve.drain()
                    return v.max_index(idx[:, 8:16], val[:, 8:16], work)

                def top_keys(i):
                    h, half = (i // 2 + PH // 2) % PH, i % 2
                    dve.wait_ge(ph_s, 16 * lay + i + 1)
                    for n in range(NT):
                        last = top16(top_v[:, n, h, half], top_i[:, n, h, half],
                                     bank[2 + i % 2][:, n * NK:(n + 1) * NK], tmp[:, n * NK:(n + 1) * NK])
                    last.then_inc(top1, 1)

                def top_pairs(i):
                    h = (i + PH // 2) % PH
                    dve.wait_ge(cand_ready, PH * lay + i + 1)
                    for n in range(NT):
                        c_ = cand[:, i % 2, n].rearrange("p a b -> p (a b)")
                        last = top16(sc[:, n, h], ci[:, n, h], c_, c_)
                    last.then_inc(top2, 1)

                for i in range(PH):
                    top_keys(2 * i)
                    top_keys(2 * i + 1)
                    if i:
                        top_pairs(i - 1)
                top_pairs(PH - 1)
                dve.drain()
                s3 = sc[:].rearrange("p n h s -> p (n h) s")
                big = stat[:, 208:224]
                cp(big, s3[:, :, 0])
                dve.drain()
                tt(s3, s3, big.unsqueeze(2).broadcast_to([P, NT * PH, TOP]), ALU.subtract).then_inc(ge_in, 1)
                cif = ci[:].rearrange("p n h s -> p (n h s)")
                caf = ca[:].rearrange("p w n h s -> p w (n h s)")
                ts(caf[:, 0], cif, 4, None, ALU.logical_shift_right)
                ts(caf[:, 1], cif, TOP - 1, None, ALU.bitwise_and)
                dve.drain()
                cp(cf[:].rearrange("p w n h s -> p (w n h s)"), ca[:].rearrange("p w n h s -> p (w n h s)"))
                cp(top_f[:].rearrange("p n h w s -> p (n h w s)"), top_i[:].rearrange("p n h w s -> p (n h w s)"))
                dve.drain()
                shape = [P, PH, TOP, TOP]
                i16 = const[:, C_IOTA:C_IOTA + TOP].unsqueeze(1).unsqueeze(1).broadcast_to(shape)
                for w in range(2):
                    for n in range(NT):
                        tt(hot[:], cf[:, w, n].unsqueeze(3).broadcast_to(shape), i16, ALU.is_equal)
                        dve.drain()
                        tt(hot[:], hot[:], top_f[:, n, :, w].unsqueeze(2).broadcast_to(shape), ALU.mult)
                        dve.drain()
                        v.reduce_sum(eg[:, w, n], hot[:], AX.X)
                        dve.drain()
                dve.wait_ge(ge_out, lay + 1)
                gs = stat[:, 176:192]
                v.reduce_sum(gs, s3, AX.X)
                dve.drain()
                v.reciprocal(gs, gs)
                dve.drain()
                tt(eg[:, 2].rearrange("p n h s -> p (n h) s"), s3, gs.unsqueeze(2).broadcast_to([P, NT * PH, TOP]),
                   ALU.mult).then_inc(eg_ready, 1)
                dve.wait_ge(ph_q, 16 * (lay + 1))
                fl = [t[:].rearrange("p c t -> p (c t)") for t in (x_hi, xT, x_lo)]
                cp(fl[0], fl[1])
                dve.drain()
                tt(fl[2], fl[1], fl[0], ALU.subtract).then_inc(split_ready, 1)

                dve.wait_ge(egT_ready, lay + 1)

                def one_hots(g, t0, count, first):
                    if not first:
                        dve.wait_ge(gate_ps, count - 1)
                    for t in range(4):
                        s_ = (g % 2) * 4 + t
                        col = [egT[:, w, bass.ds(t0 + t, 1)] for w in range(3)]
                        ts(one_j[:, s_], iota, col[1], None, ALU.is_equal)
                        last = ts(one_i[:, s_], iota, col[0], col[2], ALU.is_equal, ALU.mult)
                    last.then_inc(one_ready, 1)

                G0 = GROUPS * lay
                one_hots(0, 0, G0, True)
                one_hots(1, 4, G0 + 1, True)
                with dve.Fori(1, GROUPS // 2) as m:
                    for g in range(2):
                        one_hots(g, m * 8 + 4 * g, m * 2 + (G0 + g), False)

                def split_u(s, k):
                    dve.wait_ge(u_hi, k + 1)
                    lo, hi = (u_hl[s][:, w].rearrange("p c e -> p (c e)") for w in (1, 0))
                    tt(lo, raw_u[:, s], hi, ALU.subtract).then_inc(u_lo, 1)

                def split_v(s, k):
                    dve.wait_ge(v_hi, k + 1)
                    tt(v_hl[s][:, 1], raw_v[:, s], v_hl[s][:, 0], ALU.subtract).then_inc(v_lo, 1)

                def weigh(s, k, i):
                    dve.wait_ge(gelu_done, k + 1)
                    tt(p_full[:, s], hid_g[:, s], gate[:, bass.ds(i * SEQ, SEQ)], ALU.mult).then_inc(pf_done, 1)

                def split_p(s, k):
                    dve.wait_ge(p_hi, k + 1)
                    tt(p_hl[:, s, 1], p_full[:, s], p_hl[:, s, 0], ALU.subtract).then_inc(p_lo, 1)

                K0 = CH * lay
                split_u(0, K0)
                split_v(0, K0)
                split_u(1, K0 + 1)
                weigh(0, K0, 0)
                split_v(1, K0 + 1)
                split_p(0, K0)
                with dve.Fori(1, CH // 2) as m:
                    for s in range(2):
                        split_u(s, m * 2 + (K0 + s))
                        weigh(1 - s, m * 2 + (K0 + s - 1), m * 2 + (s - 1))
                        split_v(s, m * 2 + (K0 + s))
                        split_p(1 - s, m * 2 + (K0 + s - 1))
                weigh(1, K0 + CH - 1, CH - 1)
                split_p(1, K0 + CH - 1)
                dve.wait_ge(v_used, CH * (lay + 1))
                dve.wait_ge(s_back, 16 * (lay + 1))
                for n in range(NT):
                    for half in range(2):
                        w = slice(half * 512, (half + 1) * 512)
                        tt(x[:, n, w], x_back[:, n, w], bank[2 * n + half][:], ALU.add)
                dve.drain()
                v.memset(stat[:, 12:13], 0.0).then_inc(x_ready, 4)
            scale_x(2 * DEPTH)
            dve.wait_ge(s_nf, 16)
            dve.drain()
            for n in range(NT):
                tt(xs[:, n, :], xs[:, n, :], norm_fb[:], ALU.mult).then_inc(final, 1)

        @block.gpsimd
        def _(pool):
            for lay in range(DEPTH):
                if lay:
                    pool.wait_ge(pf_done, lay * CH)
                nc.gpsimd.memset(wlru[:], 0.0).then_inc(zeroed, 1)
                nc.gpsimd.memset(ones[:], 1.0).then_inc(ones_ready, 1)
                for i in range(PH):
                    h = (i + PH // 2) % PH
                    pool.wait_ge(top1, 16 * lay + 2 * i + 2)
                    if i >= 2:
                        pool.wait_ge(top2, PH * lay + i - 1)
                    for n in range(NT):
                        last = nc.gpsimd.tensor_tensor(
                            cand[:, i % 2, n], top_v[:, n, h, 0].unsqueeze(2).broadcast_to([P, TOP, TOP]),
                            top_v[:, n, h, 1].unsqueeze(1).broadcast_to([P, TOP, TOP]), ALU.add)
                    last.then_inc(cand_ready, 1)


def kernel(**inputs):
    import concourse.bacc as _bacc
    from concourse.bass_utils import run_bass_kernel_spmd as _run

    a = {k: np.asarray(v) for k, v in inputs.items()}
    L = DEPTH

    def chunks(w, parts):
        return w.reshape(L, parts, P, -1).transpose(0, 2, 1, 3)

    def columns(v_):
        return v_.reshape(L, -1, P).transpose(0, 2, 1)

    const = np.zeros((P, C_W), np.float32)
    const[:, C_ID:C_ID + P] = np.eye(P)
    const[:, C_IOTA:C_IOTA + NK] = np.arange(NK)
    const[:, C_INV:C_INV + HD // 2] = 10000.0 ** (-np.arange(0, HD, 2, dtype=np.float32) / HD)
    const[:, C_INV + HD // 2:C_INV + NF] = 10000.0 ** (-np.arange(0, ROPE, 2, dtype=np.float32) / ROPE)
    query = np.arange(SEQ).reshape(NT, P, 1)
    far = np.abs(query - np.arange(SEQ)) > WINDOW
    const[:, C_MASK:C_MASK + NT * SEQ] = np.where(far, NEG_BIG, 0.0).transpose(1, 0, 2).reshape(P, -1)
    const[:, C_EPS] = EPS

    vec = np.concatenate(
        [columns(a["norm_mix"]), columns(a["norm_ffn"]), columns(a["q_norm"]), columns(a["kv_norm"]),
         columns(a["grp_norm"]), columns(a["conv_w"].reshape(L, -1)), columns(a["conv_b"]),
         columns(a["lru_ba"].reshape(L, -1)), columns(a["lru_bx"].reshape(L, -1)),
         columns(a["lru_lambda"].reshape(L, -1)), np.broadcast_to(a["swa_sink"][:, None, :], (L, P, H_SWA))], axis=2)
    win = chunks(a["w_in"], DC)
    win = np.concatenate([win[..., :IN_A].reshape(L, P, -1), win[..., IN_A:].reshape(L, P, -1)], axis=2)
    gates = np.stack([a["lru_wa"], a["lru_wx"]], axis=2).reshape(L, 2, 2, LC, 2, 64, 64)
    gates = gates.transpose(0, 4, 5, 1, 2, 3, 6).reshape(L, P, 12, 64)
    wq = a["peer_wq"].reshape(L, DC, P, 2 * PH, P).transpose(0, 2, 3, 1, 4)
    sub = a["peer_subkeys"].transpose(0, 3, 1, 2)
    pu = a["peer_u"].reshape(L, NK, NK, DC, P).transpose(0, 1, 4, 3, 2).reshape(L, NK, P, D)
    arrays = {
        "x": a["x"].reshape(NT, P, D).transpose(1, 0, 2), "pos": a["positions"].reshape(NT, P).T,
        "const": const, "vec": vec, "w_in": win,
        "w_uq": chunks(a["w_uq"], 2), "w_ukv": a["w_ukv"], "w_lru": gates, "w_out": chunks(a["w_out"], DC),
        "w_q": wq, "sub_k": sub, "peer_u": pu, "peer_v": a["peer_v"].reshape(L, NK, P, D),
        "norm_f": a["norm_final"]}
    arrays = {k + "_dram": np.ascontiguousarray(v_) for k, v_ in arrays.items()}

    nc = _bacc.Bacc("TRN2", target_bir_lowering=False, num_devices=1)
    args = [nc.dram_tensor(k, v_.shape, mybir.dt.from_np(v_.dtype), kind="ExternalInput").ap()
            for k, v_ in arrays.items()]
    spill = nc.dram_tensor("x_spill_dram", (P, NT, D), F32, kind="Internal").ap()
    out = nc.dram_tensor("out_dram", (P, NT, D), F32, kind="ExternalOutput").ap()
    encoder(nc, *args, spill, out)
    r = _run(nc, [arrays], core_ids=[0])
    got = r.results[0]["out_dram"]
    return got.transpose(1, 0, 2).reshape(1, SEQ, D)
```

```python
from contextlib import ExitStack

import numpy as np

import concourse.bass as bass
from concourse import mybir

EPS = 1e-6
NEG_BIG = -1e30
P = 128
D = 1024
DC = D // P
SEQ = 256
NT = SEQ // P
DEPTH = 2
H_MLA, NOPE, ROPE, V_MLA = 6, 64, 32, 64
QK = NOPE + ROPE
Q_RANK, KV_RANK = 256, 128
MLA_W = H_MLA * V_MLA
LRU_W = 384
LC = LRU_W // P
LRU_C = 8.0
HALO = 3
H_SWA, KV_SWA, HD = 4, 2, 64
SWA_W = H_SWA * HD
WINDOW = 128
IN_A = Q_RANK + KV_RANK + ROPE + SWA_W + 2 * KV_SWA * HD
IN_W = IN_A + 2 * LRU_W
SQ0 = Q_RANK + KV_RANK + ROPE
SV0 = SQ0 + SWA_W + KV_SWA * HD
KR0 = Q_RANK + KV_RANK
PH = 8
NK = 128
TOP = 16
SLOTS = PH * TOP
PA, PB = 3, 4
PAIRS = PA * TOP + (TOP - PA) * PB
GT = 8
HK = NK // 2
RAWS = 4
F32 = mybir.dt.float32
F32R = mybir.dt.float32r
U32 = mybir.dt.uint32
I32 = mybir.dt.int32
ALU = mybir.AluOpType
ACT = mybir.ActivationFunctionType
AX = mybir.AxisListType
MAX_NEG = -3.0e38
ROUND = 1.5 * 2.0 ** 23
TWO_PI_1, TWO_PI_2 = 6.28125, 0.00193500518798828125
TWO_PI_3 = 2 * np.pi - TWO_PI_1 - TWO_PI_2
PI_IN = 3.1415925

C_ID, C_IOTA, C_INV, C_MASK = 0, 128, 256, 304
C_EPS = C_MASK + NT * SEQ
C_W = C_EPS + 1
NF = HD // 2 + ROPE // 2
V_NMIX, V_NFFN, V_QN, V_KVN, V_GRP = 0, 8, 16, 18, 19
V_CW, V_CB, V_BA, V_BX, V_LAM, V_SINK = 27, 39, 42, 48, 54, 60
V_W = 64


def encoder(nc, x_in, pos_in, const_in, vec_in, w_in, w_uq, w_ukv, w_lru, w_out, w_q, sub_k,
            peer_u, peer_v, norm_f, x_spill, gates_dram, out):
    ctx = ExitStack()
    with ctx:
        def sem(name):
            return ctx.enter_context(nc.semaphore(name))

        base_byte = -(-nc.sbuf_base // 32) * 32
        ctx.enter_context(nc.sbuf_tensor("arena", [P, 53200], F32))

        def at(name, word, shape, dt=F32):
            return nc.alloc_sbuf_tensor_at(name, shape, dt, offset=base_byte + 4 * word)

        const = at("const", 0, [P, C_W])
        cos = at("cos", 824, [P, NT, NF])
        sin = at("sin", 920, [P, NT, NF])
        vec = at("vec", 1016, [P, V_W])
        skT = at("skT", 1080, [P, 2, NK])
        stat = at("stat", 1336, [P, 256])
        x = at("x", 1600, [P, NT, D])
        xT = at("xT", 3648, [P, DC, SEQ])
        mixT = at("mixT", 5696, [P, DC, SEQ])
        ARENA_A = 7744
        ARENA_B = ARENA_A + 32768
        win_a = at("win_a", ARENA_A, [P, DC, IN_A])
        win_b = at("win_b", ARENA_A + DC * IN_A, [P, DC, 2 * LRU_W])
        wq = at("wq", ARENA_A, [P, 2 * PH, DC, P])
        wout = at("wout", ARENA_A + 16384, [P, DC, D])
        wuq = at("wuq", ARENA_A + 24576, [P, 2, H_MLA * QK])
        wukv = at("wukv", ARENA_A + 25728, [P, H_MLA * (NOPE + V_MLA)])
        wlru = at("wlru", ARENA_A + 26496, [P, 12, P])
        xs = at("xs", ARENA_A + 28032, [P, NT, D])
        ropeA = at("ropeA", ARENA_A + 28032, [P, 384])
        ropeB = at("ropeB", ARENA_A + 28032 + 384, [P, 384])
        ones = at("ones", ARENA_A + 32384, [P, P])
        qb = at("qb", ARENA_A + 30080, [P, NT, H_MLA, QK])
        kb = at("kb", ARENA_A + 31232, [P, NT, H_MLA, QK])
        hot = at("hot", ARENA_A, [P, 2, NT, TOP, TOP])
        gates = at("gates", ARENA_A, [P, SEQ * HK])
        act_g = at("act_g", ARENA_A + HK * SEQ, [P, HK * SEQ])
        lxp = at("lxp", ARENA_A, [P, LC, SEQ + HALO])
        xc = at("xc", ARENA_A + 784, [P, LC, SEQ])
        lr = at("lr", ARENA_A + 1552, [P, 2, LC, SEQ])
        li = at("li", ARENA_A + 3088, [P, 2, LC, SEQ])
        la = at("la", ARENA_A + 4624, [P, 2, LC, SEQ])
        lt = at("lt", ARENA_A + 6160, [P, 2, LC, SEQ])
        proj = at("proj", ARENA_B, [P, NT, IN_A])
        cT = at("cT", ARENA_B + 1856, [P, 3, SEQ])
        qkT = at("qkT", ARENA_B + 2624, [P, H_MLA, 2 * SEQ])
        vb = at("vb", ARENA_B + 5696, [P, NT, H_MLA, V_MLA])
        sT = at("sT", ARENA_B + 6464, [P, 6, SEQ])
        o = at("o", ARENA_B + 8000, [P, NT, MLA_W + SWA_W])
        pr = at("pr", ARENA_B + 9280, [P, 2, NT * SEQ])
        prT = at("prT", ARENA_B + 10304, [P, 2, 2 * SEQ])
        lg = at("lg", ARENA_B + 11328, [P, LC, SEQ])
        sw = at("sw", ARENA_B + 12096, [P, NT * SEQ])
        raw = at("raw", ARENA_B, [P, RAWS, D])
        x_back = at("x_back", ARENA_B, [P, NT, D])
        hl = [at(f"hl{s}", ARENA_B + 4096 + 2048 * s, [P, 2, D], F32R) for s in range(2)]
        ROUTE = ARENA_B + 8192
        qT = at("qT", ROUTE, [P, 2, SEQ])
        tmp = at("tmp", ROUTE + 512, [P, SEQ])
        top_v = at("top_v", ROUTE + 768, [P, NT, PH, 2, TOP])
        top_i = at("top_i", ROUTE + 1280, [P, NT, PH, 2, TOP], U32)
        top_f = at("top_f", ROUTE + 1792, [P, NT, PH, 2, TOP])
        sc = at("sc", ROUTE + 2304, [P, NT, PH, TOP])
        cand = at("cand", ROUTE + 2560, [P, 2, NT, PAIRS])
        ci = at("ci", ROUTE + 3584, [P, NT, PH, TOP], U32)
        egT = at("egT", ROUTE + 3728, [P, 3, SEQ])
        one_j = at("one_j", ROUTE, [P, 2, GT, NK])
        gate_out = at("gate_out", ROUTE + 2048, [P, 2, GT * HK])
        p_hl = at("p_hl", ROUTE, [P, 2, 2, 2 * SEQ], F32R)
        ca = at("ca", 1600, [P, 2, NT, PH, TOP], U32)
        cf = at("cf", 2112, [P, 2, NT, PH, TOP])
        eg = at("eg", 2624, [P, 3, NT, PH, TOP])
        one_i = at("one_i", 1600, [P, 2, GT, NK])
        x_lo = at("x_lo", 3648, [P, DC, SEQ], F32R)
        x_hi = at("x_hi", 5696, [P, DC, SEQ], F32R)
        bank = [ctx.enter_context(nc.psum_tensor(f"bank{b}", [P, 512], F32)) for b in range(8)]

        ident = const[:, C_ID:C_ID + P]
        iota = const[:, C_IOTA:C_IOTA + NK]
        eps = const[:, C_EPS:C_EPS + 1]
        ang = at("ang", ARENA_B, [P, 5, NT, NF])
        posi = at("posi", ARENA_B + 600, [P, NT], I32)
        posf = at("posf", ARENA_B + 608, [P, NT])
        norm_fb = at("norm_fb", ARENA_A, [P, D])

        s_const, s_pos, s_x, s_vec, s_win_a, s_win_b, s_wuq, s_wukv, s_lru, s_wout, s_wq1, s_wq0, s_sk = (
            sem("ld_" + n) for n in ("const", "pos", "x", "vec", "win_a", "win_b", "wuq", "wukv", "lru",
                                     "wout", "wq1", "wq0", "sk"))
        final = sem("final")
        gates_out, gates_back = [sem(f"gates_out{s}") for s in range(2)], sem("gates_back")
        s_nf, s_spill, s_back, s_out = sem("ld_nf"), sem("spilled"), sem("x_back"), sem("stored")
        ld_raw = [sem(f"ld_raw{s}") for s in range(RAWS)]
        zeroed, ones_ready = sem("zeroed"), sem("ones_ready")
        ang_ready, trig = sem("ang_ready"), sem("trig")
        x_ready, rms_ready, xs_ready, xT_ps, xT_ready = (
            sem(n) for n in ("x_ready", "rms_ready", "xs_ready", "xT_ps", "xT_ready"))
        proj_ps, proj_a, proj_d, lru_ps, lx_ready, lg_ready = (
            sem(n) for n in ("proj_ps", "proj_a", "proj_d", "lru_ps", "lx_ready", "lg_ready"))
        c_rms, cn_ready, cT_ps, cT_ready, q_ps, kv_ps, q_nope, q_rope, kv_a, k_rope, s_rope = (
            sem(n) for n in ("c_rms", "cn_ready", "cT_ps", "cT_ready", "q_ps", "kv_ps", "q_nope", "q_rope",
                             "kv_a", "k_rope", "s_rope"))
        qk_ps, qk_ready, sT_ps, sT_ready = (sem(n) for n in ("qk_ps", "qk_ready", "sT_ps", "sT_ready"))
        lam_u, lam_ready, xc_ready, gates_ps, gates_ready, a_ready, t_ready, bq_ready, b_root = (
            sem(n) for n in ("lam_u", "lam_ready", "xc_ready", "gates_ps", "gates_ready", "a_ready",
                             "t_ready", "bq_ready", "b_root"))
        osq_ready, osum_ps, orms = sem("osq_ready"), sem("osum_ps"), sem("orms")
        sc_ps, negm, p_ready, pt_ps, pt_ready, o_ps, o_done = (
            sem(n) for n in ("sc_ps", "negm", "p_ready", "pt_ps", "pt_ready", "o_ps", "o_done"))
        o_rms, on_ready, oT_ps, mix_a, mix_d, out_ps, x_mid = (
            sem(n) for n in ("o_rms", "on_ready", "oT_ps", "mix_a", "mix_d", "out_ps", "x_mid"))
        ph_q, ph_qT, ph_s, top1, cand_ready, top2, ge_in, ge_out, eg_ready, egT_ps, egT_ready = (
            sem(n) for n in ("ph_q", "ph_qT", "ph_s", "top1", "cand_ready", "top2", "ge_in", "ge_out",
                             "eg_ready", "egT_ps", "egT_ready"))
        xhi_ready, xlo_ready, one_eq, one_j_ready, one_i_ready, gate_ps, gate_ready = (
            sem(n) for n in ("xhi_ready", "xlo_ready", "one_eq", "one_j_ready", "one_i_ready", "gate_ps", "gate_ready"))
        hi_done, lo_done, blk_done, gelu_done, pf_done, p_hi, p_lo = (
            sem(n) for n in ("hi_done", "lo_done", "blk_done", "gelu_done", "pf_done", "p_hi", "p_lo"))

        def q0(lay, half):
            return (2 * lay + half) * 2 * HK

        def halves(lay, half):
            return 2 * lay + half

        NG = SEQ // GT
        GB = GT // 2
        U_LOW = (HK - NG) // 4
        TURNS = HK // 4

        def lru_bank(j):
            c = j % LC
            return bank[4 + 2 * (j // LC) + c // 2][:, (c % 2) * SEQ:(c % 2 + 1) * SEQ]

        def mix_bank(j):
            b, w = (j // 2, j % 2) if j < 3 else (2, j - 3)
            return bank[b][:, w * SEQ:(w + 1) * SEQ]

        block = ctx.enter_context(nc.Block())

        @block.sync
        def _(sp):
            sp.dma_start(x[:], x_in).then_inc(s_x, 16)
            sp.dma_start(const[:], const_in).then_inc(s_const, 16)
            sp.dma_start(posi[:], pos_in).then_inc(s_pos, 16)
            for lay in range(DEPTH):
                if lay == 0:
                    sp.dma_start(vec[:], vec_in[lay]).then_inc(s_vec, 16)
                    for c in range(DC):
                        sp.dma_start(win_a[:, c], w_in[lay, :, c * IN_A:(c + 1) * IN_A]).then_inc(s_win_a, 16)
                    sp.dma_start(win_b[:], w_in[lay, :, DC * IN_A:]).then_inc(s_win_b, 16)
                else:
                    sp.wait_ge(p_lo, halves(lay, 0) * HK // 2)
                sp.dma_start(wuq[:], w_uq[lay]).then_inc(s_wuq, 16)
                sp.dma_start(wukv[:], w_ukv[lay]).then_inc(s_wukv, 16)
                sp.wait_ge(zeroed, lay + 1)
                sp.dma_start(wlru[0:64, :, 0:64], w_lru[lay, 0:64]).then_inc(s_lru, 16)
                sp.dma_start(wlru[64:P, :, 64:P], w_lru[lay, 64:P]).then_inc(s_lru, 16)
                sp.dma_start(wout[:], w_out[lay]).then_inc(s_wout, 16)
                sp.dma_start(skT[:], sub_k[lay]).then_inc(s_sk, 16)
                sp.wait_ge(lru_ps, 6 * (lay + 1))
                sp.wait_ge(proj_ps, 4 * (lay + 1))
                sp.dma_start(wq[:, PH:], w_q[lay, :, PH:]).then_inc(s_wq1, 16)
                sp.wait_ge(mix_d, 5 * (lay + 1))
                sp.dma_start(wq[:, 0:PH], w_q[lay, :, 0:PH]).then_inc(s_wq0, 16)
                sp.wait_ge(x_mid, 4 * (lay + 1))
                sp.dma_start(x_spill, x[:]).then_inc(s_spill, 16)

                for s in range(RAWS):
                    sp.dma_start(raw[:, s], peer_u[lay, s]).then_inc(ld_raw[s], 16)
                for half in range(2):
                    for table, run in ((peer_u, 0), (peer_v, HK)):
                        first = 1 if half == 0 and run == 0 else 0

                        def turn(m):
                            for s in range(RAWS):
                                sp.wait_ge(lo_done, m * 4 + (q0(lay, half) + run + s - 3))
                                sp.dma_start(raw[:, s], table[lay, bass.ds(m * 4 + (half * HK + s), 1)]
                                             .rearrange("a p e -> p (a e)")).then_inc(ld_raw[s], 16)

                        def gates_in(m, g):
                            sp.dma_start(gates[:, bass.ds(m * (2 * GT * HK) + g * GT * HK, 2 * GT * HK)]
                                         .rearrange("p (g e) -> p g e", g=2),
                                         gates_dram[bass.ds(m * 2 + g, 2)].rearrange("g p e -> p g e")
                                         ).then_inc(gates_back, 16)

                        MID = TURNS // 2
                        if half == 0 and run:
                            with sp.Fori(0, MID) as m:
                                turn(m)
                            sp.wait_ge(pf_done, (halves(lay, 0) + 1) * TURNS)
                            for s in range(2):
                                sp.wait_ge(gates_out[s], 16 * (NG // 2) * (lay + 1))
                            with sp.Fori(MID, TURNS) as m:
                                turn(m)
                                gates_in(m, -2 * MID)
                        elif half and not run:
                            with sp.Fori(0, NG // 2 - MID) as m:
                                turn(m)
                                gates_in(m, 2 * MID)
                            with sp.Fori(NG // 2 - MID, TURNS) as m:
                                turn(m)
                        elif half and lay + 1 < DEPTH:
                            with sp.Fori(0, TURNS - DC) as m:
                                turn(m)
                            sp.wait_ge(pf_done, (halves(lay, 1) + 1) * TURNS)
                            sp.dma_start(vec[:], vec_in[lay + 1]).then_inc(s_vec, 16)
                            with sp.Fori(TURNS - DC, TURNS) as m:
                                turn(m)
                                c = m - (TURNS - DC)
                                sp.dma_start(win_a[:, bass.ds(c, 1)].rearrange("p a n -> p (a n)"),
                                             w_in[lay + 1, :, bass.ds(c * IN_A, IN_A)]).then_inc(s_win_a, 16)
                            sp.dma_start(win_b[:], w_in[lay + 1, :, DC * IN_A:]).then_inc(s_win_b, 16)
                        else:
                            with sp.Fori(first, TURNS) as m:
                                turn(m)
                sp.wait_ge(lo_done, q0(lay + 1, 0))
                sp.wait_ge(s_spill, 16 * (lay + 1))
                sp.dma_start(x_back[:], x_spill).then_inc(s_back, 16)
            sp.wait_ge(pf_done, 2 * DEPTH * TURNS)
            sp.dma_start(norm_fb[:], norm_f.partition_broadcast(P)).then_inc(s_nf, 16)
            sp.wait_ge(final, NT)
            sp.dma_start(out, xs[:]).then_inc(s_out, 16)
            sp.wait_ge(s_out, 16)

        @block.tensor
        def _(pe):
            mm = nc.tensor.matmul
            tr = nc.tensor.transpose

            def transpose_x(o_):
                pe.wait_ge(xs_ready, 2 * (o_ + 1))
                for c in range(DC):
                    b, w = bank[4 + c // 2], (c % 2) * SEQ
                    for n in range(NT):
                        last = tr(b[:, w + n * P:w + (n + 1) * P], xs[:, n, c * P:(c + 1) * P], ident)
                    if c % 2:
                        last.then_inc(xT_ps, 1)

            pe.wait_ge(s_const, 16)
            for lay in range(DEPTH):
                transpose_x(2 * lay)

                pe.wait_ge(s_win_a, 16 * DC * (lay + 1))
                pe.wait_ge(xT_ready, 8 * (2 * lay + 1))
                HALF = IN_A // 2
                for n in range(NT):
                    for half in range(2):
                        for c in range(DC):
                            last = mm(bank[2 * n + half][:, 0:HALF], xT[:, c, n * P:(n + 1) * P],
                                      win_a[:, c, half * HALF:(half + 1) * HALF], start=c == 0, stop=c == DC - 1)
                        last.then_inc(proj_ps, 1)
                pe.wait_ge(s_win_b, 16 * (lay + 1))
                for j in range(2 * LC):
                    for c in range(DC):
                        last = mm(lru_bank(j),
                                  win_b[:, c, j * P:(j + 1) * P], xT[:, c, :], start=c == 0, stop=c == DC - 1)
                    last.then_inc(lru_ps, 1)

                pe.wait_ge(cn_ready, lay + 1)
                for j in range(3):
                    for n in range(NT):
                        last = tr(bank[j // 2][:, (j % 2) * SEQ + n * P:(j % 2) * SEQ + (n + 1) * P],
                                  proj[:, n, j * P:(j + 1) * P], ident)
                last.then_inc(cT_ps, 1)
                pe.wait_ge(cT_ready, 3 * (lay + 1))
                pe.wait_ge(s_wuq, 16 * (lay + 1))
                W3 = 3 * QK
                for n in range(NT):
                    for half in range(2):
                        for c in range(2):
                            last = mm(bank[2 * n + half][:, 0:W3], cT[:, c, n * P:(n + 1) * P],
                                      wuq[:, c, half * W3:(half + 1) * W3], start=c == 0, stop=c == 1)
                        last.then_inc(q_ps, 1)
                pe.wait_ge(lx_ready, 3 * (lay + 1))
                pe.wait_ge(lg_ready, 3 * (lay + 1))
                pe.wait_ge(s_wukv, 16 * (lay + 1))
                W3 = 3 * (NOPE + V_MLA)
                for n in range(NT):
                    for half in range(2):
                        mm(bank[4 + 2 * n + half][:, 0:W3], cT[:, 2, n * P:(n + 1) * P],
                           wukv[:, half * W3:(half + 1) * W3], start=True, stop=True).then_inc(kv_ps, 1)

                pe.wait_ge(q_nope, 4 * (lay + 1))
                pe.wait_ge(q_rope, 4 * (lay + 1))
                pe.wait_ge(kv_a, 4 * (lay + 1))
                pe.wait_ge(k_rope, 2 * (lay + 1))
                for h in range(H_MLA):
                    if h >= 4:
                        pe.wait_ge(qk_ready, H_MLA * lay + h - 3)
                    for w, src in enumerate((qb, kb)):
                        for n in range(NT):
                            last = tr(bank[h % 4][0:QK, w * SEQ + n * P:w * SEQ + (n + 1) * P],
                                      src[:, n, h, :], ident)
                    last.then_inc(qk_ps, 1)
                pe.wait_ge(s_rope, 2 * (lay + 1))
                for j in range(H_SWA + KV_SWA):
                    for n in range(NT):
                        last = tr(bank[4 + j // 2][0:HD, (j % 2) * SEQ + n * P:(j % 2) * SEQ + (n + 1) * P],
                                  proj[:, n, SQ0 + j * HD:SQ0 + (j + 1) * HD], ident)
                    if j % 2:
                        last.then_inc(sT_ps, 1)

                pe.wait_ge(xc_ready, lay + 1)
                pe.wait_ge(s_lru, 32 * (lay + 1))
                pe.wait_ge(sT_ready, 3 * (lay + 1))
                for g in range(12):
                    if g >= 4:
                        pe.wait_ge(gates_ready, 12 * lay + 2 * (g // 2) - 2)
                    mm(bank[4 + (g // 2) % 2][:, (g % 2) * SEQ:(g % 2 + 1) * SEQ], wlru[:, g, :],
                       xc[:, g % LC, :], start=True, stop=True).then_inc(gates_ps, 1)

                NH = H_MLA + H_SWA

                def scores(h):
                    if h >= 2:
                        pe.wait_ge(p_ready, NH * lay + h - 1)
                    for n in range(NT):
                        if h < H_MLA:
                            q_, k_ = qkT[0:QK, h, n * P:(n + 1) * P], qkT[0:QK, h, SEQ:]
                        else:
                            g = h - H_MLA
                            q_, k_ = sT[0:HD, g, n * P:(n + 1) * P], sT[0:HD, H_SWA + g // 2, :]
                        last = mm(bank[h % 2][:, n * SEQ:(n + 1) * SEQ], q_, k_, start=True, stop=True)
                    last.then_inc(sc_ps, 1)

                def transpose_p(h):
                    pe.wait_ge(p_ready, NH * lay + h + 1)
                    if h >= 2:
                        pe.wait_ge(pt_ready, NH * lay + h - 1)
                    for kt in range(NT):
                        for n in range(NT):
                            last = tr(bank[2 + h % 2][:, (kt * NT + n) * P:(kt * NT + n + 1) * P],
                                      pr[:, h % 2, n * SEQ + kt * P:n * SEQ + (kt + 1) * P], ident)
                    last.then_inc(pt_ps, 1)

                def weigh_v(h):
                    pe.wait_ge(pt_ready, NH * lay + h + 1)
                    if h >= 2:
                        pe.wait_ge(o_done, NH * lay + h - 1)
                    for n in range(NT):
                        for kt in range(NT):
                            if h < H_MLA:
                                v_ = vb[:, kt, h, :]
                            else:
                                g = (h - H_MLA) // 2
                                v_ = proj[:, kt, SV0 + g * HD:SV0 + (g + 1) * HD]
                            last = mm(bank[6 + h % 2][:, n * HD:(n + 1) * HD],
                                      prT[:, h % 2, (kt * NT + n) * P:(kt * NT + n + 1) * P], v_,
                                      start=kt == 0, stop=kt == NT - 1)
                    last.then_inc(o_ps, 1)

                pe.wait_ge(qk_ready, H_MLA * (lay + 1))
                scores(0)
                for h in range(NH):
                    if h + 1 < NH:
                        scores(h + 1)
                    transpose_p(h)
                    if h:
                        weigh_v(h - 1)
                weigh_v(NH - 1)

                pe.wait_ge(ones_ready, lay + 1)
                pe.wait_ge(osq_ready, lay + 1)
                for c in range(LC):
                    last = mm(bank[4][:, 0:SEQ], ones[:], lt[:, 0, c, :], start=c == 0, stop=c == LC - 1)
                last.then_inc(osum_ps, 1)

                pe.wait_ge(on_ready, 2 * (lay + 1))
                for j in range(5):
                    for n in range(NT):
                        last = tr(mix_bank(j)[:, n * P:(n + 1) * P],
                                  o[:, n, j * P:(j + 1) * P], ident)
                last.then_inc(oT_ps, 1)
                pe.wait_ge(mix_d, 5 * (lay + 1))
                pe.wait_ge(mix_a, 3 * (lay + 1))
                pe.wait_ge(s_wout, 16 * (lay + 1))
                for n in range(NT):
                    for half in range(2):
                        for c in range(DC):
                            last = mm(bank[4 + 2 * n + half][:], mixT[:, c, n * P:(n + 1) * P],
                                      wout[:, c, half * 512:(half + 1) * 512], start=c == 0, stop=c == DC - 1)
                        last.then_inc(out_ps, 1)

                transpose_x(2 * lay + 1)

                pe.wait_ge(xT_ready, 8 * (2 * lay + 2))
                pe.wait_ge(s_sk, 16 * (lay + 1))
                pe.wait_ge(s_wq1, 16 * (lay + 1))

                def key_scores(i):
                    pe.wait_ge(ph_qT, 16 * lay + i + 1)
                    if i >= 2:
                        pe.wait_ge(top1, 16 * lay + i - 1)
                    for n in range(NT):
                        last = mm(bank[2 + i % 2][:, n * NK:(n + 1) * NK], qT[:, i % 2, n * P:(n + 1) * P],
                                  skT[:, i % 2, :], start=True, stop=True)
                    last.then_inc(ph_s, 1)

                for i in range(2 * PH):
                    blk = (i + PH) % (2 * PH)
                    if i == PH:
                        pe.wait_ge(s_wq0, 16 * (lay + 1))
                    if i >= 2:
                        pe.wait_ge(ph_qT, 16 * lay + i - 1)
                    for c in range(DC):
                        last = mm(bank[i % 2][:, 0:SEQ], wq[:, blk, c, :], xT[:, c, :], start=c == 0,
                                  stop=c == DC - 1)
                    last.then_inc(ph_q, 1)
                    if i:
                        key_scores(i - 1)
                key_scores(2 * PH - 1)

                def u_block(s, q, g, wait_gelu=True):
                    pe.wait_ge(hi_done, q + 1)
                    if wait_gelu:
                        pe.wait_ge(gelu_done, g - 1)
                    u_ = hl[s % 2][:].rearrange("p w (c e) -> p w c e", c=DC)
                    for c in range(DC):
                        for xh in (x_hi, x_lo):
                            mm(bank[4 + s % 2][:, 0:SEQ], u_[:, 0, c, :], xh[:, c, :],
                               start=c == 0 and xh is x_hi, stop=False)
                    pe.wait_ge(lo_done, q + 1)
                    for c in range(DC):
                        last = mm(bank[4 + s % 2][:, 0:SEQ], u_[:, 1, c, :], x_hi[:, c, :], start=False,
                                  stop=c == DC - 1)
                    last.then_inc(blk_done, 1)

                def gate_group(s, g, wait_gate=True):
                    pe.wait_ge(one_i_ready, g + 1)
                    pe.wait_ge(one_j_ready, g + 1)
                    for b in range(2):
                        if wait_gate:
                            pe.wait_ge(gate_ready, g * 2 + (b - 1))
                        for t in range(GB):
                            last = mm(bank[6 + b][:, t * NK:(t + 1) * NK], one_j[:, s % 2, b * GB + t, :],
                                      one_i[:, s % 2, b * GB + t, :], start=True, stop=True)
                        last.then_inc(gate_ps, 1)

                def v_block(s, q, pair, first=False, last_block=False):
                    pe.wait_ge(hi_done, q + 1)
                    if s % 2 == 0:
                        pe.wait_ge(p_lo, pair + 1)
                    for ph, vh in ((0, 0), (1, 0), (0, 1)):
                        if vh:
                            pe.wait_ge(lo_done, q + 1)
                        for n in range(NT):
                            for w in range(2):
                                t0 = (s % 2) * SEQ + n * P
                                last = mm(bank[2 * n + w][:], p_hl[:, s // 2, ph, t0:t0 + P],
                                          hl[s % 2][:, vh, w * 512:(w + 1) * 512], start=first and ph == vh,
                                          stop=last_block and vh == 1)
                    last.then_inc(blk_done, 1)

                pe.wait_ge(xhi_ready, lay + 1)
                pe.wait_ge(xlo_ready, lay + 1)
                for half in range(2):
                    Q, G, H = q0(lay, half), halves(lay, half) * HK, lay * NG
                    for s in range(4):
                        u_block(s, Q + s, G + s, G + s > 1)
                    with pe.Fori(1, TURNS if half else U_LOW) as m:
                        for s in range(4):
                            u_block(s, m * 4 + (Q + s), m * 4 + (G + s))
                    if half == 0:
                        pe.wait_ge(eg_ready, lay + 1)
                        for w in range(3):
                            for n in range(NT):
                                last = tr(bank[6 + w // 2][:, (w % 2) * SEQ + n * P:(w % 2) * SEQ + (n + 1) * P],
                                          eg[:, w, n].rearrange("p h s -> p (h s)"), ident)
                        last.then_inc(egT_ps, 1)
                        for s in range(4):
                            u_block(s, Q + 4 * U_LOW + s, G + 4 * U_LOW + s)
                            gate_group(s, H + s, H + s > 0)
                        with pe.Fori(1, NG // 4) as m:
                            for s in range(4):
                                u_block(s, m * 4 + (Q + 4 * U_LOW + s), m * 4 + (G + 4 * U_LOW + s))
                                gate_group(s, m * 4 + (H + s))
                    V, R = Q + HK, halves(lay, half) * HK // 2
                    for s in range(4):
                        v_block(s, V + s, R + s // 2, first=half == 0 and s == 0)
                    with pe.Fori(1, TURNS - 1) as m:
                        for s in range(4):
                            v_block(s, m * 4 + (V + s), m * 2 + (R + s // 2))
                    for s in range(4):
                        v_block(s, V + HK - 4 + s, R + HK // 2 - 2 + s // 2, last_block=half == 1 and s == 3)

        @block.scalar
        def _(act):
            af = nc.scalar.activation

            def rms(o_):
                act.wait_ge(x_ready, 4 * (o_ + 1))
                for n in range(NT):
                    af(xs[:, n, :], x[:, n, :], ACT.Square, accum_out=stat[:, n:n + 1])
                act.drain()
                af(stat[:, 2:4], stat[:, 0:2], ACT.Sqrt, bias=eps, scale=1.0 / D).then_inc(rms_ready, 1)

            def copy_xT(o_, gain):
                for b in (0, 2):
                    act.wait_ge(xT_ps, 4 * o_ + b + 1)
                    for c in (2 * b, 2 * b + 1):
                        af(xT[:, c, :], bank[4 + b][:, (c % 2) * SEQ:(c % 2 + 1) * SEQ], ACT.Copy,
                           scale=vec[:, gain + c:gain + c + 1]).then_inc(xT_ready, 1)

            act.wait_ge(s_const, 16)
            act.wait_ge(ang_ready, 1)
            af(sin[:], ang[:, 1], ACT.Sin).then_inc(trig, 1)
            af(cos[:], ang[:, 2], ACT.Sin).then_inc(trig, 1)
            for lay in range(DEPTH):
                rms(2 * lay)
                act.wait_ge(s_vec, 16 * (lay + 1))
                af(stat[:, 16:22], vec[:, V_LAM:V_LAM + 6], ACT.Abs)
                act.drain()
                af(stat[:, 16:22], stat[:, 16:22], ACT.Exp, scale=-1.0).then_inc(lam_u, 1)
                copy_xT(2 * lay, V_NMIX)

                HALF = IN_A // 2
                for half in range(2):
                    act.wait_ge(proj_ps, 4 * lay + half + 1)
                    af(proj[:, 0, half * HALF:(half + 1) * HALF], bank[half][:, 0:HALF],
                       ACT.Copy).then_inc(proj_a, 1)
                act.wait_ge(proj_d, 2 * (lay + 1))
                act.drain()
                for w, (c0, c1) in enumerate(((0, Q_RANK), (Q_RANK, KR0))):
                    for n in range(NT):
                        af(xs[:, 0, 0:c1 - c0], proj[:, n, c0:c1], ACT.Square,
                           accum_out=stat[:, 4 + 2 * w + n:5 + 2 * w + n])
                        act.drain()
                af(stat[:, 8:10], stat[:, 4:6], ACT.Sqrt, bias=eps, scale=1.0 / Q_RANK)
                af(stat[:, 10:12], stat[:, 6:8], ACT.Sqrt, bias=eps, scale=1.0 / KV_RANK).then_inc(c_rms, 1)
                for c in range(LC):
                    j = LC + c
                    act.wait_ge(lru_ps, 6 * (lay + 1))
                    af(lg[:, c, :], lru_bank(j), ACT.Gelu).then_inc(lg_ready, 1)
                act.wait_ge(cT_ps, lay + 1)
                for j in range(3):
                    g = V_QN + j if j < 2 else V_KVN
                    af(cT[:, j, :], bank[j // 2][:, (j % 2) * SEQ:(j % 2 + 1) * SEQ], ACT.Copy,
                       scale=vec[:, g:g + 1]).then_inc(cT_ready, 1)
                for n in range(NT):
                    for half in range(2):
                        act.wait_ge(q_ps, 4 * lay + 2 * n + half + 1)
                        b = bank[2 * n + half][:, 0:3 * QK].rearrange("p (h d) -> p h d", h=3)
                        af(qb[:, n, 3 * half:3 * half + 3, 0:NOPE], b[:, :, 0:NOPE], ACT.Copy).then_inc(q_nope, 1)
                for n in range(NT):
                    for half in range(2):
                        act.wait_ge(kv_ps, 4 * lay + 2 * n + half + 1)
                        b = bank[4 + 2 * n + half][:, 0:3 * (NOPE + V_MLA)].rearrange("p (h d) -> p h d", h=3)
                        af(kb[:, n, 3 * half:3 * half + 3, 0:NOPE], b[:, :, 0:NOPE], ACT.Copy)
                        af(vb[:, n, 3 * half:3 * half + 3, :], b[:, :, NOPE:], ACT.Copy).then_inc(kv_a, 1)
                for h in range(H_MLA):
                    act.wait_ge(qk_ps, H_MLA * lay + h + 1)
                    af(qkT[0:QK, h, :], bank[h % 4][0:QK, :], ACT.Copy).then_inc(qk_ready, 1)

                for g in range(12):
                    d, kind, c = g // 6, (g // 3) % 2, g % 3
                    act.wait_ge(gates_ps, 12 * lay + 2 * (g // 2) + 2)
                    v0 = (V_BX if kind else V_BA) + 3 * d + c
                    af((li if kind else lr)[:, d, c, :], bank[4 + (g // 2) % 2][:, (g % 2) * SEQ:(g % 2 + 1) * SEQ],
                       ACT.Sigmoid, bias=vec[:, v0:v0 + 1]).then_inc(gates_ready, 1)
                act.drain()
                act.wait_ge(lam_ready, lay + 1)
                for g in range(6):
                    last = af(la[:, g // 3, g % 3, :], lr[:, g // 3, g % 3, :], ACT.Exp, scale=stat[:, 28 + g:29 + g])
                last.then_inc(a_ready, 1)
                for g in range(6):
                    last = af(lr[:, g // 3, g % 3, :], lr[:, g // 3, g % 3, :], ACT.Tanh, scale=stat[:, 22 + g:23 + g])
                last.then_inc(t_ready, 1)

                NH = H_MLA + H_SWA
                for h in range(NH):
                    act.wait_ge(negm, NH * lay + h + 1)
                    if h >= 2:
                        act.wait_ge(pt_ps, NH * lay + h - 1)
                    for n in range(NT):
                        src = bank[h % 2] if h < H_MLA else sw
                        last = af(pr[:, h % 2, n * SEQ:(n + 1) * SEQ], src[:, n * SEQ:(n + 1) * SEQ], ACT.Exp,
                                  bias=stat[:, 84 + 2 * h + n:85 + 2 * h + n],
                                  scale=QK ** -0.5 if h < H_MLA else 1.0,
                                  accum_out=stat[:, 104 + 2 * h + n:105 + 2 * h + n])
                        if h >= H_MLA:
                            g = V_SINK + h - H_MLA
                            last = af(stat[:, 124 + 2 * h + n:125 + 2 * h + n], vec[:, g:g + 1], ACT.Exp,
                                      bias=stat[:, 84 + 2 * h + n:85 + 2 * h + n])
                    last.then_inc(p_ready, 1)
                    if h == 6:
                        act.wait_ge(bq_ready, lay + 1)
                        af(lr[:], lr[:], ACT.Sqrt, scale=2.0).then_inc(b_root, 1)

                act.wait_ge(o_done, NH * (lay + 1))
                for w, (c0, c1) in enumerate(((0, MLA_W), (MLA_W, MLA_W + SWA_W))):
                    for n in range(NT):
                        af(xs[:, 0, 0:c1 - c0], o[:, n, c0:c1], ACT.Square,
                           accum_out=stat[:, 164 + 2 * w + n:165 + 2 * w + n])
                        act.drain()
                af(stat[:, 168:170], stat[:, 164:166], ACT.Sqrt, bias=eps, scale=1.0 / MLA_W)
                af(stat[:, 170:172], stat[:, 166:168], ACT.Sqrt, bias=eps, scale=1.0 / SWA_W).then_inc(o_rms, 1)
                act.wait_ge(osum_ps, lay + 1)
                af(lt[:, 1, 0, :], bank[4][:, 0:SEQ], ACT.Sqrt, bias=eps, scale=1.0 / LRU_W).then_inc(orms, 1)
                act.wait_ge(oT_ps, lay + 1)
                for j in range(3):
                    af(mixT[:, j, :], mix_bank(j), ACT.Copy,
                       scale=vec[:, V_GRP + j:V_GRP + j + 1]).then_inc(mix_a, 1)

                rms(2 * lay + 1)
                copy_xT(2 * lay + 1, V_NFFN)

                def split_hi(s, q, ld):
                    act.wait_ge(ld_raw[s], ld)
                    if type(q) is not int or q > 1:
                        act.wait_ge(blk_done, q - 1)
                    af(hl[s % 2][:, 0], raw[:, s], ACT.Copy).then_inc(hi_done, 1)

                def hi_at(s, Q, m=None):
                    if m is None:
                        split_hi(s, Q + s, 4 * Q + 16)
                    else:
                        split_hi(s, m * 4 + (Q + s), m * 16 + (4 * Q + 16))

                def activate(s, q, i):
                    act.wait_ge(blk_done, q + 1)
                    af(act_g[:, bass.ds(i * SEQ, SEQ)], bank[4 + s % 2][:, 0:SEQ], ACT.Gelu).then_inc(gelu_done, 1)

                def copy_gates(s, g, t0, stored):
                    for b in range(2):
                        act.wait_ge(gate_ps, g * 2 + (b + 1))
                        if b == 0 and (type(stored) is not int or stored):
                            act.wait_ge(gates_out[s % 2], stored)
                        src = bank[6 + b][:].rearrange("p (t i) -> p t i", t=GB)
                        af(gates[:, bass.ds(t0 * HK + b * GB * HK, GB * HK)].rearrange("p (t i) -> p t i", t=GB),
                           src[:, :, 0:HK], ACT.Copy)
                        af(gate_out[:, s % 2, b * GB * HK:(b + 1) * GB * HK].rearrange("p (t i) -> p t i", t=GB),
                           src[:, :, HK:], ACT.Copy).then_inc(gate_ready, 1)

                def store_gates(s, g, n):
                    act.wait_ge(gate_ready, g * 2 + 2)
                    nc.scalar.dma_start(gates_dram[bass.ds(n, 1)].rearrange("a p e -> p (a e)"),
                                        gate_out[:, s % 2]).then_inc(gates_out[s % 2], 16)

                def split_p(s, pair, i, v_after):
                    act.wait_ge(pf_done, v_after)
                    act.wait_ge(blk_done, pair)
                    af(p_hl[:, s, 0], act_g[:, bass.ds(i * SEQ, 2 * SEQ)], ACT.Copy).then_inc(p_hi, 1)

                Q = q0(lay, 0)
                hi_at(0, Q)
                hi_at(1, Q)
                for i in range(2 * PH):
                    act.wait_ge(ph_q, 16 * lay + i + 1)
                    if i >= 2:
                        act.wait_ge(ph_s, 16 * lay + i - 1)
                    af(qT[:, i % 2, :], bank[i % 2][:, 0:SEQ], ACT.Copy).then_inc(ph_qT, 1)
                for half in range(2):
                    Q, H = q0(lay, half), lay * NG
                    for s in range(4):
                        if half or s > 1:
                            hi_at(s, Q)
                        if s > 1:
                            activate(s, Q + s - 2, s - 2)
                    if half == 0:
                        act.wait_ge(ge_in, lay + 1)
                        af(sc[:], sc[:], ACT.Exp).then_inc(ge_out, 1)
                    with act.Fori(1, TURNS if half else U_LOW) as m:
                        for s in range(4):
                            hi_at(s, Q, m)
                            activate(s, m * 4 + (Q + s - 2), m * 4 + (s - 2))
                    if half == 0:
                        act.wait_ge(egT_ps, lay + 1)
                        af(egT[:, 0:2, :].rearrange("p w t -> p (w t)"), bank[6][:], ACT.Copy)
                        af(egT[:, 2, :], bank[7][:, 0:SEQ], ACT.Copy).then_inc(egT_ready, 1)
                        for s in range(4):
                            hi_at(s, Q + 4 * U_LOW)
                            if s > 2:
                                store_gates(s - 3, H + s - 3, s - 3)
                            activate(s, Q + 4 * U_LOW + s - 2, 4 * U_LOW + s - 2)
                            if s > 1:
                                copy_gates(s, H + s - 2, (s - 2) * GT, 8 * H)
                        with act.Fori(1, NG // 4) as m:
                            for s in range(4):
                                hi_at(s, Q + 4 * U_LOW, m)
                                store_gates(s - 3, m * 4 + (H + s - 3), m * 4 + (s - 3))
                                activate(s, m * 4 + (Q + 4 * U_LOW + s - 2), m * 4 + (4 * U_LOW + s - 2))
                                copy_gates(s, m * 4 + (H + s - 2), m * (4 * GT) + (s - 2) * GT,
                                           m * 32 + (8 * H + 16 * (s // 2 - 1)))
                    V, R, F = Q + HK, halves(lay, half) * HK // 2, halves(lay, half) * TURNS
                    hi_at(0, V)
                    activate(0, Q + HK - 2, HK - 2)
                    if half == 0:
                        store_gates(1, H + NG - 3, NG - 3)
                        copy_gates(0, H + NG - 2, (NG - 2) * GT, 8 * (H + NG - 2))
                    activate(1, Q + HK - 1, HK - 1)
                    if half == 0:
                        store_gates(0, H + NG - 2, NG - 2)
                        copy_gates(1, H + NG - 1, (NG - 1) * GT, 8 * (H + NG - 2))
                        store_gates(1, H + NG - 1, NG - 1)
                    split_p(0, V, 0, F + 1)
                    for s in range(1, 4):
                        hi_at(s, V)
                        if s % 2:
                            split_p((s + 1) // 2 % 2, V + s - 1, s + 1, F + 1 + (s + 1) // 4)
                    with act.Fori(1, TURNS - 1) as m:
                        for s in range(4):
                            hi_at(s, V, m)
                            if s % 2:
                                split_p((s + 1) // 2 % 2, m * 4 + (V + s - 1), m * 4 + (s + 1),
                                        m + (F + 1 + (s + 1) // 4))
                    for s in range(4):
                        hi_at(s, V + HK - 4)
                        if s == 1:
                            split_p(1, V + HK - 4, HK - 2, F + TURNS)
            rms(2 * DEPTH)

        @block.vector
        def _(dve):
            v = nc.vector
            cp, tt, ts, stt = v.tensor_copy, v.tensor_tensor, v.tensor_scalar, v.scalar_tensor_tensor

            def scale_x(o_):
                dve.wait_ge(rms_ready, o_ + 1)
                v.reciprocal(stat[:, 2:4], stat[:, 2:4])
                dve.drain()
                for n in range(NT):
                    ts(xs[:, n, :], x[:, n, :], stat[:, 2 + n:3 + n], None, ALU.mult).then_inc(xs_ready, 1)

            def copy_xT(o_, gain):
                for b in (1, 3):
                    dve.wait_ge(xT_ps, 4 * o_ + b + 1)
                    for c in (2 * b, 2 * b + 1):
                        ts(xT[:, c, :], bank[4 + b][:, (c % 2) * SEQ:(c % 2 + 1) * SEQ],
                           vec[:, gain + c:gain + c + 1], None, ALU.mult).then_inc(xT_ready, 1)

            def rotate(out1, out2, src, trig_n, heads, half):
                c0 = 0 if half == HD // 2 else HD // 2
                shape = [P, heads, 2, half]
                a = ropeA[:, 0:heads * 2 * half].rearrange("p (h w d) -> p h w d", h=heads, w=2)
                b = ropeB[:, 0:heads * 2 * half].rearrange("p (h w d) -> p h w d", h=heads, w=2)
                cs, sn = (t[:, trig_n, c0:c0 + half].unsqueeze(1).unsqueeze(1).broadcast_to(shape)
                          for t in (cos, sin))
                tt(a, src, cs, ALU.mult)
                tt(b, src, sn, ALU.mult)
                dve.drain()
                tt(out1, a[:, :, 0], b[:, :, 1], ALU.subtract)
                r = tt(out2, a[:, :, 1], b[:, :, 0], ALU.add)
                dve.drain()
                return r

            dve.wait_ge(s_pos, 16)
            dve.wait_ge(s_const, 16)
            cp(posf[:], posi[:])
            dve.drain()
            for n in range(NT):
                ts(ang[:, 0, n], const[:, C_INV:C_INV + NF], posf[:, n:n + 1], None, ALU.mult)
            dve.drain()
            for w, quarter in ((1, 0.0), (2, 0.25)):
                ts(ang[:, 3], ang[:, 0], 1.0 / (2 * np.pi), quarter, ALU.mult, ALU.add)
                dve.drain()
                ts(ang[:, 3], ang[:, 3], ROUND, ROUND, ALU.add, ALU.subtract)
                dve.drain()
                src = ang[:, 0]
                for part in (TWO_PI_1, TWO_PI_2, TWO_PI_3):
                    stt(ang[:, w], ang[:, 3], -part, src, ALU.mult, ALU.add)
                    src = ang[:, w]
                    dve.drain()
                ts(ang[:, w], ang[:, w], quarter * 2 * np.pi, PI_IN, ALU.add, ALU.min)
                dve.drain()
                ts(ang[:, w], ang[:, w], -PI_IN, None, ALU.max)
            dve.drain()
            cp(ang[:, 4], ang[:, 3]).then_inc(ang_ready, 1)
            dve.wait_ge(s_x, 16)
            v.memset(stat[:, 12:13], 0.0).then_inc(x_ready, 4)
            for lay in range(DEPTH):
                scale_x(2 * lay)
                dve.wait_ge(lam_u, lay + 1)
                u, z, z2, q, s8, n8 = (stat[:, 16 + 6 * k:22 + 6 * k] for k in (0, 3, 4, 5, 1, 2))
                ts(z, u, 2.0, None, ALU.add)
                dve.drain()
                v.reciprocal(z, z)
                dve.drain()
                tt(z, z, u, ALU.mult)
                dve.drain()
                tt(z2, z, z, ALU.mult)
                dve.drain()
                ts(q, z2, 1.0 / 19, None, ALU.mult)
                for k in range(8, 0, -1):
                    dve.drain()
                    stt(q, q, 1.0 / (2 * k + 1), z2, ALU.add, ALU.mult)
                ts(s8, vec[:, V_LAM:V_LAM + 6], -LRU_C, 0.0, ALU.mult, ALU.max)
                dve.drain()
                stt(q, q, 1.0, z, ALU.add, ALU.mult)
                dve.drain()
                stt(s8, q, 2 * LRU_C, s8, ALU.mult, ALU.add)
                dve.drain()
                ts(n8, s8, -1.0, None, ALU.mult).then_inc(lam_ready, 1)
                copy_xT(2 * lay, V_NMIX)

                HALF = IN_A // 2
                for half in range(2):
                    dve.wait_ge(proj_ps, 4 * lay + 2 + half + 1)
                    cp(proj[:, 1, half * HALF:(half + 1) * HALF], bank[2 + half][:, 0:HALF]).then_inc(proj_d, 1)
                dve.wait_ge(lru_ps, 6 * (lay + 1))
                v.memset(lxp[:, :, 0:1], 0.0)
                v.memset(lxp[:, :, SEQ + 1:], 0.0)
                for c in range(LC):
                    cp(lxp[:, c, 1:SEQ + 1], lru_bank(c)).then_inc(lx_ready, 1)
                dve.wait_ge(c_rms, lay + 1)
                v.reciprocal(stat[:, 8:12], stat[:, 8:12])
                dve.drain()
                for w, (c0, c1) in enumerate(((0, Q_RANK), (Q_RANK, KR0))):
                    for n in range(NT):
                        last = ts(proj[:, n, c0:c1], proj[:, n, c0:c1], stat[:, 8 + 2 * w + n:9 + 2 * w + n],
                                  None, ALU.mult)
                last.then_inc(cn_ready, 1)
                dve.wait_ge(proj_a, 2 * (lay + 1))
                dve.wait_ge(trig, 2)
                for n in range(NT):
                    src = proj[:, n, SQ0:SV0].rearrange("p (h w d) -> p h w d", h=6, w=2)
                    rotate(src[:, :, 0], src[:, :, 1], src, n, 6, HD // 2).then_inc(s_rope, 1)
                for n in range(NT):
                    src = proj[:, n, KR0:KR0 + ROPE].rearrange("p (h w d) -> p h w d", h=1, w=2)
                    rotate(src[:, :, 0], src[:, :, 1], src, n, 1, ROPE // 2)
                    cp(kb[:, n, :, NOPE:], proj[:, n, KR0:KR0 + ROPE].unsqueeze(1)
                       .broadcast_to([P, H_MLA, ROPE])).then_inc(k_rope, 1)
                for n in range(NT):
                    for half in range(2):
                        dve.wait_ge(q_nope, 4 * lay + 2 * n + half + 1)
                        src = (bank[2 * n + half][:, 0:3 * QK].rearrange("p (h d) -> p h d", h=3)[:, :, NOPE:]
                               .rearrange("p h (w d) -> p h w d", w=2))
                        dst = qb[:, n, 3 * half:3 * half + 3, NOPE:]
                        rotate(dst[:, :, 0:ROPE // 2], dst[:, :, ROPE // 2:], src, n, 3,
                               ROPE // 2).then_inc(q_rope, 1)
                for k in range(HALO + 1):
                    for c in range(LC):
                        w_ = vec[:, V_CW + LC * k + c:V_CW + LC * k + c + 1]
                        src = lxp[:, c, k:k + SEQ]
                        if k == 0:
                            last = ts(xc[:, c], src, w_, vec[:, V_CB + c:V_CB + c + 1], ALU.mult, ALU.add)
                        else:
                            last = stt(xc[:, c], src, w_, xc[:, c], ALU.mult, ALU.add)
                    if k < HALO:
                        dve.drain()
                last.then_inc(xc_ready, 1)
                for j in range(3):
                    dve.wait_ge(sT_ps, 3 * lay + j + 1)
                    cp(sT[0:HD, 2 * j:2 * j + 2].rearrange("p a t -> p (a t)"), bank[4 + j][0:HD, :]).then_inc(sT_ready, 1)

                NH = H_MLA + H_SWA

                def row_max(h):
                    dve.wait_ge(sc_ps, NH * lay + h + 1)
                    nm = stat[:, 84 + 2 * h:86 + 2 * h]
                    mx = stat[:, 64 + 2 * h:66 + 2 * h]
                    if h < H_MLA:
                        v.reduce_max(mx, bank[h % 2][:].rearrange("p (n k) -> p n k", n=NT), AX.X)
                        dve.drain()
                        ts(nm, mx, -QK ** -0.5, None, ALU.mult).then_inc(negm, 1)
                    else:
                        if h > H_MLA:
                            dve.wait_ge(p_ready, NH * lay + h)
                        stt(sw[:], bank[h % 2][:], HD ** -0.5, const[:, C_MASK:C_MASK + NT * SEQ], ALU.mult, ALU.add)
                        dve.drain()
                        v.reduce_max(mx, sw[:].rearrange("p (n k) -> p n k", n=NT), AX.X)
                        dve.drain()
                        g = V_SINK + h - H_MLA
                        ts(nm, mx, vec[:, g:g + 1], -1.0, ALU.max, ALU.mult).then_inc(negm, 1)

                def copy_pT(h):
                    dve.wait_ge(pt_ps, NH * lay + h + 1)
                    if h >= 2:
                        dve.wait_ge(o_ps, NH * lay + h - 1)
                    cp(prT[:, h % 2, :], bank[2 + h % 2][:]).then_inc(pt_ready, 1)

                def norm_o(h):
                    dve.wait_ge(o_ps, NH * lay + h + 1)
                    s_ = stat[:, 104 + 2 * h:106 + 2 * h]
                    if h >= H_MLA:
                        tt(s_, s_, stat[:, 124 + 2 * h:126 + 2 * h], ALU.add)
                        dve.drain()
                    v.reciprocal(s_, s_)
                    dve.drain()
                    for n in range(NT):
                        last = ts(o[:, n, h * HD:(h + 1) * HD], bank[6 + h % 2][:, n * HD:(n + 1) * HD],
                                  stat[:, 104 + 2 * h + n:105 + 2 * h + n], None, ALU.mult)
                    last.then_inc(o_done, 1)

                def flat(t):
                    return t[:].rearrange("p d c t -> p (d c t)")

                def lru_gain():
                    dve.wait_ge(t_ready, lay + 1)
                    ts(flat(lt), flat(lr), 1.0, None, ALU.add)
                    dve.drain()
                    v.reciprocal(flat(lt), flat(lt))
                    dve.drain()
                    tt(flat(lr), flat(lr), flat(lt), ALU.mult).then_inc(bq_ready, 1)
                    tt(li[:].rearrange("p d c t -> p d (c t)"), li[:].rearrange("p d c t -> p d (c t)"),
                       xc[:].rearrange("p c t -> p (c t)").unsqueeze(1).broadcast_to([P, 2, LC * SEQ]), ALU.mult)

                def lru_scan():
                    dve.wait_ge(b_root, lay + 1)
                    dve.wait_ge(a_ready, lay + 1)
                    tt(flat(li), flat(li), flat(lr), ALU.mult)
                    dve.drain()
                    for c in range(LC):
                        v.tensor_tensor_scan(lr[:, 0, c, :], la[:, 0, c, :], li[:, 0, c, :], 0.0, ALU.mult, ALU.add)
                        v.tensor_tensor_scan(lr[:, 1, c, ::-1], la[:, 1, c, ::-1], li[:, 1, c, ::-1], 0.0,
                                             ALU.mult, ALU.add)

                def lru_out():
                    f = [lr[:, d].rearrange("p c t -> p (c t)") for d in range(2)]
                    tt(f[0], f[0], f[1], ALU.add)
                    dve.drain()
                    tt(f[0], f[0], lg[:].rearrange("p c t -> p (c t)"), ALU.mult)
                    dve.drain()
                    tt(lt[:, 0].rearrange("p c t -> p (c t)"), f[0], f[0], ALU.mult).then_inc(osq_ready, 1)

                row_max(0)
                for h in range(NH):
                    if h + 1 < NH:
                        row_max(h + 1)
                    copy_pT(h)
                    if h:
                        norm_o(h - 1)
                    if h == 3:
                        lru_gain()
                    if h == 7:
                        lru_scan()
                norm_o(NH - 1)
                lru_out()
                dve.wait_ge(lg_ready, 3 * (lay + 1))

                dve.wait_ge(o_rms, lay + 1)
                v.reciprocal(stat[:, 168:172], stat[:, 168:172])
                dve.drain()
                for w, (c0, c1) in enumerate(((0, MLA_W), (MLA_W, MLA_W + SWA_W))):
                    for n in range(NT):
                        last = ts(o[:, n, c0:c1], o[:, n, c0:c1], stat[:, 168 + 2 * w + n:169 + 2 * w + n], None,
                                  ALU.mult)
                    last.then_inc(on_ready, 1)
                dve.wait_ge(orms, lay + 1)
                v.reciprocal(lt[:, 1, 0, :], lt[:, 1, 0, :])
                dve.drain()
                for c in range(LC):
                    stt(mixT[:, 3 + c, :], lr[:, 0, c, :], vec[:, V_GRP + 3 + c:V_GRP + 4 + c], lt[:, 1, 0, :],
                        ALU.mult, ALU.mult).then_inc(mix_d, 1)
                dve.wait_ge(oT_ps, lay + 1)
                for j in (3, 4):
                    ts(mixT[:, 3 + j, :], mix_bank(j),
                       vec[:, V_GRP + 3 + j:V_GRP + 4 + j], None, ALU.mult).then_inc(mix_d, 1)
                for n in range(NT):
                    for half in range(2):
                        dve.wait_ge(out_ps, 4 * lay + 2 * n + half + 1)
                        w = x[:, n, half * 512:(half + 1) * 512]
                        r = tt(w, w, bank[4 + 2 * n + half][:], ALU.add)
                        r.then_inc(x_mid, 1)
                dve.drain()
                v.memset(stat[:, 12:13], 0.0).then_inc(x_ready, 4)
                scale_x(2 * lay + 1)
                copy_xT(2 * lay + 1, V_NFFN)

                def split_lo(s, q):
                    dve.wait_ge(hi_done, q + 1)
                    tt(hl[s % 2][:, 1], raw[:, s], hl[s % 2][:, 0], ALU.subtract).then_inc(lo_done, 1)

                def top16(val, idx, src, work):
                    v.max(val[:, 0:8], src)
                    dve.drain()
                    v.max_index(idx[:, 0:8], val[:, 0:8], src)
                    v.match_replace(work, val[:, 0:8], src, MAX_NEG)
                    dve.drain()
                    v.max(val[:, 8:16], work)
                    dve.drain()
                    return v.max_index(idx[:, 8:16], val[:, 8:16], work)

                def top_keys(i):
                    h, half = (i // 2 + PH // 2) % PH, i % 2
                    dve.wait_ge(ph_s, 16 * lay + i + 1)
                    for n in range(NT):
                        last = top16(top_v[:, n, h, half], top_i[:, n, h, half],
                                     bank[2 + i % 2][:, n * NK:(n + 1) * NK], tmp[:, n * NK:(n + 1) * NK])
                    last.then_inc(top1, 1)

                def top_pairs(i):
                    h = (i + PH // 2) % PH
                    dve.wait_ge(cand_ready, PH * lay + i + 1)
                    for n in range(NT):
                        c_ = cand[:, i % 2, n]
                        last = top16(sc[:, n, h], ci[:, n, h], c_, c_)
                    last.then_inc(top2, 1)

                parts = [t[:].rearrange("p c t -> p (c t)") for t in (x_hi, xT, x_lo)]
                dve.wait_ge(xT_ready, 8 * (2 * lay + 2))
                cp(parts[0], parts[1]).then_inc(xhi_ready, 1)
                Q = q0(lay, 0)
                for i in range(PH):
                    top_keys(2 * i)
                    if i == 1:
                        split_lo(0, Q)
                        split_lo(1, Q + 1)
                    if i == PH - 1:
                        dve.wait_ge(ph_q, 16 * (lay + 1))
                        tt(parts[2], parts[1], parts[0], ALU.subtract).then_inc(xlo_ready, 1)
                    top_keys(2 * i + 1)
                    if i:
                        top_pairs(i - 1)
                split_lo(2, Q + 2)
                top_pairs(PH - 1)
                split_lo(3, Q + 3)
                dve.drain()
                s3 = sc[:].rearrange("p n h s -> p (n h) s")
                big = stat[:, 208:224]
                cp(big, s3[:, :, 0])
                dve.drain()
                tt(s3, s3, big.unsqueeze(2).broadcast_to([P, NT * PH, TOP]), ALU.subtract).then_inc(ge_in, 1)
                cif = ci[:].rearrange("p n h s -> p (n h s)")
                caf = ca[:].rearrange("p w n h s -> p w (n h s)")
                dve.wait_ge(s_spill, 16 * (lay + 1))
                SKIP = PA * (TOP - PB)
                cff = cf[:].rearrange("p w n h s -> p w (n h s)")
                b16, b4 = (eg[:, w].rearrange("p n h s -> p (n h s)") for w in range(2))
                ts(caf[:, 0], cif, 4, None, ALU.logical_shift_right)
                ts(caf[:, 1], cif, 2, None, ALU.logical_shift_right)
                cp(tmp[:], cif)
                dve.drain()
                cp(cff, caf)
                dve.drain()
                stt(cff[:, 0], cff[:, 1], -float(SKIP // PB), cff[:, 0], ALU.add, ALU.max)
                dve.drain()
                ts(b16, cff[:, 0], -float(TOP), None, ALU.mult)
                ts(b4, cff[:, 0], -float(PB), -float(SKIP), ALU.mult, ALU.add)
                dve.drain()
                tt(b16, b16, b4, ALU.max)
                dve.drain()
                tt(cff[:, 1], b16, tmp[:], ALU.add)
                cp(top_f[:].rearrange("p n h w s -> p (n h w s)"), top_i[:].rearrange("p n h w s -> p (n h w s)"))
                dve.drain()
                shape = [P, NT, TOP, TOP]
                i16 = const[:, C_IOTA:C_IOTA + TOP].unsqueeze(1).unsqueeze(1).broadcast_to(shape)

                def decode(h, part):
                    dve.drain()
                    for w in range(2):
                        if part == 0:
                            c_ = cf[:, w, :, bass.ds(h, 1), :].rearrange("p n a s -> p n (a s)")
                            tt(hot[:, w], c_.unsqueeze(3).broadcast_to(shape), i16, ALU.is_equal)
                        elif part == 1:
                            f_ = top_f[:, :, bass.ds(h, 1), w, :].rearrange("p n a s -> p n (a s)")
                            tt(hot[:, w], hot[:, w], f_.unsqueeze(2).broadcast_to(shape), ALU.mult)
                        else:
                            v.reduce_sum(eg[:, w, :, bass.ds(h, 1), :].rearrange("p n a s -> p n (a s)"),
                                         hot[:, w], AX.X)

                def one_hots(s, g, t0, wait_ps=True):
                    if wait_ps:
                        dve.wait_ge(gate_ps, g * 2 - 2)
                    k1, k2 = (egT[:, w, bass.ds(t0, GT)].unsqueeze(2) for w in range(2))
                    sh = [P, GT, NK]
                    tt(one_i[:, s % 2], iota.unsqueeze(1).broadcast_to(sh), k1.broadcast_to(sh),
                       ALU.is_equal).then_inc(one_eq, 1)
                    tt(one_j[:, s % 2], iota.unsqueeze(1).broadcast_to(sh), k2.broadcast_to(sh),
                       ALU.is_equal).then_inc(one_j_ready, 1)

                def weigh(m):
                    a_ = act_g[:, bass.ds(m * (4 * SEQ), 4 * SEQ)].rearrange("p (i t) -> p i t", i=4)
                    tt(a_, a_, gates[:].rearrange("p (t i) -> p i t", i=HK)[:, bass.ds(m * 4, 4), :],
                       ALU.mult).then_inc(pf_done, 1)

                def split_p(s, pair, i):
                    dve.wait_ge(p_hi, pair + 1)
                    tt(p_hl[:, s, 1], act_g[:, bass.ds(i * SEQ, 2 * SEQ)], p_hl[:, s, 0],
                       ALU.subtract).then_inc(p_lo, 1)

                for part in range(3):
                    decode(0, part)
                for half in range(2):
                    Q, H = q0(lay, half), lay * NG
                    if half:
                        for s in range(4):
                            split_lo(s, Q + s)
                    with dve.Fori(1, TURNS if half else U_LOW) as m:
                        for s in range(4):
                            split_lo(s, m * 4 + (Q + s))
                            if half == 0 and s < 3:
                                decode(m, s)
                    if half == 0:
                        dve.drain()
                        dve.wait_ge(ge_out, lay + 1)
                        gs = stat[:, 176:192]
                        v.reduce_sum(gs, s3, AX.X)
                        dve.drain()
                        v.reciprocal(gs, gs)
                        dve.drain()
                        tt(eg[:, 2].rearrange("p n h s -> p (n h) s"), s3,
                           gs.unsqueeze(2).broadcast_to([P, NT * PH, TOP]), ALU.mult).then_inc(eg_ready, 1)
                        split_lo(0, Q + 4 * U_LOW)
                        dve.wait_ge(egT_ready, lay + 1)
                        for s in range(4):
                            if s:
                                split_lo(s, Q + 4 * U_LOW + s)
                            one_hots(s, H + s, s * GT, H + s > 1)
                        with dve.Fori(1, NG // 4) as m:
                            for s in range(4):
                                split_lo(s, m * 4 + (Q + 4 * U_LOW + s))
                                one_hots(s, m * 4 + (H + s), m * (4 * GT) + s * GT)
                    V, R, F = Q + HK, halves(lay, half) * HK // 2, halves(lay, half) * TURNS
                    split_lo(0, V)
                    if half:
                        dve.wait_ge(gates_back, 16 * (NG // 2) * (lay + 1))
                    else:
                        dve.wait_ge(gate_ready, 2 * (H + NG))
                    dve.wait_ge(gelu_done, (halves(lay, half) + 1) * HK)
                    weigh(0)
                    split_p(0, R, 0)
                    for s in range(1, 4):
                        split_lo(s, V + s)
                        if s == 2:
                            weigh(1)
                        if s % 2:
                            split_p((s + 1) // 2 % 2, R + (s + 1) // 2, s + 1)
                    for first, last_turn in ((1, TURNS // 2), (TURNS // 2, TURNS - 1)):
                        with dve.Fori(first, last_turn) as m:
                            for s in range(4):
                                split_lo(s, m * 4 + (V + s))
                                if s % 2 == 0 and first == 1:
                                    weigh(m * 2 + s // 2)
                                if s % 2:
                                    split_p((s + 1) // 2 % 2, m * 2 + (R + (s + 1) // 2), m * 4 + (s + 1))
                    for s in range(4):
                        split_lo(s, V + HK - 4 + s)
                        if s == 1:
                            split_p(1, R + HK // 2 - 1, HK - 2)
                dve.wait_ge(blk_done, q0(lay + 1, 0))
                dve.wait_ge(s_back, 16 * (lay + 1))
                for n in range(NT):
                    for half in range(2):
                        w = slice(half * 512, (half + 1) * 512)
                        tt(x[:, n, w], x_back[:, n, w], bank[2 * n + half][:], ALU.add)
                dve.drain()
                v.memset(stat[:, 12:13], 0.0).then_inc(x_ready, 4)
            scale_x(2 * DEPTH)
            dve.wait_ge(s_nf, 16)
            dve.drain()
            for n in range(NT):
                tt(xs[:, n, :], xs[:, n, :], norm_fb[:], ALU.mult).then_inc(final, 1)

        @block.gpsimd
        def _(pool):
            for lay in range(DEPTH):
                if lay:
                    pool.wait_ge(p_lo, halves(lay, 0) * HK // 2)
                nc.gpsimd.memset(wlru[:], 0.0).then_inc(zeroed, 1)
                nc.gpsimd.memset(ones[:], 1.0).then_inc(ones_ready, 1)
                for i in range(PH):
                    h = (i + PH // 2) % PH
                    pool.wait_ge(top1, 16 * lay + 2 * i + 2)
                    if i >= 2:
                        pool.wait_ge(top2, PH * lay + i - 1)
                    for a0, a1, nb, c0 in ((0, PA, TOP, 0), (PA, TOP, PB, PA * TOP)):
                        sh = [P, NT, a1 - a0, nb]
                        last = nc.gpsimd.tensor_tensor(
                            cand[:, i % 2, :, c0:c0 + (a1 - a0) * nb].rearrange("p n (a b) -> p n a b", b=nb),
                            top_v[:, :, h, 0, a0:a1].unsqueeze(3).broadcast_to(sh),
                            top_v[:, :, h, 1, 0:nb].unsqueeze(2).broadcast_to(sh), ALU.add)
                    last.then_inc(cand_ready, 1)

                def times_gate(s, g, t0):
                    pool.wait_ge(one_eq, g + 1)
                    nc.gpsimd.tensor_tensor(
                        one_i[:, s % 2], one_i[:, s % 2],
                        egT[:, 2, bass.ds(t0, GT)].unsqueeze(2).broadcast_to([P, GT, NK]),
                        ALU.mult).then_inc(one_i_ready, 1)

                pool.wait_ge(egT_ready, lay + 1)
                with pool.Fori(0, NG // 2) as m:
                    for s in range(2):
                        times_gate(s, m * 2 + (lay * NG + s), m * (2 * GT) + s * GT)


def kernel(**inputs):
    import concourse.bacc as _bacc
    from concourse.bass_utils import run_bass_kernel_spmd as _run

    a = {k: np.asarray(v) for k, v in inputs.items()}
    L = DEPTH

    def chunks(w, parts):
        return w.reshape(L, parts, P, -1).transpose(0, 2, 1, 3)

    def columns(v_):
        return v_.reshape(L, -1, P).transpose(0, 2, 1)

    const = np.zeros((P, C_W), np.float32)
    const[:, C_ID:C_ID + P] = np.eye(P)
    const[:, C_IOTA:C_IOTA + NK] = np.arange(NK)
    const[:, C_INV:C_INV + HD // 2] = 10000.0 ** (-np.arange(0, HD, 2, dtype=np.float32) / HD)
    const[:, C_INV + HD // 2:C_INV + NF] = 10000.0 ** (-np.arange(0, ROPE, 2, dtype=np.float32) / ROPE)
    query = np.arange(SEQ).reshape(NT, P, 1)
    far = np.abs(query - np.arange(SEQ)) > WINDOW
    const[:, C_MASK:C_MASK + NT * SEQ] = np.where(far, NEG_BIG, 0.0).transpose(1, 0, 2).reshape(P, -1)
    const[:, C_EPS] = EPS

    vec = np.concatenate(
        [columns(a["norm_mix"]), columns(a["norm_ffn"]), columns(a["q_norm"]), columns(a["kv_norm"]),
         columns(a["grp_norm"]), columns(a["conv_w"].reshape(L, -1)), columns(a["conv_b"]),
         columns(a["lru_ba"].reshape(L, -1)), columns(a["lru_bx"].reshape(L, -1)),
         columns(a["lru_lambda"].reshape(L, -1)), np.broadcast_to(a["swa_sink"][:, None, :], (L, P, H_SWA))], axis=2)
    win = chunks(a["w_in"], DC)
    win = np.concatenate([win[..., :IN_A].reshape(L, P, -1), win[..., IN_A:].reshape(L, P, -1)], axis=2)
    gates = np.stack([a["lru_wa"], a["lru_wx"]], axis=2).reshape(L, 2, 2, LC, 2, 64, 64)
    gates = gates.transpose(0, 4, 5, 1, 2, 3, 6).reshape(L, P, 12, 64)
    wq = a["peer_wq"].reshape(L, DC, P, 2 * PH, P).transpose(0, 2, 3, 1, 4)
    sub = a["peer_subkeys"].transpose(0, 3, 1, 2)
    pu = a["peer_u"].reshape(L, NK, NK, DC, P).transpose(0, 1, 4, 3, 2).reshape(L, NK, P, D)
    arrays = {
        "x": a["x"].reshape(NT, P, D).transpose(1, 0, 2), "pos": a["positions"].reshape(NT, P).T,
        "const": const, "vec": vec, "w_in": win,
        "w_uq": chunks(a["w_uq"], 2), "w_ukv": a["w_ukv"], "w_lru": gates, "w_out": chunks(a["w_out"], DC),
        "w_q": wq, "sub_k": sub, "peer_u": pu, "peer_v": a["peer_v"].reshape(L, NK, P, D),
        "norm_f": a["norm_final"]}
    arrays = {k + "_dram": np.ascontiguousarray(v_) for k, v_ in arrays.items()}

    nc = _bacc.Bacc("TRN2", target_bir_lowering=False, num_devices=1)
    args = [nc.dram_tensor(k, v_.shape, mybir.dt.from_np(v_.dtype), kind="ExternalInput").ap()
            for k, v_ in arrays.items()]
    spill = nc.dram_tensor("x_spill_dram", (P, NT, D), F32, kind="Internal").ap()
    out = nc.dram_tensor("out_dram", (P, NT, D), F32, kind="ExternalOutput").ap()
    gates_dram = nc.dram_tensor("gates_dram", (SEQ // GT, P, GT * HK), F32, kind="Internal").ap()
    encoder(nc, *args, spill, gates_dram, out)
    r = _run(nc, [arrays], core_ids=[0])
    got = r.results[0]["out_dram"]
    return got.transpose(1, 0, 2).reshape(1, SEQ, D)
```

```python
from contextlib import ExitStack

import numpy as np

import concourse.bass as bass
from concourse import mybir

EPS = 1e-6
NEG_BIG = -1e30
P = 128
D = 1024
DC = D // P
SEQ = 256
NT = SEQ // P
DEPTH = 2
H_MLA, NOPE, ROPE, V_MLA = 6, 64, 32, 64
QK = NOPE + ROPE
Q_RANK, KV_RANK = 256, 128
MLA_W = H_MLA * V_MLA
LRU_W = 384
LC = LRU_W // P
LRU_C = 8.0
HALO = 3
H_SWA, KV_SWA, HD = 4, 2, 64
SWA_W = H_SWA * HD
WINDOW = 128
IN_A = Q_RANK + KV_RANK + ROPE + SWA_W + 2 * KV_SWA * HD
IN_W = IN_A + 2 * LRU_W
SQ0 = Q_RANK + KV_RANK + ROPE
SV0 = SQ0 + SWA_W + KV_SWA * HD
KR0 = Q_RANK + KV_RANK
PH = 8
NK = 128
TOP = 16
SLOTS = PH * TOP
PA, PB = 3, 4
PAIRS = PA * TOP + (TOP - PA) * PB
GT = 8
HK = NK // 2
RAWS = 4
F32 = mybir.dt.float32
F32R = mybir.dt.float32r
U32 = mybir.dt.uint32
I32 = mybir.dt.int32
ALU = mybir.AluOpType
ACT = mybir.ActivationFunctionType
AX = mybir.AxisListType
MAX_NEG = -3.0e38
ROUND = 1.5 * 2.0 ** 23
TWO_PI_1, TWO_PI_2 = 6.28125, 0.00193500518798828125
TWO_PI_3 = 2 * np.pi - TWO_PI_1 - TWO_PI_2
PI_IN = 3.1415925

C_ID, C_IOTA, C_INV, C_MASK = 0, 128, 256, 304
C_EPS = C_MASK + NT * SEQ
C_W = C_EPS + 1
NF = HD // 2 + ROPE // 2
V_NMIX, V_NFFN, V_QN, V_KVN, V_GRP = 0, 8, 16, 18, 19
V_CW, V_CB, V_BA, V_BX, V_LAM, V_SINK = 27, 39, 42, 48, 54, 60
V_W = 64


def encoder(nc, x_in, pos_in, const_in, vec_in, w_in, w_uq, w_ukv, w_lru, w_out, w_q, sub_k,
            peer_u, peer_v, norm_f, x_spill, gates_dram, out):
    ctx = ExitStack()
    with ctx:
        def sem(name):
            return ctx.enter_context(nc.semaphore(name))

        base_byte = -(-nc.sbuf_base // 32) * 32
        ctx.enter_context(nc.sbuf_tensor("arena", [P, 53200], F32))

        def at(name, word, shape, dt=F32):
            return nc.alloc_sbuf_tensor_at(name, shape, dt, offset=base_byte + 4 * word)

        const = at("const", 0, [P, C_W])
        cos = at("cos", 824, [P, NT, NF])
        sin = at("sin", 920, [P, NT, NF])
        vec = at("vec", 1016, [P, V_W])
        skT = at("skT", 1080, [P, 2, NK])
        stat = at("stat", 1336, [P, 256])
        x = at("x", 1600, [P, NT, D])
        xT = at("xT", 3648, [P, DC, SEQ])
        mixT = at("mixT", 5696, [P, DC, SEQ])
        ARENA_A = 7744
        ARENA_B = ARENA_A + 32768
        win_a = at("win_a", ARENA_A, [P, DC, IN_A])
        win_b = at("win_b", ARENA_A + DC * IN_A, [P, DC, 2 * LRU_W])
        win_a_lo = at("win_a_lo", ARENA_A, [P, DC, IN_A], F32R)
        win_b_lo = at("win_b_lo", ARENA_A + DC * IN_A, [P, DC, 2 * LRU_W], F32R)
        win_b_hi = at("win_b_hi", ARENA_B + 2048, [P, DC, 2 * LRU_W], F32R)
        win_a_hi = [at(f"win_a_hi{r}", ARENA_B + w, [P, IN_A], F32R) for r, w in enumerate((10240, 11168, 8192, 9216))]
        xT_lo = at("xT_lo", 3648, [P, DC, SEQ], F32R)
        wq = at("wq", ARENA_A, [P, 2 * PH, DC, P])
        wout = at("wout", ARENA_A + 16384, [P, DC, D])
        wout_lo = at("wout_lo", ARENA_A + 16384, [P, DC, D], F32R)
        wout_hi = [at(f"wout_hi{r}", w, [P, D], F32R)
                   for r, w in enumerate((ARENA_A + 28928, 3648, 4672, ARENA_A + 24576, ARENA_A + 25600,
                                          ARENA_A + 26624, ARENA_B + 2624, ARENA_B + 3648))]
        mix_lo = at("mix_lo", 5696, [P, DC, SEQ], F32R)
        mix_hi = at("mix_hi", ARENA_A + 30080, [P, DC, SEQ], F32R)
        wq_lo = at("wq_lo", ARENA_A, [P, 2 * PH, DC, P], F32R)
        OUT_ORDER = (0, 1, 2, 6, 7, 3, 4, 5)
        wq_hi = [at(f"wq_hi{r}", ARENA_A + 16384 + D * w, [P, DC, P], F32R)
                 for r, w in enumerate(OUT_ORDER + (8, 9, 10))]
        WQ_RING = len(wq_hi)
        wuq = at("wuq", ARENA_A + 24576, [P, 2, H_MLA * QK])
        wukv = at("wukv", ARENA_A + 25728, [P, H_MLA * (NOPE + V_MLA)])
        wlru = at("wlru", ARENA_A + 26496, [P, 12, P])
        xs = at("xs", ARENA_A + 28032, [P, NT, D])
        ropeA = at("ropeA", ARENA_A + 28032, [P, 384])
        ropeB = at("ropeB", ARENA_A + 28032 + 384, [P, 384])
        ones = at("ones", ARENA_A + 32384, [P, P])
        qb = at("qb", ARENA_A + 30080, [P, NT, H_MLA, QK])
        kb = at("kb", ARENA_A + 31232, [P, NT, H_MLA, QK])
        hot = at("hot", ARENA_A, [P, 2, NT, TOP, TOP])
        gates = at("gates", ARENA_A, [P, SEQ * HK])
        act_g = at("act_g", ARENA_A + HK * SEQ, [P, HK * SEQ])
        lxp = at("lxp", ARENA_A, [P, LC, SEQ + HALO])
        xc = at("xc", ARENA_A + 784, [P, LC, SEQ])
        lr = at("lr", ARENA_A + 1552, [P, 2, LC, SEQ])
        li = at("li", ARENA_A + 3088, [P, 2, LC, SEQ])
        la = at("la", ARENA_A + 4624, [P, 2, LC, SEQ])
        lt = at("lt", ARENA_A + 6160, [P, 2, LC, SEQ])
        proj = at("proj", ARENA_B, [P, NT, IN_A])
        cT = at("cT", ARENA_B + 9280, [P, 3, SEQ])
        qkT = at("qkT", ARENA_B + 2624, [P, H_MLA, 2 * SEQ])
        vb = at("vb", ARENA_B + 5696, [P, NT, H_MLA, V_MLA])
        sT = at("sT", ARENA_B + 6464, [P, 6, SEQ])
        o = at("o", ARENA_B + 8000, [P, NT, MLA_W + SWA_W])
        pr = at("pr", ARENA_B + 9280, [P, 2, NT * SEQ])
        prT = at("prT", ARENA_B + 10304, [P, 2, 2 * SEQ])
        lg = at("lg", ARENA_B + 11328, [P, LC, SEQ])
        sw = at("sw", ARENA_B + 12096, [P, NT * SEQ])
        raw = at("raw", ARENA_B, [P, RAWS, D])
        x_back = at("x_back", ARENA_A + DC * IN_W, [P, NT, D])
        assert DC * IN_W + NT * D <= HK * SEQ
        hl = [at(f"hl{s}", ARENA_B + 4096 + 2048 * s, [P, 2, D], F32R) for s in range(2)]
        ROUTE = ARENA_B + 8192
        qT = at("qT", ROUTE, [P, 2, SEQ])
        tmp = at("tmp", ROUTE + 512, [P, SEQ])
        top_v = at("top_v", ROUTE + 768, [P, NT, PH, 2, TOP])
        top_i = at("top_i", ROUTE + 1280, [P, NT, PH, 2, TOP], U32)
        top_f = at("top_f", ROUTE + 1792, [P, NT, PH, 2, TOP])
        sc = at("sc", ROUTE + 2304, [P, NT, PH, TOP])
        cand = at("cand", ROUTE + 2560, [P, 2, NT, PAIRS])
        ci = at("ci", ROUTE + 3584, [P, NT, PH, TOP], U32)
        egT = at("egT", ROUTE + 3728, [P, 3, SEQ])
        one_j = at("one_j", ROUTE, [P, 2, GT, NK])
        gate_out = at("gate_out", ROUTE + 2048, [P, 2, GT * HK])
        p_hl = at("p_hl", ROUTE, [P, 2, 2, 2 * SEQ], F32R)
        ca = at("ca", 3648, [P, 2, NT, PH, TOP], U32)
        cf = at("cf", 4160, [P, 2, NT, PH, TOP])
        eg = at("eg", 4672, [P, 3, NT, PH, TOP])
        one_i = at("one_i", 3648, [P, 2, GT, NK])
        x_lo = at("x_lo", 1600, [P, DC, SEQ], F32R)
        assert WQ_RING * D <= 28032 - 16384
        x_hi = at("x_hi", 5696, [P, DC, SEQ], F32R)
        bank = [ctx.enter_context(nc.psum_tensor(f"bank{b}", [P, 512], F32)) for b in range(8)]

        ident = const[:, C_ID:C_ID + P]
        iota = const[:, C_IOTA:C_IOTA + NK]
        eps = const[:, C_EPS:C_EPS + 1]
        ang = at("ang", ARENA_B + 12096, [P, 5, NT, NF])
        posi = at("posi", ARENA_B + 12576, [P, NT], I32)
        posf = at("posf", ARENA_B + 12584, [P, NT])
        norm_fb = at("norm_fb", ARENA_A, [P, D])

        s_const, s_pos, s_x0, s_x1, s_vec, s_win_a, s_win_b, s_wuq, s_wukv, s_lru, s_wout, s_wq1, s_wq0, s_sk = (
            sem("ld_" + n) for n in ("const", "pos", "x0", "x1", "vec", "win_a", "win_b", "wuq", "wukv", "lru",
                                     "wout", "wq1", "wq0", "sk"))
        ld_win_a = [sem(f"ld_win_a{c}") for c in range(DC)]
        wa_hi, wa_lo, wa_used, wb_hi, wb_lo, xT_lo_ready = (
            sem(n) for n in ("wa_hi", "wa_lo", "wa_used", "wb_hi", "wb_lo", "xT_lo_ready"))
        final = sem("final")
        gates_out, gates_back = [sem(f"gates_out{s}") for s in range(2)], sem("gates_back")
        s_nf, s_spill, s_back, s_out = sem("ld_nf"), sem("spilled"), sem("x_back"), [sem(f"stored{n}") for n in range(NT)]
        y_done = sem("y_done")
        ld_raw = [sem(f"ld_raw{s}") for s in range(RAWS)]
        zeroed, ones_ready = sem("zeroed"), sem("ones_ready")
        ang_ready, trig = sem("ang_ready"), sem("trig")
        x_ready, rms_ready, xs_ready, xT_ps, xT_ready = (
            sem(n) for n in ("x_ready", "rms_ready", "xs_ready", "xT_ps", "xT_ready"))
        proj_ps, proj_a, proj_d, lru_ps, lx_ready, lg_ready = (
            sem(n) for n in ("proj_ps", "proj_a", "proj_d", "lru_ps", "lx_ready", "lg_ready"))
        c_rms, cn_ready, cT_ps, cT_ready, q_ps, kv_ps, q_nope, q_rope, kv_a, k_rope, s_rope = (
            sem(n) for n in ("c_rms", "cn_ready", "cT_ps", "cT_ready", "q_ps", "kv_ps", "q_nope", "q_rope",
                             "kv_a", "k_rope", "s_rope"))
        qk_ps, qk_ready, sT_ps, sT_ready = (sem(n) for n in ("qk_ps", "qk_ready", "sT_ps", "sT_ready"))
        lam_u, lam_ready, xc_ready, gates_ps, gates_ready, a_ready, b_root, b_ready = (
            sem(n) for n in ("lam_u", "lam_ready", "xc_ready", "gates_ps", "gates_ready", "a_ready",
                             "b_root", "b_ready"))
        wo_hi, wo_lo, mixlo_ready = (sem(n) for n in ("wo_hi", "wo_lo", "mixlo_ready"))
        wout_used, wq_hi_ready, wq_lo_ready = (sem(n) for n in ("wout_used", "wq_hi_ready", "wq_lo_ready"))
        osq_ready, osum_ps, orms = sem("osq_ready"), sem("osum_ps"), sem("orms")
        sc_ps, negm, p_ready, pt_ps, pt_ready, o_ps, o_done = (
            sem(n) for n in ("sc_ps", "negm", "p_ready", "pt_ps", "pt_ready", "o_ps", "o_done"))
        o_rms, on_ready, oT_ps, mix_a, mix_d, out_ps = (
            sem(n) for n in ("o_rms", "on_ready", "oT_ps", "mix_a", "mix_d", "out_ps"))
        ph_q, ph_qT, ph_s, top1, cand_ready, top2, ge_in, ge_out, eg_ready, egT_ps, egT_ready = (
            sem(n) for n in ("ph_q", "ph_qT", "ph_s", "top1", "cand_ready", "top2", "ge_in", "ge_out",
                             "eg_ready", "egT_ps", "egT_ready"))
        xhi_ready, xlo_ready, one_eq, one_j_ready, one_i_ready, gate_ps, gate_ready = (
            sem(n) for n in ("xhi_ready", "xlo_ready", "one_eq", "one_j_ready", "one_i_ready", "gate_ps", "gate_ready"))
        hi_done, lo_done, blk_done, gelu_done, pf_done, p_hi, p_lo = (
            sem(n) for n in ("hi_done", "lo_done", "blk_done", "gelu_done", "pf_done", "p_hi", "p_lo"))

        def q0(lay, half):
            return (2 * lay + half) * 2 * HK

        def halves(lay, half):
            return 2 * lay + half

        NG = SEQ // GT
        GB = GT // 2
        U_LOW = (HK - NG) // 4
        TURNS = HK // 4
        EARLY = 16

        def lru_bank(j):
            c = j % LC
            return bank[4 + 2 * (j // LC) + c // 2][:, (c % 2) * SEQ:(c % 2 + 1) * SEQ]

        def mix_bank(j):
            b, w = (4 + j // 2, j % 2) if j < 3 else (6, j - 3)
            return bank[b][:, w * SEQ:(w + 1) * SEQ]

        score_bank = [bank[b][:, 0:NT * NK] for b in (2, 3, 6, 7)]

        osum = bank[5][:, SEQ:]

        block = ctx.enter_context(nc.Block())

        @block.sync
        def _(sp):
            sp.dma_start(x[:, 0], x_in[:, 0]).then_inc(s_x0, 16)
            sp.dma_start(const[:], const_in).then_inc(s_const, 16)
            sp.dma_start(x[:, 1], x_in[:, 1]).then_inc(s_x1, 16)
            sp.dma_start(posi[:], pos_in).then_inc(s_pos, 16)
            for lay in range(DEPTH):
                if lay == 0:
                    sp.dma_start(vec[:], vec_in[lay]).then_inc(s_vec, 16)
                    for c in range(DC):
                        sp.dma_start(win_a[:, c], w_in[lay, :, c * IN_A:(c + 1) * IN_A]).then_inc(ld_win_a[c], 16)
                    sp.dma_start(win_b[:], w_in[lay, :, DC * IN_A:]).then_inc(s_win_b, 16)
                else:
                    sp.wait_ge(p_lo, halves(lay, 0) * HK // 2)
                sp.dma_start(wuq[:], w_uq[lay]).then_inc(s_wuq, 16)
                sp.dma_start(wukv[:], w_ukv[lay]).then_inc(s_wukv, 16)
                sp.wait_ge(zeroed, lay + 1)
                sp.dma_start(wlru[0:64, :, 0:64], w_lru[lay, 0:64]).then_inc(s_lru, 16)
                sp.dma_start(wlru[64:P, :, 64:P], w_lru[lay, 64:P]).then_inc(s_lru, 16)
                sp.dma_start(wout[:], w_out[lay]).then_inc(s_wout, 16)
                sp.dma_start(skT[:], sub_k[lay]).then_inc(s_sk, 16)
                sp.wait_ge(lru_ps, 6 * (lay + 1))
                sp.wait_ge(proj_ps, 4 * (lay + 1))
                sp.dma_start(wq[:, PH:], w_q[lay, :, PH:]).then_inc(s_wq1, 16)
                sp.wait_ge(mix_d, 5 * (lay + 1))
                sp.dma_start(wq[:, 0:PH], w_q[lay, :, 0:PH]).then_inc(s_wq0, 16)
                sp.wait_ge(x_ready, 4 * lay + 2)
                sp.dma_start(x_spill, x[:]).then_inc(s_spill, 16)

                for s in range(RAWS):
                    sp.dma_start(raw[:, s], peer_u[lay, s]).then_inc(ld_raw[s], 16)
                for half in range(2):
                    for table, run in ((peer_u, 0), (peer_v, HK)):
                        first = 1 if half == 0 and run == 0 else 0

                        def turn(m):
                            for s in range(RAWS):
                                sp.wait_ge(lo_done, m * 4 + (q0(lay, half) + run + s - 3))
                                sp.dma_start(raw[:, s], table[lay, bass.ds(m * 4 + (half * HK + s), 1)]
                                             .rearrange("a p e -> p (a e)")).then_inc(ld_raw[s], 16)

                        def gates_in(m, g):
                            sp.dma_start(gates[:, bass.ds(m * (2 * GT * HK) + g * GT * HK, 2 * GT * HK)]
                                         .rearrange("p (g e) -> p g e", g=2),
                                         gates_dram[bass.ds(m * 2 + g, 2)].rearrange("g p e -> p g e")
                                         ).then_inc(gates_back, 16)

                        MID = TURNS // 2 + 1
                        if half == 0 and run:
                            with sp.Fori(0, MID) as m:
                                turn(m)
                            sp.wait_ge(pf_done, (halves(lay, 0) + 1) * TURNS)
                            for s in range(2):
                                sp.wait_ge(gates_out[s], 16 * (NG // 2) * (lay + 1))
                            with sp.Fori(MID, TURNS) as m:
                                turn(m)
                                gates_in(m, -2 * MID)
                        elif half and not run:
                            late = NG // 2 - (TURNS - MID)
                            with sp.Fori(0, late) as m:
                                turn(m)
                                gates_in(m, NG - 2 * late)
                            with sp.Fori(late, TURNS) as m:
                                turn(m)
                        elif half:
                            with sp.Fori(0, MID) as m:
                                turn(m)
                            sp.wait_ge(pf_done, (halves(lay, 1) + 1) * TURNS)
                            sp.wait_ge(s_spill, 16 * (lay + 1))
                            sp.dma_start(x_back[:], x_spill).then_inc(s_back, 16)
                            if lay + 1 == DEPTH:
                                with sp.Fori(MID, TURNS) as m:
                                    turn(m)
                                continue
                            sp.dma_start(vec[:], vec_in[lay + 1]).then_inc(s_vec, 16)
                            with sp.Fori(MID, TURNS) as m:
                                turn(m)
                                c = m - MID
                                sp.dma_start(win_a[:, bass.ds(c, 1)].rearrange("p a n -> p (a n)"),
                                             w_in[lay + 1, :, bass.ds(c * IN_A, IN_A)]).then_inc(s_win_a, 16)
                            for c in range(TURNS - MID, DC):
                                sp.dma_start(win_a[:, c], w_in[lay + 1, :, c * IN_A:(c + 1) * IN_A]).then_inc(s_win_a, 16)
                            sp.dma_start(win_b[:], w_in[lay + 1, :, DC * IN_A:]).then_inc(s_win_b, 16)
                        else:
                            with sp.Fori(first, TURNS) as m:
                                turn(m)
            sp.wait_ge(pf_done, 2 * DEPTH * TURNS)
            sp.dma_start(norm_fb[:], norm_f.partition_broadcast(P)).then_inc(s_nf, 16)
            for n in range(NT):
                sp.wait_ge(final, n + 1)
                sp.dma_start(out[:, n], xs[:, n]).then_inc(s_out[n], 16)
            for n in range(NT):
                sp.wait_ge(s_out[n], 16)

        @block.tensor
        def _(pe):
            mm = nc.tensor.matmul
            tr = nc.tensor.transpose

            def transpose_x(o_):
                for n in range(NT):
                    pe.wait_ge(xs_ready, 2 * o_ + n + 1)
                    for c in range(DC):
                        b, w = bank[4 + c // 2], (c % 2) * SEQ
                        last = tr(b[:, w + n * P:w + (n + 1) * P], xs[:, n, c * P:(c + 1) * P], ident)
                        if c % 2 and n:
                            last.then_inc(xT_ps, 1)

            pe.wait_ge(s_const, 16)
            for lay in range(DEPTH):
                transpose_x(2 * lay)

                pe.wait_ge(xhi_ready, DC * (2 * lay + 1))
                HALF = IN_A // 2
                for c in range(DC):
                    for p_, (wait, x_, w_) in enumerate(((wa_hi, x_hi, win_a_hi[c % 4]), (wa_lo, x_hi, win_a_lo[:, c]),
                                                         (None, xT_lo, win_a_hi[c % 4]))):
                        if wait is not None:
                            pe.wait_ge(wait, DC * lay + c + 1)
                        elif c % 2 == 0:
                            pe.wait_ge(xT_lo_ready, DC // 2 * lay + c // 2 + 1)
                        for n in range(NT):
                            for half in range(2):
                                last = mm(bank[2 * n + half][:, 0:HALF], x_[:, c, n * P:(n + 1) * P],
                                          w_[:, half * HALF:(half + 1) * HALF], start=c == 0 and p_ == 0,
                                          stop=c == DC - 1 and p_ == 2)
                                if p_ == 2 and c == DC - 1:
                                    last.then_inc(proj_ps, 1)
                    if c < DC - 1:
                        last.then_inc(wa_used, 1)
                pe.wait_ge(xT_ready, DC * (2 * lay + 1))
                pe.wait_ge(wb_hi, DC * (lay + 1))
                pe.wait_ge(wb_lo, DC * (lay + 1))
                for j in range(2 * LC):
                    for p_, (w_, x_) in enumerate(((win_b_hi, x_hi), (win_b_lo, x_hi), (win_b_hi, xT_lo))):
                        for c in range(DC):
                            last = mm(lru_bank(j), w_[:, c, j * P:(j + 1) * P], x_[:, c, :],
                                      start=c == 0 and p_ == 0, stop=c == DC - 1 and p_ == 2)
                    last.then_inc(lru_ps, 1)
                    if j == 3:
                        pe.wait_ge(cn_ready, lay + 1)
                        for k in range(3):
                            for n in range(NT):
                                last = tr(bank[k // 2][:, (k % 2) * SEQ + n * P:(k % 2) * SEQ + (n + 1) * P],
                                          proj[:, n, k * P:(k + 1) * P], ident)
                        last.then_inc(cT_ps, 1)

                pe.wait_ge(cT_ready, 3 * (lay + 1))
                pe.wait_ge(s_wuq, 16 * (lay + 1))
                W3 = 3 * QK
                for n in range(NT):
                    for half in range(2):
                        for c in range(2):
                            last = mm(bank[2 * n + half][:, 0:W3], cT[:, c, n * P:(n + 1) * P],
                                      wuq[:, c, half * W3:(half + 1) * W3], start=c == 0, stop=c == 1)
                        last.then_inc(q_ps, 1)
                pe.wait_ge(lx_ready, 3 * (lay + 1))
                pe.wait_ge(lg_ready, 3 * (lay + 1))
                pe.wait_ge(s_wukv, 16 * (lay + 1))
                W3 = 3 * (NOPE + V_MLA)
                for n in range(NT):
                    for half in range(2):
                        mm(bank[4 + 2 * n + half][:, 0:W3], cT[:, 2, n * P:(n + 1) * P],
                           wukv[:, half * W3:(half + 1) * W3], start=True, stop=True).then_inc(kv_ps, 1)

                pe.wait_ge(xc_ready, lay + 1)
                pe.wait_ge(s_lru, 32 * (lay + 1))
                for g in range(12):
                    if g % 2 == 0 and g < 8:
                        pe.wait_ge(kv_a, 4 * lay + g // 2 + 1)
                    elif g % 2 == 0:
                        pe.wait_ge(gates_ready, 12 * lay + g - 6)
                    mm(bank[4 + (g // 2) % 4][:, (g % 2) * SEQ:(g % 2 + 1) * SEQ], wlru[:, g, :],
                       xc[:, g % LC, :], start=True, stop=True).then_inc(gates_ps, 1)

                pe.wait_ge(q_nope, 4 * (lay + 1))
                pe.wait_ge(q_rope, 4 * (lay + 1))
                pe.wait_ge(kv_a, 4 * (lay + 1))
                pe.wait_ge(k_rope, 2 * (lay + 1))
                for h in range(H_MLA):
                    if h >= 4:
                        pe.wait_ge(qk_ready, H_MLA * lay + h - 3)
                    for w, src in enumerate((qb, kb)):
                        for n in range(NT):
                            last = tr(bank[h % 4][0:QK, w * SEQ + n * P:w * SEQ + (n + 1) * P],
                                      src[:, n, h, :], ident)
                    last.then_inc(qk_ps, 1)

                def windowed_T(k):
                    if k == 0:
                        pe.wait_ge(s_rope, 2 * (lay + 1))
                        pe.wait_ge(gates_ready, 12 * (lay + 1))
                    if k == 2:
                        pe.wait_ge(sT_ready, 3 * lay + 1)
                    for j in (2 * k, 2 * k + 1):
                        for n in range(NT):
                            last = tr(bank[4 + k % 2][0:HD, (j % 2) * SEQ + n * P:(j % 2) * SEQ + (n + 1) * P],
                                      proj[:, n, SQ0 + j * HD:SQ0 + (j + 1) * HD], ident)
                    last.then_inc(sT_ps, 1)

                NH = H_MLA + H_SWA

                def scores(h):
                    if h == H_MLA:
                        pe.wait_ge(sT_ready, 3 * (lay + 1))
                    if h >= 2:
                        pe.wait_ge(p_ready, NH * lay + h - 1)
                    for n in range(NT):
                        if h < H_MLA:
                            q_, k_ = qkT[0:QK, h, n * P:(n + 1) * P], qkT[0:QK, h, SEQ:]
                        else:
                            g = h - H_MLA
                            q_, k_ = sT[0:HD, g, n * P:(n + 1) * P], sT[0:HD, H_SWA + g // 2, :]
                        last = mm(bank[h % 2][:, n * SEQ:(n + 1) * SEQ], q_, k_, start=True, stop=True)
                    last.then_inc(sc_ps, 1)

                def transpose_p(h):
                    pe.wait_ge(p_ready, NH * lay + h + 1)
                    if h >= 2:
                        pe.wait_ge(pt_ready, NH * lay + h - 1)
                    for kt in range(NT):
                        for n in range(NT):
                            last = tr(bank[2 + h % 2][:, (kt * NT + n) * P:(kt * NT + n + 1) * P],
                                      pr[:, h % 2, n * SEQ + kt * P:n * SEQ + (kt + 1) * P], ident)
                    last.then_inc(pt_ps, 1)

                def weigh_v(h):
                    pe.wait_ge(pt_ready, NH * lay + h + 1)
                    if h >= 2:
                        pe.wait_ge(o_done, NH * lay + h - 1)
                    for n in range(NT):
                        for kt in range(NT):
                            if h < H_MLA:
                                v_ = vb[:, kt, h, :]
                            else:
                                g = (h - H_MLA) // 2
                                v_ = proj[:, kt, SV0 + g * HD:SV0 + (g + 1) * HD]
                            last = mm(bank[6 + h % 2][:, n * HD:(n + 1) * HD],
                                      prT[:, h % 2, (kt * NT + n) * P:(kt * NT + n + 1) * P], v_,
                                      start=kt == 0, stop=kt == NT - 1)
                    last.then_inc(o_ps, 1)

                pe.wait_ge(qk_ready, H_MLA * lay + 5)
                scores(0)
                pe.wait_ge(qk_ready, H_MLA * (lay + 1))
                for h in range(NH):
                    if h + 1 < NH:
                        scores(h + 1)
                    if h == 0:
                        windowed_T(0)
                        windowed_T(1)
                    transpose_p(h)
                    if h:
                        weigh_v(h - 1)
                    if h == 1:
                        windowed_T(2)

                def mixed_T(blocks):
                    for j in blocks:
                        for n in range(NT):
                            last = tr(mix_bank(j)[:, n * P:(n + 1) * P],
                                      o[:, n, j * P:(j + 1) * P], ident)
                    last.then_inc(oT_ps, 1)

                pe.wait_ge(on_ready, 2 * lay + 1)
                mixed_T((0, 1, 2))
                weigh_v(NH - 1)

                def out_pass(n, half, k, p_):
                    c = OUT_ORDER[k]
                    x_ = mix_lo if p_ == 2 else mix_hi
                    w_ = wout_lo[:, c] if p_ == 1 else wout_hi[k]
                    return mm(bank[2 * n + half][:], x_[:, c, n * P:(n + 1) * P],
                              w_[:, half * 512:(half + 1) * 512], start=k == 0 and p_ == 0, stop=k == DC - 1 and p_ == 2)

                def out_wait(k, p_):
                    if p_ == 0:
                        pe.wait_ge(wo_hi, DC * lay + k + 1)
                        if k < 3:
                            pe.wait_ge(mix_a, 3 * lay + k + 1)
                        else:
                            pe.wait_ge(mix_d, 5 * lay + k - 2)
                    elif p_ == 1:
                        pe.wait_ge(wo_lo, DC * lay + k + 1)
                    else:
                        pe.wait_ge(mixlo_ready, DC * lay + k + 1)

                for k in range(5):
                    for p_ in range(3):
                        out_wait(k, p_)
                        for n in range(NT):
                            for half in range(2):
                                last = out_pass(n, half, k, p_)
                    last.then_inc(wout_used, 1)
                    if k == 2:
                        pe.wait_ge(mix_a, 3 * (lay + 1))
                        pe.wait_ge(ones_ready, lay + 1)
                        pe.wait_ge(osq_ready, lay + 1)
                        for c in range(LC):
                            last = mm(osum, ones[:], lt[:, 0, c, :], start=c == 0, stop=c == LC - 1)
                        last.then_inc(osum_ps, 1)
                    if k == 1:
                        pe.wait_ge(on_ready, 2 * (lay + 1))
                        mixed_T((3, 4))
                for k in range(5, DC):
                    for p_ in range(3):
                        out_wait(k, p_)
                for n in range(NT):
                    for half in range(2):
                        for k in range(5, DC):
                            for p_ in range(3):
                                last = out_pass(n, half, k, p_)
                        last.then_inc(out_ps, 1)

                transpose_x(2 * lay + 1)

                pe.wait_ge(xhi_ready, DC * (2 * lay + 2))
                pe.wait_ge(s_sk, 16 * (lay + 1))

                def key_scores(i):
                    pe.wait_ge(ph_qT, 16 * lay + i + 1)
                    if i >= 4:
                        pe.wait_ge(top1, 16 * lay + i - 3)
                    for n in range(NT):
                        last = mm(score_bank[i % 4][:, n * NK:(n + 1) * NK], qT[:, i % 2, n * P:(n + 1) * P],
                                  skT[:, i % 2, :], start=True, stop=True)
                    last.then_inc(ph_s, 1)

                def query(i, passes):
                    blk = (i + PH) % (2 * PH)
                    for p_ in passes:
                        if p_ == 0:
                            pe.wait_ge(wq_hi_ready, 2 * PH * lay + i + 1)
                            if i >= 2:
                                pe.wait_ge(ph_qT, 16 * lay + i - 1)
                        if p_ == 1:
                            pe.wait_ge(wq_lo_ready, 2 * PH * lay + i + 1)
                        w_ = wq_lo[:, blk] if p_ == 1 else wq_hi[i % WQ_RING]
                        x_ = x_lo if p_ == 2 else x_hi
                        for c in range(DC):
                            if p_ == 2 and i == 0 and c % 2 == 0:
                                pe.wait_ge(xlo_ready, DC // 2 * lay + c // 2 + 1)
                            last = mm(bank[i % 2][:, 0:SEQ], w_[:, c, :], x_[:, c, :],
                                      start=c == 0 and p_ == 0, stop=c == DC - 1 and p_ == 2)
                    if p_ == 2:
                        last.then_inc(ph_q, 1)

                query(0, (0, 1))
                query(1, (0, 1))
                query(0, (2,))
                query(1, (2,))
                pe.wait_ge(xT_ready, DC * (2 * lay + 2))
                key_scores(0)
                for i in range(2, 2 * PH):
                    query(i, (0, 1, 2))
                    key_scores(i - 1)
                key_scores(2 * PH - 1)

                def u_block(s, q, g, wait_gelu=True):
                    pe.wait_ge(hi_done, q + 1)
                    if wait_gelu:
                        pe.wait_ge(gelu_done, g - 1)
                    u_ = hl[s % 2][:].rearrange("p w (c e) -> p w c e", c=DC)
                    for c in range(DC):
                        for xh in (x_hi, x_lo):
                            mm(bank[4 + s % 2][:, 0:SEQ], u_[:, 0, c, :], xh[:, c, :],
                               start=c == 0 and xh is x_hi, stop=False)
                    pe.wait_ge(lo_done, q + 1)
                    for c in range(DC):
                        last = mm(bank[4 + s % 2][:, 0:SEQ], u_[:, 1, c, :], x_hi[:, c, :], start=False,
                                  stop=c == DC - 1)
                    last.then_inc(blk_done, 1)

                def gate_group(s, g, wait_gate=True):
                    pe.wait_ge(one_i_ready, g + 1)
                    pe.wait_ge(one_j_ready, g + 1)
                    for b in range(2):
                        if wait_gate:
                            pe.wait_ge(gate_ready, g * 2 + (b - 1))
                        for t in range(GB):
                            last = mm(bank[6 + b][:, t * NK:(t + 1) * NK], one_j[:, s % 2, b * GB + t, :],
                                      one_i[:, s % 2, b * GB + t, :], start=True, stop=True)
                        last.then_inc(gate_ps, 1)

                def v_block(s, q, pair, first=False, last_block=False):
                    pe.wait_ge(hi_done, q + 1)
                    if s % 2 == 0:
                        pe.wait_ge(p_hi, pair + 1)
                    for tiles in ((0,), (1,)) if last_block else ((0, 1),):
                        for ph, vh in ((0, 0), (1, 0), (0, 1)):
                            if vh:
                                pe.wait_ge(lo_done, q + 1)
                            elif ph and s % 2 == 0:
                                pe.wait_ge(p_lo, pair + 1)
                            for n in tiles:
                                for w in range(2):
                                    t0 = (s % 2) * SEQ + n * P
                                    last = mm(bank[2 * n + w][:], p_hl[:, s // 2, ph, t0:t0 + P],
                                              hl[s % 2][:, vh, w * 512:(w + 1) * 512], start=first and ph == vh,
                                              stop=last_block and vh == 1)
                        if last_block and tiles == (0,):
                            last.then_inc(y_done, 1)
                    last.then_inc(blk_done, 1)

                for half in range(2):
                    Q, G, H = q0(lay, half), halves(lay, half) * HK, lay * NG
                    for s in range(4):
                        u_block(s, Q + s, G + s, G + s > 1)
                    with pe.Fori(1, TURNS if half else U_LOW - 1) as m:
                        for s in range(4):
                            u_block(s, m * 4 + (Q + s), m * 4 + (G + s))
                    if half == 0:
                        for s in range(4):
                            if s == 3:
                                pe.wait_ge(eg_ready, lay + 1)
                                for w in range(3):
                                    for n in range(NT):
                                        c0 = (w % 2) * SEQ + n * P
                                        last = tr(bank[6 + w // 2][:, c0:c0 + P],
                                                  eg[:, w, n].rearrange("p h s -> p (h s)"), ident)
                                last.then_inc(egT_ps, 1)
                            u_block(s, Q + 4 * U_LOW - 4 + s, G + 4 * U_LOW - 4 + s)
                        for s in range(4):
                            u_block(s, Q + 4 * U_LOW + s, G + 4 * U_LOW + s)
                            gate_group(s, H + s, H + s > 0)
                        with pe.Fori(1, NG // 4) as m:
                            for s in range(4):
                                gate_group(s, m * 4 + (H + s))
                                u_block(s, m * 4 + (Q + 4 * U_LOW + s), m * 4 + (G + 4 * U_LOW + s))
                    V, R = Q + HK, halves(lay, half) * HK // 2
                    for s in range(4):
                        v_block(s, V + s, R + s // 2, first=half == 0 and s == 0)
                    with pe.Fori(1, TURNS - 1) as m:
                        for s in range(4):
                            v_block(s, m * 4 + (V + s), m * 2 + (R + s // 2))
                    for s in range(4):
                        v_block(s, V + HK - 4 + s, R + HK // 2 - 2 + s // 2, last_block=half == 1 and s == 3)

        @block.scalar
        def _(act):
            af = nc.scalar.activation

            def rms(o_):
                if o_ and o_ % 2 == 0:
                    af(stat[:, 13:14], eps, ACT.Sqrt)
                for n in range(NT):
                    if o_:
                        act.wait_ge(x_ready, 2 * (o_ - 1) + n + 1)
                    else:
                        act.wait_ge((s_x0, s_x1)[n], 16)
                    af(xs[:, n, :], x[:, n, :], ACT.Square, accum_out=stat[:, n:n + 1])
                    act.drain()
                    af(stat[:, 2 + n:3 + n], stat[:, n:n + 1], ACT.Sqrt, bias=eps,
                       scale=1.0 / D).then_inc(rms_ready, 1)

            def copy_xT(o_, gain):
                for dst, ready in ((x_hi, xhi_ready), (xT, xT_ready)):
                    for b in (0, 2):
                        act.wait_ge(xT_ps, 4 * o_ + b + 1)
                        for c in (2 * b, 2 * b + 1):
                            af(dst[:, c, :], bank[4 + b][:, (c % 2) * SEQ:(c % 2 + 1) * SEQ], ACT.Copy,
                               scale=vec[:, gain + c:gain + c + 1]).then_inc(ready, 1)

            act.wait_ge(s_const, 16)
            for lay in range(DEPTH):
                def split_wa(c):
                    if lay == 0:
                        act.wait_ge(ld_win_a[c], 16)
                    else:
                        act.wait_ge(s_win_a, 16 * DC * lay)
                    if c >= 2 and lay:
                        act.wait_ge(blk_done, q0(lay, 0))
                    if c >= 4:
                        act.wait_ge(wa_used, (DC - 1) * lay + c - 3)
                    af(win_a_hi[c % 4][:], win_a[:, c], ACT.Copy).then_inc(wa_hi, 1)

                if lay:
                    split_wa(0)
                    split_wa(1)
                rms(2 * lay)
                act.wait_ge(s_vec, 16 * (lay + 1))
                af(stat[:, 16:22], vec[:, V_LAM:V_LAM + 6], ACT.Abs)
                act.drain()
                af(stat[:, 16:22], stat[:, 16:22], ACT.Exp, scale=-1.0).then_inc(lam_u, 1)
                if lay == 0:
                    split_wa(0)
                copy_xT(2 * lay, V_NMIX)
                for c in range(2 if lay else 1, DC):
                    split_wa(c)
                for c in range(DC):
                    act.wait_ge(s_win_b, 16 * (lay + 1))
                    af(win_b_hi[:, c], win_b[:, c], ACT.Copy).then_inc(wb_hi, 1)
                if lay == 0:
                    act.wait_ge(ang_ready, 1)
                    af(sin[:], ang[:, 1], ACT.Sin).then_inc(trig, 1)
                    af(cos[:], ang[:, 2], ACT.Sin).then_inc(trig, 1)

                HALF = IN_A // 2
                for half in range(2):
                    act.wait_ge(proj_ps, 4 * lay + half + 1)
                    af(proj[:, 0, half * HALF:(half + 1) * HALF], bank[half][:, 0:HALF],
                       ACT.Copy).then_inc(proj_a, 1)
                act.wait_ge(proj_d, 2 * (lay + 1))
                act.drain()
                for w, (c0, c1) in enumerate(((0, Q_RANK), (Q_RANK, KR0))):
                    for n in range(NT):
                        af(xs[:, 0, 0:c1 - c0], proj[:, n, c0:c1], ACT.Square,
                           accum_out=stat[:, 4 + 2 * w + n:5 + 2 * w + n])
                        act.drain()
                af(stat[:, 8:10], stat[:, 4:6], ACT.Sqrt, bias=eps, scale=1.0 / Q_RANK)
                af(stat[:, 10:12], stat[:, 6:8], ACT.Sqrt, bias=eps, scale=1.0 / KV_RANK).then_inc(c_rms, 1)
                act.wait_ge(cT_ps, lay + 1)
                for j in range(3):
                    g = V_QN + j if j < 2 else V_KVN
                    af(cT[:, j, :], bank[j // 2][:, (j % 2) * SEQ:(j % 2 + 1) * SEQ], ACT.Copy,
                       scale=vec[:, g:g + 1]).then_inc(cT_ready, 1)
                def split_wo(k):
                    if k == 0:
                        act.wait_ge(s_wout, 16 * (lay + 1))
                    if k == 1:
                        act.wait_ge(lru_ps, 6 * (lay + 1))
                    if k == 3:
                        act.wait_ge(gates_ps, 12 * (lay + 1))
                    if k == 6:
                        act.wait_ge(sc_ps, (H_MLA + H_SWA) * lay + H_MLA)
                    af(wout_hi[k][:], wout[:, OUT_ORDER[k]], ACT.Copy).then_inc(wo_hi, 1)

                split_wo(0)
                for c in range(LC):
                    j = LC + c
                    act.wait_ge(lru_ps, 6 * (lay + 1))
                    af(lg[:, c, :], lru_bank(j), ACT.Gelu).then_inc(lg_ready, 1)
                split_wo(1)
                split_wo(2)
                for n in range(NT):
                    for half in range(2):
                        act.wait_ge(q_ps, 4 * lay + 2 * n + half + 1)
                        b = bank[2 * n + half][:, 0:3 * QK].rearrange("p (h d) -> p h d", h=3)
                        af(qb[:, n, 3 * half:3 * half + 3, 0:NOPE], b[:, :, 0:NOPE], ACT.Copy).then_inc(q_nope, 1)
                for n in range(NT):
                    for half in range(2):
                        act.wait_ge(kv_ps, 4 * lay + 2 * n + half + 1)
                        b = bank[4 + 2 * n + half][:, 0:3 * (NOPE + V_MLA)].rearrange("p (h d) -> p h d", h=3)
                        af(kb[:, n, 3 * half:3 * half + 3, 0:NOPE], b[:, :, 0:NOPE], ACT.Copy)
                        af(vb[:, n, 3 * half:3 * half + 3, :], b[:, :, NOPE:], ACT.Copy).then_inc(kv_a, 1)
                for g in range(12):
                    d, kind, c = g // 6, (g // 3) % 2, g % 3
                    act.wait_ge(gates_ps, 12 * lay + 2 * (g // 2) + 2)
                    v0 = (V_BX if kind else V_BA) + 3 * d + c
                    af((li if kind else lr)[:, d, c, :], bank[4 + (g // 2) % 4][:, (g % 2) * SEQ:(g % 2 + 1) * SEQ],
                       ACT.Sigmoid, bias=vec[:, v0:v0 + 1]).then_inc(gates_ready, 1)
                for h in range(H_MLA):
                    act.wait_ge(qk_ps, H_MLA * lay + h + 1)
                    af(qkT[0:QK, h, :], bank[h % 4][0:QK, :], ACT.Copy).then_inc(qk_ready, 1)
                act.wait_ge(lam_ready, lay + 1)

                def square_o(w, c0, c1):
                    for n in range(NT):
                        af(xs[:, 0, 0:c1 - c0], o[:, n, c0:c1], ACT.Square,
                           accum_out=stat[:, 164 + 2 * w + n:165 + 2 * w + n])
                        act.drain()

                def root_o(w, c0, c1):
                    af(stat[:, 168 + 2 * w:170 + 2 * w], stat[:, 164 + 2 * w:166 + 2 * w], ACT.Sqrt, bias=eps,
                       scale=1.0 / (c1 - c0)).then_inc(o_rms, 1)

                NH = H_MLA + H_SWA
                for h in range(NH):
                    act.wait_ge(negm, NH * lay + h + 1)
                    if h >= 2:
                        act.wait_ge(pt_ps, NH * lay + h - 1)
                    for n in range(NT):
                        src = bank[h % 2] if h < H_MLA else sw
                        last = af(pr[:, h % 2, n * SEQ:(n + 1) * SEQ], src[:, n * SEQ:(n + 1) * SEQ], ACT.Exp,
                                  bias=stat[:, 84 + 2 * h + n:85 + 2 * h + n],
                                  scale=QK ** -0.5 if h < H_MLA else 1.0,
                                  accum_out=stat[:, 104 + 2 * h + n:105 + 2 * h + n])
                    if h >= H_MLA:
                        last = af(stat[:, 124 + 2 * h:126 + 2 * h], stat[:, 124 + 2 * h:126 + 2 * h], ACT.Exp)
                    last.then_inc(p_ready, 1)
                    if h < 6:
                        af(la[:, h // 3, h % 3, :], lr[:, h // 3, h % 3, :], ACT.Exp,
                           scale=stat[:, 28 + h:29 + h]).then_inc(a_ready, 1)
                        af(lr[:, h // 3, h % 3, :], lr[:, h // 3, h % 3, :], ACT.Tanh, scale=stat[:, 22 + h:23 + h])
                    if h in (1, 3, 5, 6, 7):
                        split_wo({1: 3, 3: 4, 5: 5, 6: 6, 7: 7}[h])
                    if h == 8:
                        act.wait_ge(o_done, NH * lay + H_MLA)
                        square_o(0, 0, MLA_W)

                root_o(0, 0, MLA_W)
                act.drain()
                af(lr[:], lr[:], ACT.Sqrt).then_inc(b_root, 1)
                act.wait_ge(oT_ps, 2 * lay + 1)
                for j in range(3):
                    af(mix_hi[:, j, :], mix_bank(j), ACT.Copy, scale=vec[:, V_GRP + j:V_GRP + j + 1])
                    af(mixT[:, j, :], mix_bank(j), ACT.Copy,
                       scale=vec[:, V_GRP + j:V_GRP + j + 1]).then_inc(mix_a, 1)
                act.wait_ge(o_done, NH * (lay + 1))
                square_o(1, MLA_W, MLA_W + SWA_W)
                root_o(1, MLA_W, MLA_W + SWA_W)
                act.wait_ge(osum_ps, lay + 1)
                af(lt[:, 1, 0, :], osum, ACT.Sqrt, bias=eps, scale=1.0 / LRU_W).then_inc(orms, 1)

                def wq_split(i):
                    if i == 0:
                        act.wait_ge(s_wq1, 16 * (lay + 1))
                    if i == PH:
                        act.wait_ge(s_wq0, 16 * (lay + 1))
                    if i < 5:
                        act.wait_ge(wout_used, 5 * lay + i + 1)
                    elif i < WQ_RING:
                        act.wait_ge(out_ps, 4 * (lay + 1))
                    else:
                        act.wait_ge(ph_q, 2 * PH * lay + i - WQ_RING + 1)
                    af(wq_hi[i % WQ_RING][:], wq[:, (i + PH) % (2 * PH)], ACT.Copy).then_inc(wq_hi_ready, 1)

                for i in range(4):
                    wq_split(i)
                rms(2 * lay + 1)
                copy_xT(2 * lay + 1, V_NFFN)

                def split_hi(s, q, ld):
                    act.wait_ge(ld_raw[s], ld)
                    if type(q) is not int or q > 1:
                        act.wait_ge(blk_done, q - 1)
                    af(hl[s % 2][:, 0], raw[:, s], ACT.Copy).then_inc(hi_done, 1)

                def hi_at(s, Q, m=None):
                    if m is None:
                        split_hi(s, Q + s, 4 * Q + 16)
                    else:
                        split_hi(s, m * 4 + (Q + s), m * 16 + (4 * Q + 16))

                def activate(s, q, i):
                    act.wait_ge(blk_done, q + 1)
                    af(act_g[:, bass.ds(i * SEQ, SEQ)], bank[4 + s % 2][:, 0:SEQ], ACT.Gelu).then_inc(gelu_done, 1)

                def copy_gates(s, g, t0, stored):
                    for b in range(2):
                        act.wait_ge(gate_ps, g * 2 + (b + 1))
                        if b == 0 and (type(stored) is not int or stored):
                            act.wait_ge(gates_out[s % 2], stored)
                        src = bank[6 + b][:].rearrange("p (t i) -> p t i", t=GB)
                        af(gates[:, bass.ds(t0 * HK + b * GB * HK, GB * HK)].rearrange("p (t i) -> p t i", t=GB),
                           src[:, :, 0:HK], ACT.Copy)
                        af(gate_out[:, s % 2, b * GB * HK:(b + 1) * GB * HK].rearrange("p (t i) -> p t i", t=GB),
                           src[:, :, HK:], ACT.Copy).then_inc(gate_ready, 1)

                def store_gates(s, g, n):
                    act.wait_ge(gate_ready, g * 2 + 2)
                    nc.scalar.dma_start(gates_dram[bass.ds(n, 1)].rearrange("a p e -> p (a e)"),
                                        gate_out[:, s % 2]).then_inc(gates_out[s % 2], 16)

                def split_p(s, pair, i, v_after):
                    act.wait_ge(pf_done, v_after)
                    act.wait_ge(blk_done, pair)
                    af(p_hl[:, s, 0], act_g[:, bass.ds(i * SEQ, 2 * SEQ)], ACT.Copy).then_inc(p_hi, 1)

                Q = q0(lay, 0)
                for i in range(2 * PH):
                    if i == 4:
                        hi_at(0, Q)
                    if i == 6:
                        hi_at(1, Q)
                    if i + 4 < 2 * PH:
                        wq_split(i + 4)
                    act.wait_ge(ph_q, 16 * lay + i + 1)
                    if i >= 2:
                        act.wait_ge(ph_s, 16 * lay + i - 1)
                    af(qT[:, i % 2, :], bank[i % 2][:, 0:SEQ], ACT.Copy).then_inc(ph_qT, 1)
                for half in range(2):
                    Q, H = q0(lay, half), lay * NG
                    for s in range(4):
                        if half or s > 1:
                            hi_at(s, Q)
                        if s > 1:
                            activate(s, Q + s - 2, s - 2)
                    for first, end in ((1, U_LOW - 2), (U_LOW - 2, TURNS if half else U_LOW)):
                        with act.Fori(first, end) as m:
                            for s in range(4):
                                hi_at(s, Q, m)
                                activate(s, m * 4 + (Q + s - 2), m * 4 + (s - 2))
                        if half == 0 and first == 1:
                            act.wait_ge(ge_in, lay + 1)
                            af(sc[:], sc[:], ACT.Exp).then_inc(ge_out, 1)
                    if half == 0:
                        act.wait_ge(egT_ps, lay + 1)
                        af(egT[:, 0:2, :].rearrange("p w t -> p (w t)"), bank[6][:], ACT.Copy)
                        af(egT[:, 2, :], bank[7][:, 0:SEQ], ACT.Copy).then_inc(egT_ready, 1)
                        for s in range(4):
                            hi_at(s, Q + 4 * U_LOW)
                            if s > 2:
                                store_gates(s - 3, H + s - 3, s - 3)
                            activate(s, Q + 4 * U_LOW + s - 2, 4 * U_LOW + s - 2)
                            if s > 1:
                                copy_gates(s, H + s - 2, (s - 2) * GT, 8 * H)
                        store_gates(1, H + 1, 1)
                        copy_gates(0, H + 2, 2 * GT, 8 * (H + 2))
                        with act.Fori(1, NG // 4) as m:
                            for s in range(4):
                                hi_at(s, Q + 4 * U_LOW, m)
                                store_gates(s, m * 4 + (H + s - 2), m * 4 + (s - 2))
                                activate(s, m * 4 + (Q + 4 * U_LOW + s - 2), m * 4 + (4 * U_LOW + s - 2))
                                copy_gates(s - 1, m * 4 + (H + s - 1), m * (4 * GT) + (s - 1) * GT,
                                           m * 32 + (8 * H + 16 * ((s - 1) // 2)))
                    V, R, F = Q + HK, halves(lay, half) * HK // 2, halves(lay, half) * TURNS
                    if half:
                        split_p(0, V - 1, 0, F + 1)
                    hi_at(0, V)
                    activate(0, Q + HK - 2, HK - 2)
                    if half == 0:
                        store_gates(0, H + NG - 2, NG - 2)
                        copy_gates(1, H + NG - 1, (NG - 1) * GT, 8 * (H + NG - 2))
                        store_gates(1, H + NG - 1, NG - 1)
                        split_p(0, V - 1, 0, F + 1)
                    activate(1, Q + HK - 1, HK - 1)
                    for s in range(1, 4):
                        hi_at(s, V)
                        if s % 2:
                            split_p((s + 1) // 2 % 2, V + s - 1, s + 1, F + 1 + (s + 1) // 4)
                    with act.Fori(1, TURNS - 1) as m:
                        for s in range(4):
                            hi_at(s, V, m)
                            if s % 2:
                                split_p((s + 1) // 2 % 2, m * 4 + (V + s - 1), m * 4 + (s + 1),
                                        m + (F + 1 + (s + 1) // 4))
                    for s in range(4):
                        hi_at(s, V + HK - 4)
                        if s == 1:
                            split_p(1, V + HK - 4, HK - 2, F + TURNS)
            rms(2 * DEPTH)

        @block.vector
        def _(dve):
            v = nc.vector
            cp, tt, ts, stt = v.tensor_copy, v.tensor_tensor, v.tensor_scalar, v.scalar_tensor_tensor

            def scale_x(o_):
                for n in range(NT):
                    dve.wait_ge(rms_ready, 2 * o_ + n + 1)
                    v.reciprocal(stat[:, 2 + n:3 + n], stat[:, 2 + n:3 + n])
                    dve.drain()
                    ts(xs[:, n, :], x[:, n, :], stat[:, 2 + n:3 + n], None, ALU.mult).then_inc(xs_ready, 1)

            def copy_xT(o_, gain):
                for dst, ready in ((x_hi, xhi_ready), (xT, xT_ready)):
                    for b in (1, 3):
                        dve.wait_ge(xT_ps, 4 * o_ + b + 1)
                        for c in (2 * b, 2 * b + 1):
                            ts(dst[:, c, :], bank[4 + b][:, (c % 2) * SEQ:(c % 2 + 1) * SEQ],
                               vec[:, gain + c:gain + c + 1], None, ALU.mult).then_inc(ready, 1)

            def rotate(out1, out2, src, trig_n, heads, half):
                c0 = 0 if half == HD // 2 else HD // 2
                shape = [P, heads, 2, half]
                a = ropeA[:, 0:heads * 2 * half].rearrange("p (h w d) -> p h w d", h=heads, w=2)
                b = ropeB[:, 0:heads * 2 * half].rearrange("p (h w d) -> p h w d", h=heads, w=2)
                cs, sn = (t[:, trig_n, c0:c0 + half].unsqueeze(1).unsqueeze(1).broadcast_to(shape)
                          for t in (cos, sin))
                tt(a, src, cs, ALU.mult)
                tt(b, src, sn, ALU.mult)
                dve.drain()
                tt(out1, a[:, :, 0], b[:, :, 1], ALU.subtract)
                r = tt(out2, a[:, :, 1], b[:, :, 0], ALU.add)
                dve.drain()
                return r

            def add_experts(lay):
                dve.wait_ge(s_back, 16 * (lay + 1))
                for n in range(NT):
                    if n == 0:
                        dve.wait_ge(y_done, lay + 1)
                    else:
                        dve.wait_ge(blk_done, q0(lay + 1, 0))
                    for half in range(2):
                        w = slice(half * 512, (half + 1) * 512)
                        last = tt(x[:, n, w], x_back[:, n, w], bank[2 * n + half][:], ALU.add)
                    last.then_inc(x_ready, 1)

            def angles():
                dve.wait_ge(s_pos, 16)
                dve.wait_ge(s_const, 16)
                cp(posf[:], posi[:])
                dve.drain()
                for n in range(NT):
                    ts(ang[:, 0, n], const[:, C_INV:C_INV + NF], posf[:, n:n + 1], None, ALU.mult)
                dve.drain()
                for w, quarter in ((1, 0.0), (2, 0.25)):
                    ts(ang[:, 3], ang[:, 0], 1.0 / (2 * np.pi), quarter, ALU.mult, ALU.add)
                    dve.drain()
                    ts(ang[:, 3], ang[:, 3], ROUND, ROUND, ALU.add, ALU.subtract)
                    dve.drain()
                    src = ang[:, 0]
                    for part in (TWO_PI_1, TWO_PI_2, TWO_PI_3):
                        stt(ang[:, w], ang[:, 3], -part, src, ALU.mult, ALU.add)
                        src = ang[:, w]
                        dve.drain()
                    ts(ang[:, w], ang[:, w], quarter * 2 * np.pi, PI_IN, ALU.add, ALU.min)
                    dve.drain()
                    ts(ang[:, w], ang[:, w], -PI_IN, None, ALU.max)
                dve.drain()
                cp(ang[:, 4], ang[:, 3]).then_inc(ang_ready, 1)

            for lay in range(DEPTH):
                def split_wa(c):
                    dve.wait_ge(wa_hi, DC * lay + c + 1)
                    tt(win_a_lo[:, c], win_a[:, c], win_a_hi[c % 4][:], ALU.subtract).then_inc(wa_lo, 1)

                if lay:
                    split_wa(0)
                    split_wa(1)
                    add_experts(lay - 1)
                scale_x(2 * lay)
                dve.wait_ge(s_vec, 16 * (lay + 1))
                copy_xT(2 * lay, V_NMIX)
                for k in range(DC // 2):
                    if k == 0:
                        dve.wait_ge(xT_ready, DC * (2 * lay + 1))
                        dve.drain()
                    w = slice(2 * k, 2 * k + 2)
                    tt(xT_lo[:, w], xT[:, w], x_hi[:, w], ALU.subtract).then_inc(xT_lo_ready, 1)
                for c in range(2 if lay else 0, DC):
                    split_wa(c)
                for c in range(DC):
                    dve.wait_ge(wb_hi, DC * lay + c + 1)
                    tt(win_b_lo[:, c], win_b[:, c], win_b_hi[:, c], ALU.subtract).then_inc(wb_lo, 1)
                if lay == 0:
                    angles()

                HALF = IN_A // 2
                for half in range(2):
                    dve.wait_ge(proj_ps, 4 * lay + 2 + half + 1)
                    cp(proj[:, 1, half * HALF:(half + 1) * HALF], bank[2 + half][:, 0:HALF]).then_inc(proj_d, 1)
                dve.wait_ge(c_rms, lay + 1)
                v.reciprocal(stat[:, 8:12], stat[:, 8:12])
                dve.drain()
                for w, (c0, c1) in enumerate(((0, Q_RANK), (Q_RANK, KR0))):
                    for n in range(NT):
                        last = ts(proj[:, n, c0:c1], proj[:, n, c0:c1], stat[:, 8 + 2 * w + n:9 + 2 * w + n],
                                  None, ALU.mult)
                last.then_inc(cn_ready, 1)
                dve.wait_ge(proj_a, 2 * (lay + 1))
                dve.wait_ge(trig, 2)
                for n in range(NT):
                    src = proj[:, n, SQ0:SV0].rearrange("p (h w d) -> p h w d", h=6, w=2)
                    rotate(src[:, :, 0], src[:, :, 1], src, n, 6, HD // 2).then_inc(s_rope, 1)
                for n in range(NT):
                    src = proj[:, n, KR0:KR0 + ROPE].rearrange("p (h w d) -> p h w d", h=1, w=2)
                    rotate(src[:, :, 0], src[:, :, 1], src, n, 1, ROPE // 2)
                    cp(kb[:, n, :, NOPE:], proj[:, n, KR0:KR0 + ROPE].unsqueeze(1)
                       .broadcast_to([P, H_MLA, ROPE])).then_inc(k_rope, 1)
                dve.wait_ge(lru_ps, 6 * (lay + 1))
                v.memset(lxp[:, :, 0:1], 0.0)
                v.memset(lxp[:, :, SEQ + 1:], 0.0)
                for c in range(LC):
                    cp(lxp[:, c, 1:SEQ + 1], lru_bank(c)).then_inc(lx_ready, 1)
                dve.drain()
                for k in range(HALO + 1):
                    for c in range(LC):
                        w_ = vec[:, V_CW + LC * k + c:V_CW + LC * k + c + 1]
                        src = lxp[:, c, k:k + SEQ]
                        if k == 0:
                            last = ts(xc[:, c], src, w_, vec[:, V_CB + c:V_CB + c + 1], ALU.mult, ALU.add)
                        else:
                            last = stt(xc[:, c], src, w_, xc[:, c], ALU.mult, ALU.add)
                    if k < HALO:
                        dve.drain()
                last.then_inc(xc_ready, 1)
                for n in range(NT):
                    for half in range(2):
                        dve.wait_ge(q_nope, 4 * lay + 2 * n + half + 1)
                        src = (bank[2 * n + half][:, 0:3 * QK].rearrange("p (h d) -> p h d", h=3)[:, :, NOPE:]
                               .rearrange("p h (w d) -> p h w d", w=2))
                        dst = qb[:, n, 3 * half:3 * half + 3, NOPE:]
                        rotate(dst[:, :, 0:ROPE // 2], dst[:, :, ROPE // 2:], src, n, 3,
                               ROPE // 2).then_inc(q_rope, 1)
                dve.wait_ge(lam_u, lay + 1)
                u, z, z2, q, s8, n8 = (stat[:, 16 + 6 * k:22 + 6 * k] for k in (0, 3, 4, 5, 1, 2))
                ts(z, u, 2.0, None, ALU.add)
                dve.drain()
                v.reciprocal(z, z)
                dve.drain()
                tt(z, z, u, ALU.mult)
                dve.drain()
                tt(z2, z, z, ALU.mult)
                dve.drain()
                ts(q, z2, 1.0 / 19, None, ALU.mult)
                for k in range(8, 0, -1):
                    dve.drain()
                    stt(q, q, 1.0 / (2 * k + 1), z2, ALU.add, ALU.mult)
                ts(s8, vec[:, V_LAM:V_LAM + 6], -LRU_C, 0.0, ALU.mult, ALU.max)
                dve.drain()
                stt(q, q, 1.0, z, ALU.add, ALU.mult)
                dve.drain()
                stt(s8, q, 2 * LRU_C, s8, ALU.mult, ALU.add)
                dve.drain()
                ts(n8, s8, -1.0, None, ALU.mult)
                ts(s8, s8, 0.5, None, ALU.mult).then_inc(lam_ready, 1)
                def copy_sT(k):
                    dve.wait_ge(sT_ps, 3 * lay + k + 1)
                    cp(sT[0:HD, 2 * k:2 * k + 2].rearrange("p a t -> p (a t)"),
                       bank[4 + k % 2][0:HD, :]).then_inc(sT_ready, 1)

                NH = H_MLA + H_SWA

                def row_max(h):
                    dve.wait_ge(sc_ps, NH * lay + h + 1)
                    nm = stat[:, 84 + 2 * h:86 + 2 * h]
                    mx = stat[:, 64 + 2 * h:66 + 2 * h]
                    if h < H_MLA:
                        v.reduce_max(mx, bank[h % 2][:].rearrange("p (n k) -> p n k", n=NT), AX.X)
                        dve.drain()
                        ts(nm, mx, -QK ** -0.5, None, ALU.mult).then_inc(negm, 1)
                    else:
                        if h > H_MLA:
                            dve.wait_ge(p_ready, NH * lay + h)
                        stt(sw[:], bank[h % 2][:], HD ** -0.5, const[:, C_MASK:C_MASK + NT * SEQ], ALU.mult, ALU.add)
                        dve.drain()
                        v.reduce_max(mx, sw[:].rearrange("p (n k) -> p n k", n=NT), AX.X)
                        dve.drain()
                        g = V_SINK + h - H_MLA
                        ts(nm, mx, vec[:, g:g + 1], -1.0, ALU.max, ALU.mult)
                        dve.drain()
                        ts(stat[:, 124 + 2 * h:126 + 2 * h], nm, vec[:, g:g + 1], None, ALU.add).then_inc(negm, 1)

                def copy_pT(h):
                    dve.wait_ge(pt_ps, NH * lay + h + 1)
                    if h >= 2:
                        dve.wait_ge(o_ps, NH * lay + h - 1)
                    cp(prT[:, h % 2, :], bank[2 + h % 2][:]).then_inc(pt_ready, 1)

                def norm_o(h):
                    dve.wait_ge(o_ps, NH * lay + h + 1)
                    s_ = stat[:, 104 + 2 * h:106 + 2 * h]
                    if h >= H_MLA:
                        tt(s_, s_, stat[:, 124 + 2 * h:126 + 2 * h], ALU.add)
                        dve.drain()
                    v.reciprocal(s_, s_)
                    dve.drain()
                    for n in range(NT):
                        last = ts(o[:, n, h * HD:(h + 1) * HD], bank[6 + h % 2][:, n * HD:(n + 1) * HD],
                                  stat[:, 104 + 2 * h + n:105 + 2 * h + n], None, ALU.mult)
                    last.then_inc(o_done, 1)

                def flat(t):
                    return t[:].rearrange("p d c t -> p (d c t)")

                def lru_scan(d):
                    dve.wait_ge(b_ready, lay + 1)
                    for c in range(LC):
                        if d == 0:
                            v.tensor_tensor_scan(lr[:, 0, c, :], la[:, 0, c, :], li[:, 0, c, :], 0.0,
                                                 ALU.mult, ALU.add)
                        else:
                            v.tensor_tensor_scan(lr[:, 1, c, ::-1], la[:, 1, c, ::-1], li[:, 1, c, ::-1], 0.0,
                                                 ALU.mult, ALU.add)

                def lru_out():
                    f = [lr[:, d].rearrange("p c t -> p (c t)") for d in range(2)]
                    tt(f[0], f[0], f[1], ALU.add)
                    dve.drain()
                    tt(f[0], f[0], lg[:].rearrange("p c t -> p (c t)"), ALU.mult)
                    dve.drain()
                    tt(lt[:, 0].rearrange("p c t -> p (c t)"), f[0], f[0], ALU.mult).then_inc(osq_ready, 1)

                row_max(0)
                for h in range(NH):
                    if h + 1 < NH:
                        row_max(h + 1)
                    if h == 0:
                        copy_sT(0)
                        copy_sT(1)
                    copy_pT(h)
                    if h:
                        norm_o(h - 1)
                    if h == 1:
                        copy_sT(2)

                def scale_o(w, c0, c1):
                    dve.wait_ge(o_rms, 2 * lay + w + 1)
                    r_ = stat[:, 168 + 2 * w:170 + 2 * w]
                    v.reciprocal(r_, r_)
                    dve.drain()
                    for n in range(NT):
                        last = ts(o[:, n, c0:c1], o[:, n, c0:c1], r_[:, n:n + 1], None, ALU.mult)
                    last.then_inc(on_ready, 1)

                scale_o(0, 0, MLA_W)
                norm_o(NH - 1)
                lru_scan(0)
                scale_o(1, MLA_W, MLA_W + SWA_W)
                lru_scan(1)
                dve.drain()
                lru_out()
                dve.wait_ge(oT_ps, 2 * (lay + 1))
                for j in (3, 4):
                    for dst in (mix_hi, mixT):
                        last = ts(dst[:, 3 + j, :], mix_bank(j), vec[:, V_GRP + 3 + j:V_GRP + 4 + j], None, ALU.mult)
                    last.then_inc(mix_d, 1)
                dve.wait_ge(orms, lay + 1)
                v.reciprocal(lt[:, 1, 0, :], lt[:, 1, 0, :])
                dve.drain()
                for c in range(LC):
                    for dst in (mix_hi, mixT):
                        last = stt(dst[:, 3 + c, :], lr[:, 0, c, :], vec[:, V_GRP + 3 + c:V_GRP + 4 + c],
                                   lt[:, 1, 0, :], ALU.mult, ALU.mult)
                    last.then_inc(mix_d, 1)
                for n in range(NT):
                    for half in range(2):
                        dve.wait_ge(out_ps, 4 * lay + 2 * n + half + 1)
                        w = x[:, n, half * 512:(half + 1) * 512]
                        last = tt(w, w, bank[2 * n + half][:], ALU.add)
                    last.then_inc(x_ready, 1)
                scale_x(2 * lay + 1)
                copy_xT(2 * lay + 1, V_NFFN)

                def split_lo(s, q):
                    dve.wait_ge(hi_done, q + 1)
                    tt(hl[s % 2][:, 1], raw[:, s], hl[s % 2][:, 0], ALU.subtract).then_inc(lo_done, 1)

                def top16(val, idx, src, work):
                    for n in range(NT):
                        v.max(val[:, n, 0:8], src[:, n])
                    dve.drain()
                    for n in range(NT):
                        v.max_index(idx[:, n, 0:8], val[:, n, 0:8], src[:, n])
                        v.match_replace(work[:, n], val[:, n, 0:8], src[:, n], MAX_NEG)
                    dve.drain()
                    for n in range(NT):
                        v.max(val[:, n, 8:16], work[:, n])
                    dve.drain()
                    for n in range(NT):
                        last = v.max_index(idx[:, n, 8:16], val[:, n, 8:16], work[:, n])
                    return last

                def top_keys(i):
                    h, half = (i // 2 + PH // 2) % PH, i % 2
                    dve.wait_ge(ph_s, 16 * lay + i + 1)
                    tiles = [t.rearrange("p (n k) -> p n k", n=NT) for t in (score_bank[i % 4], tmp[:])]
                    top16(top_v[:, :, h, half], top_i[:, :, h, half], *tiles).then_inc(top1, 1)

                def top_pairs(i):
                    h = (i + PH // 2) % PH
                    dve.wait_ge(cand_ready, PH * lay + i + 1)
                    c_ = cand[:, i % 2]
                    top16(sc[:, :, h], ci[:, :, h], c_, c_).then_inc(top2, 1)

                dve.wait_ge(xhi_ready, DC * (2 * lay + 2))
                dve.wait_ge(xT_ready, 8 * (2 * lay + 2))
                dve.wait_ge(s_spill, 16 * (lay + 1))
                for k in range(DC // 2):
                    w = slice(2 * k, 2 * k + 2)
                    tt(x_lo[:, w], xT[:, w], x_hi[:, w], ALU.subtract).then_inc(xlo_ready, 1)
                for i in range(PH):
                    top_keys(2 * i)
                    top_keys(2 * i + 1)
                    if i:
                        top_pairs(i - 1)
                top_pairs(PH - 1)
                dve.drain()
                s3 = sc[:].rearrange("p n h s -> p (n h) s")
                big = stat[:, 208:224]
                cp(big, s3[:, :, 0])
                dve.drain()
                tt(s3, s3, big.unsqueeze(2).broadcast_to([P, NT * PH, TOP]), ALU.subtract).then_inc(ge_in, 1)
                cif = ci[:].rearrange("p n h s -> p (n h s)")
                caf = ca[:].rearrange("p w n h s -> p w (n h s)")
                SKIP = PA * (TOP - PB)
                cff = cf[:].rearrange("p w n h s -> p w (n h s)")
                b16, b4 = (eg[:, w].rearrange("p n h s -> p (n h s)") for w in range(2))
                ts(caf[:, 0], cif, 4, None, ALU.logical_shift_right)
                ts(caf[:, 1], cif, 2, None, ALU.logical_shift_right)
                cp(tmp[:], cif)
                dve.drain()
                cp(cff, caf)
                dve.drain()
                stt(cff[:, 0], cff[:, 1], -float(SKIP // PB), cff[:, 0], ALU.add, ALU.max)
                dve.drain()
                ts(b16, cff[:, 0], -float(TOP), None, ALU.mult)
                ts(b4, cff[:, 0], -float(PB), -float(SKIP), ALU.mult, ALU.add)
                dve.drain()
                tt(b16, b16, b4, ALU.max)
                dve.drain()
                tt(cff[:, 1], b16, tmp[:], ALU.add)
                cp(top_f[:].rearrange("p n h w s -> p (n h w s)"), top_i[:].rearrange("p n h w s -> p (n h w s)"))
                dve.drain()
                shape = [P, NT, TOP, TOP]
                i16 = const[:, C_IOTA:C_IOTA + TOP].unsqueeze(1).unsqueeze(1).broadcast_to(shape)

                def decode(h, part):
                    dve.drain()
                    for w in range(2):
                        if part == 0:
                            c_ = cf[:, w, :, bass.ds(h, 1), :].rearrange("p n a s -> p n (a s)")
                            tt(hot[:, w], c_.unsqueeze(3).broadcast_to(shape), i16, ALU.is_equal)
                        elif part == 1:
                            f_ = top_f[:, :, bass.ds(h, 1), w, :].rearrange("p n a s -> p n (a s)")
                            tt(hot[:, w], hot[:, w], f_.unsqueeze(2).broadcast_to(shape), ALU.mult)
                        else:
                            last = v.reduce_sum(eg[:, w, :, bass.ds(h, 1), :].rearrange("p n a s -> p n (a s)"),
                                                hot[:, w], AX.X)
                    return last if part == 2 else None

                def one_hots(s, g, t0, wait_ps=True):
                    if wait_ps:
                        dve.wait_ge(gate_ps, g * 2 - 2)
                    k1, k2 = (egT[:, w, bass.ds(t0, GT)].unsqueeze(2) for w in range(2))
                    sh = [P, GT, NK]
                    tt(one_i[:, s % 2], iota.unsqueeze(1).broadcast_to(sh), k1.broadcast_to(sh),
                       ALU.is_equal).then_inc(one_eq, 1)
                    tt(one_j[:, s % 2], iota.unsqueeze(1).broadcast_to(sh), k2.broadcast_to(sh),
                       ALU.is_equal).then_inc(one_j_ready, 1)

                def weigh(m):
                    a_ = act_g[:, bass.ds(m * (4 * SEQ), 4 * SEQ)].rearrange("p (i t) -> p i t", i=4)
                    tt(a_, a_, gates[:].rearrange("p (t i) -> p i t", i=HK)[:, bass.ds(m * 4, 4), :],
                       ALU.mult).then_inc(pf_done, 1)

                def split_p(s, pair, i):
                    dve.wait_ge(p_hi, pair + 1)
                    tt(p_hl[:, s, 1], act_g[:, bass.ds(i * SEQ, 2 * SEQ)], p_hl[:, s, 0],
                       ALU.subtract).then_inc(p_lo, 1)

                for h in range(EARLY // 4):
                    for part in range(3):
                        decode(h, part)
                dve.wait_ge(lo_done, q0(lay, 0) + EARLY)
                for half in range(2):
                    Q, H = q0(lay, half), lay * NG
                    if half:
                        for s in range(4):
                            split_lo(s, Q + s)
                    with dve.Fori(1 if half else EARLY // 4, TURNS if half else U_LOW - 1) as m:
                        for s in range(4):
                            split_lo(s, m * 4 + (Q + s))
                            if half == 0 and s < 3:
                                decode(m, s)
                    if half == 0:
                        dve.wait_ge(ge_out, lay + 1)
                        gs = stat[:, 176:192]
                        v.reduce_sum(gs, s3, AX.X)
                        dve.drain()
                        v.reciprocal(gs, gs)
                        dve.drain()
                        tt(eg[:, 2].rearrange("p n h s -> p (n h) s"), s3,
                           gs.unsqueeze(2).broadcast_to([P, NT * PH, TOP]), ALU.mult)
                        for s in range(4):
                            split_lo(s, Q + 4 * U_LOW - 4 + s)
                            if s < 3:
                                last = decode(U_LOW - 1, s)
                            if s == 2:
                                last.then_inc(eg_ready, 1)
                        split_lo(0, Q + 4 * U_LOW)
                        dve.wait_ge(egT_ready, lay + 1)
                        for s in range(4):
                            if s:
                                split_lo(s, Q + 4 * U_LOW + s)
                            one_hots(s, H + s, s * GT, H + s > 1)
                        with dve.Fori(1, NG // 4) as m:
                            for s in range(4):
                                one_hots(s, m * 4 + (H + s), m * (4 * GT) + s * GT)
                                split_lo(s, m * 4 + (Q + 4 * U_LOW + s))
                    V, R, F = Q + HK, halves(lay, half) * HK // 2, halves(lay, half) * TURNS
                    dve.wait_ge(gelu_done, halves(lay, half) * HK + 8)
                    if half:
                        dve.wait_ge(gates_back, 16 * (NG // 2) * (lay + 1))
                        weigh(0)
                        split_p(0, R, 0)
                        split_lo(0, V)
                    else:
                        split_lo(0, V)
                        dve.wait_ge(gate_ready, 2 * (H + NG))
                        weigh(0)
                        split_p(0, R, 0)
                    for s in range(1, 4):
                        split_lo(s, V + s)
                        if s == 2:
                            weigh(1)
                        if s % 2:
                            split_p((s + 1) // 2 % 2, R + (s + 1) // 2, s + 1)
                    dve.wait_ge(gelu_done, (halves(lay, half) + 1) * HK)
                    for first, last_turn in ((1, TURNS // 2), (TURNS // 2, TURNS - 1)):
                        with dve.Fori(first, last_turn) as m:
                            for s in range(4):
                                split_lo(s, m * 4 + (V + s))
                                if s % 2 == 0 and first == 1:
                                    weigh(m * 2 + s // 2)
                                if s % 2:
                                    split_p((s + 1) // 2 % 2, m * 2 + (R + (s + 1) // 2), m * 4 + (s + 1))
                    for s in range(4):
                        split_lo(s, V + HK - 4 + s)
                        if s == 1:
                            split_p(1, R + HK // 2 - 1, HK - 2)
            add_experts(DEPTH - 1)
            dve.wait_ge(s_nf, 16)
            for n in range(NT):
                dve.wait_ge(rms_ready, 2 * 2 * DEPTH + n + 1)
                v.reciprocal(stat[:, 2 + n:3 + n], stat[:, 2 + n:3 + n])
                dve.drain()
                stt(xs[:, n, :], x[:, n, :], stat[:, 2 + n:3 + n], norm_fb[:], ALU.mult, ALU.mult).then_inc(final, 1)

        @block.gpsimd
        def _(pool):
            for lay in range(DEPTH):
                if lay:
                    pool.wait_ge(p_lo, halves(lay, 0) * HK // 2)
                nc.gpsimd.memset(wlru[:], 0.0).then_inc(zeroed, 1)
                nc.gpsimd.memset(ones[:], 1.0).then_inc(ones_ready, 1)
                def split_wo(k):
                    pool.wait_ge(wo_hi, DC * lay + k + 1)
                    c = OUT_ORDER[k]
                    nc.gpsimd.tensor_tensor(wout_lo[:, c], wout[:, c], wout_hi[k][:],
                                            ALU.subtract).then_inc(wo_lo, 1)

                split_wo(0)
                pool.wait_ge(gates_ready, 12 * (lay + 1))
                two = li[:].rearrange("p d c t -> p d (c t)")
                nc.gpsimd.tensor_tensor(two, two, xc[:].rearrange("p c t -> p (c t)").unsqueeze(1)
                                        .broadcast_to([P, 2, LC * SEQ]), ALU.mult)

                def split_mix(k):
                    if k < 3:
                        pool.wait_ge(mix_a, 3 * lay + k + 1)
                    else:
                        pool.wait_ge(mix_d, 5 * lay + k - 2)
                    c = OUT_ORDER[k]
                    nc.gpsimd.tensor_tensor(mix_lo[:, c], mixT[:, c], mix_hi[:, c],
                                            ALU.subtract).then_inc(mixlo_ready, 1)

                for k in (1, 2, 3, 4):
                    split_wo(k)
                flat_li, flat_lt, flat_la, flat_lr = (t[:].rearrange("p d c t -> p (d c t)") for t in (li, lt, la, lr))
                pool.wait_ge(a_ready, 6 * (lay + 1))
                pool.drain()
                nc.gpsimd.tensor_tensor(flat_lt, flat_li, flat_la, ALU.mult)
                pool.drain()
                nc.gpsimd.tensor_tensor(flat_li, flat_li, flat_lt, ALU.add)
                for k in (5, 6, 7):
                    split_wo(k)
                pool.drain()
                pool.wait_ge(b_root, lay + 1)
                nc.gpsimd.tensor_tensor(flat_li, flat_li, flat_lr, ALU.mult).then_inc(b_ready, 1)
                for k in range(DC):
                    split_mix(k)

                def split_lo(s):
                    pool.wait_ge(hi_done, q0(lay, 0) + s + 1)
                    nc.gpsimd.tensor_tensor(hl[s % 2][:, 1], raw[:, s % RAWS], hl[s % 2][:, 0],
                                            ALU.subtract).then_inc(lo_done, 1)

                def wq_split(i):
                    pool.wait_ge(wq_hi_ready, 2 * PH * lay + i + 1)
                    blk = (i + PH) % (2 * PH)
                    nc.gpsimd.tensor_tensor(wq_lo[:, blk], wq[:, blk], wq_hi[i % WQ_RING][:],
                                            ALU.subtract).then_inc(wq_lo_ready, 1)

                for i in range(6):
                    wq_split(i)
                for i in range(PH):
                    h = (i + PH // 2) % PH
                    for k in (2 * i + 6, 2 * i + 7):
                        if k < 2 * PH:
                            wq_split(k)
                    if i in (4, 5):
                        split_lo(i - 4)
                    if i == PH - 1:
                        for s in range(2, 5):
                            split_lo(s)
                    pool.wait_ge(top1, 16 * lay + 2 * i + 2)
                    if i >= 2:
                        pool.wait_ge(top2, PH * lay + i - 1)
                    for a0, a1, nb, c0 in ((0, PA, TOP, 0), (PA, TOP, PB, PA * TOP)):
                        sh = [P, NT, a1 - a0, nb]
                        last = nc.gpsimd.tensor_tensor(
                            cand[:, i % 2, :, c0:c0 + (a1 - a0) * nb].rearrange("p n (a b) -> p n a b", b=nb),
                            top_v[:, :, h, 0, a0:a1].unsqueeze(3).broadcast_to(sh),
                            top_v[:, :, h, 1, 0:nb].unsqueeze(2).broadcast_to(sh), ALU.add)
                    last.then_inc(cand_ready, 1)

                for s in range(5, EARLY):
                    split_lo(s)

                def times_gate(s, g, t0):
                    pool.wait_ge(one_eq, g + 1)
                    nc.gpsimd.tensor_tensor(
                        one_i[:, s % 2], one_i[:, s % 2],
                        egT[:, 2, bass.ds(t0, GT)].unsqueeze(2).broadcast_to([P, GT, NK]),
                        ALU.mult).then_inc(one_i_ready, 1)

                pool.wait_ge(egT_ready, lay + 1)
                with pool.Fori(0, NG // 2) as m:
                    for s in range(2):
                        times_gate(s, m * 2 + (lay * NG + s), m * (2 * GT) + s * GT)


def kernel(**inputs):
    import concourse.bacc as _bacc
    from concourse.bass_utils import run_bass_kernel_spmd as _run

    a = {k: np.asarray(v) for k, v in inputs.items()}
    L = DEPTH

    def chunks(w, parts):
        return w.reshape(L, parts, P, -1).transpose(0, 2, 1, 3)

    def columns(v_):
        return v_.reshape(L, -1, P).transpose(0, 2, 1)

    const = np.zeros((P, C_W), np.float32)
    const[:, C_ID:C_ID + P] = np.eye(P)
    const[:, C_IOTA:C_IOTA + NK] = np.arange(NK)
    const[:, C_INV:C_INV + HD // 2] = 10000.0 ** (-np.arange(0, HD, 2, dtype=np.float32) / HD)
    const[:, C_INV + HD // 2:C_INV + NF] = 10000.0 ** (-np.arange(0, ROPE, 2, dtype=np.float32) / ROPE)
    query = np.arange(SEQ).reshape(NT, P, 1)
    far = np.abs(query - np.arange(SEQ)) > WINDOW
    const[:, C_MASK:C_MASK + NT * SEQ] = np.where(far, NEG_BIG, 0.0).transpose(1, 0, 2).reshape(P, -1)
    const[:, C_EPS] = EPS

    vec = np.concatenate(
        [columns(a["norm_mix"]), columns(a["norm_ffn"]), columns(a["q_norm"]), columns(a["kv_norm"]),
         columns(a["grp_norm"]), columns(a["conv_w"].reshape(L, -1)), columns(a["conv_b"]),
         columns(a["lru_ba"].reshape(L, -1)), columns(a["lru_bx"].reshape(L, -1)),
         columns(a["lru_lambda"].reshape(L, -1)), np.broadcast_to(a["swa_sink"][:, None, :], (L, P, H_SWA))], axis=2)
    win = chunks(a["w_in"], DC)
    win = np.concatenate([win[..., :IN_A].reshape(L, P, -1), win[..., IN_A:].reshape(L, P, -1)], axis=2)
    gates = np.stack([a["lru_wa"], a["lru_wx"]], axis=2).reshape(L, 2, 2, LC, 2, 64, 64)
    gates = gates.transpose(0, 4, 5, 1, 2, 3, 6).reshape(L, P, 12, 64)
    wq = a["peer_wq"].reshape(L, DC, P, 2 * PH, P).transpose(0, 2, 3, 1, 4)
    sub = a["peer_subkeys"].transpose(0, 3, 1, 2)
    pu = a["peer_u"].reshape(L, NK, NK, DC, P).transpose(0, 1, 4, 3, 2).reshape(L, NK, P, D)
    arrays = {
        "x": a["x"].reshape(NT, P, D).transpose(1, 0, 2), "pos": a["positions"].reshape(NT, P).T,
        "const": const, "vec": vec, "w_in": win,
        "w_uq": chunks(a["w_uq"], 2), "w_ukv": a["w_ukv"], "w_lru": gates, "w_out": chunks(a["w_out"], DC),
        "w_q": wq, "sub_k": sub, "peer_u": pu, "peer_v": a["peer_v"].reshape(L, NK, P, D),
        "norm_f": a["norm_final"]}
    arrays = {k + "_dram": np.ascontiguousarray(v_) for k, v_ in arrays.items()}

    nc = _bacc.Bacc("TRN2", target_bir_lowering=False, num_devices=1)
    args = [nc.dram_tensor(k, v_.shape, mybir.dt.from_np(v_.dtype), kind="ExternalInput").ap()
            for k, v_ in arrays.items()]
    spill = nc.dram_tensor("x_spill_dram", (P, NT, D), F32, kind="Internal").ap()
    out = nc.dram_tensor("out_dram", (P, NT, D), F32, kind="ExternalOutput").ap()
    gates_dram = nc.dram_tensor("gates_dram", (SEQ // GT, P, GT * HK), F32, kind="Internal").ap()
    encoder(nc, *args, spill, gates_dram, out)
    r = _run(nc, [arrays], core_ids=[0])
    got = r.results[0]["out_dram"]
    return got.transpose(1, 0, 2).reshape(1, SEQ, D)
```
